# Optimizing a Trainium2 kernel written in Bass

```python
import math
import numpy as np
import jax
import jax.numpy as jnp
from jax import lax
import jax, jax.numpy as jnp

D_MODEL = 1024
BATCH = 1
SEQ = 256
DEPTH = 1

HEAD_DIM = 64
GRID_W = 64
NA_HEADS = 8
NA_WIN_ROWS = 8
NA_WIN_COLS = 16
NA_QCOL_BLOCK = 16
NA_KCOL_BLOCK = NA_QCOL_BLOCK + NA_WIN_COLS
DIL_CONFIGS = ((128, 1), (512, 4), (2048, 16))
DIL_HEADS_PER_GROUP = 4
DIL_N_GROUPS = len(DIL_CONFIGS)
DIL_QBLOCK = 64
ROT_DIM = HEAD_DIM // 4
ROPE_THETA = 500000.0
NA_WIDTH = NA_HEADS * HEAD_DIM
DIL_WIDTH = DIL_N_GROUPS * DIL_HEADS_PER_GROUP * HEAD_DIM
DIL_OUT_WIDTH = DIL_HEADS_PER_GROUP * HEAD_DIM
IN_WIDTH = 3 * NA_WIDTH + 3 * DIL_WIDTH + 2 * D_MODEL
PEER_HEADS = 8
PEER_NKEYS = 128
PEER_NEXPERTS = PEER_NKEYS * PEER_NKEYS
PEER_QDIM = 256
PEER_TOPK = 16
PEER_CHUNK = 256
PLE_DIM = 256
RMS_EPS = 1e-6


def rms_norm(x, gain):
    x32 = x.astype(jnp.float32)
    y = x32 * lax.rsqrt(jnp.mean(x32 * x32, axis=-1, keepdims=True) + RMS_EPS)
    return (y * gain.astype(jnp.float32)).astype(x.dtype)

def partial_rotary(x, pos):
    half = ROT_DIM // 2
    inv_freq = jnp.power(jnp.float32(ROPE_THETA), -jnp.arange(half, dtype=jnp.float32) * 2.0 / ROT_DIM)
    ang = pos.astype(jnp.float32)[:, None] * inv_freq[None, :]
    cos = jnp.cos(ang)[:, None, :]
    sin = jnp.sin(ang)[:, None, :]
    xr = x[..., :ROT_DIM].astype(jnp.float32)
    x1, x2 = xr[..., :half], xr[..., half:]
    rot = jnp.concatenate([x1 * cos - x2 * sin, x2 * cos + x1 * sin], axis=-1)
    return jnp.concatenate([rot.astype(x.dtype), x[..., ROT_DIM:]], axis=-1)

def _na_static(width):
    ncb = width // NA_QCOL_BLOCK
    qc = np.arange(width).reshape(ncb, NA_QCOL_BLOCK)
    kc_start = np.clip(np.arange(ncb) * NA_QCOL_BLOCK - NA_WIN_COLS // 2, 0, width - NA_KCOL_BLOCK)
    kc = kc_start[:, None] + np.arange(NA_KCOL_BLOCK)[None, :]
    cs = np.clip(qc - NA_WIN_COLS // 2, 0, width - NA_WIN_COLS)
    kcb = kc[:, None, :]
    mask = (kcb >= cs[..., None]) & (kcb < cs[..., None] + NA_WIN_COLS)
    dc_idx = np.clip(kcb - qc[..., None] + NA_WIN_COLS - 1, 0, 2 * NA_WIN_COLS - 2)
    return kc, mask, dc_idx

def neighbourhood_attention(q, k, v, rpb):
    B, S, H, dh = q.shape
    rows = S // GRID_W
    kh = min(NA_WIN_ROWS, rows)
    ncb = GRID_W // NA_QCOL_BLOCK
    kc, mask, dc_idx = _na_static(GRID_W)
    mask_j = jnp.asarray(mask)[None, None, :, :, None, :]
    qg = q.reshape(B, rows, GRID_W, H, dh)
    kg = k.reshape(B, rows, GRID_W, H, dh)
    vg = v.reshape(B, rows, GRID_W, H, dh)
    scale = HEAD_DIM ** -0.5

    def one_row(r):
        rs = jnp.clip(r - kh // 2, 0, rows - kh)
        q_row = lax.dynamic_index_in_dim(qg, r, axis=1, keepdims=False)
        k_rows = lax.dynamic_slice_in_dim(kg, rs, kh, axis=1)
        v_rows = lax.dynamic_slice_in_dim(vg, rs, kh, axis=1)
        q_cb = q_row.reshape(B, ncb, NA_QCOL_BLOCK, H, dh)
        k_cb = jnp.take(k_rows, kc, axis=2)
        v_cb = jnp.take(v_rows, kc, axis=2)
        s = jnp.einsum('bjqhd,bljkhd->bhjqlk', q_cb, k_cb).astype(jnp.float32) * scale
        dr_idx = rs + jnp.arange(kh) - r + NA_WIN_ROWS - 1
        bias = rpb[:, dr_idx][:, :, dc_idx]
        bias = bias.transpose(0, 2, 3, 1, 4).astype(jnp.float32)
        s = jnp.where(mask_j, s + bias[None], -jnp.inf)
        shp = s.shape
        pr = jax.nn.softmax(s.reshape(shp[:4] + (kh * NA_KCOL_BLOCK,)), axis=-1).reshape(shp)
        o = jnp.einsum('bhjqlk,bljkhd->bjqhd', pr.astype(v.dtype), v_cb)
        return o.reshape(B, GRID_W, H, dh)

    out = lax.map(one_row, jnp.arange(rows))
    return out.transpose(1, 0, 2, 3, 4).reshape(B, S, H * dh)

def dilated_window_attention(q, k, v, window, dilation):
    B, S, H, dh = q.shape
    n = window // (2 * dilation)
    L = S // dilation
    qbs = math.gcd(L, DIL_QBLOCK)
    nblk = L // qbs
    kbs = qbs + 2 * n

    def to_res(t):
        return t.reshape(B, L, dilation, H, dh).transpose(0, 2, 1, 3, 4)

    qr, kr, vr = to_res(q), to_res(k), to_res(v)
    pad = ((0, 0), (0, 0), (n, n), (0, 0), (0, 0))
    kp = jnp.pad(kr, pad)
    vp = jnp.pad(vr, pad)
    kidx = (np.arange(nblk) * qbs)[:, None] + np.arange(kbs)[None, :]
    kb = jnp.take(kp, kidx, axis=2)
    vb = jnp.take(vp, kidx, axis=2)
    qb = qr.reshape(B, dilation, nblk, qbs, H, dh)
    s = jnp.einsum('brnqhd,brnkhd->brnhqk', qb, kb).astype(jnp.float32) * (HEAD_DIM ** -0.5)
    qi = np.arange(qbs)[:, None]
    kj = np.arange(kbs)[None, :]
    band = (kj - qi >= 0) & (kj - qi <= 2 * n)
    m_key = kidx - n
    inside = (m_key >= 0) & (m_key < L)
    mask = band[None] & inside[:, None, :]
    s = jnp.where(jnp.asarray(mask)[None, None, :, None, :, :], s, -jnp.inf)
    lse = jax.nn.logsumexp(s, axis=-1, keepdims=True)
    pr = jnp.exp(s - lse).astype(v.dtype)
    o = jnp.einsum('brnhqk,brnkhd->brnqhd', pr, vb)
    o = o.reshape(B, dilation, L, H, dh).transpose(0, 2, 1, 3, 4).reshape(B, S, H, dh)
    lse = lse[..., 0].transpose(0, 1, 2, 4, 3).reshape(B, dilation, L, H)
    lse = lse.transpose(0, 2, 1, 3).reshape(B, S, H)
    return o, lse

def peer_ffn(h, w_query, sub_keys, expert_u, expert_v):
    B, S, D = h.shape
    T = B * S
    chunk = math.gcd(T, PEER_CHUNK)
    half = PEER_QDIM // 2
    hf = h.reshape(T // chunk, chunk, D)
    k1 = sub_keys[0].astype(jnp.float32)
    k2 = sub_keys[1].astype(jnp.float32)

    def run(hc):
        q = (hc @ w_query).reshape(chunk, PEER_HEADS, PEER_QDIM).astype(jnp.float32)
        s1 = jnp.einsum('thd,nd->thn', q[..., :half], k1)
        s2 = jnp.einsum('thd,nd->thn', q[..., half:], k2)
        v1, i1 = lax.top_k(s1, PEER_TOPK)
        v2, i2 = lax.top_k(s2, PEER_TOPK)
        cand = (v1[..., :, None] + v2[..., None, :]).reshape(chunk, PEER_HEADS, PEER_TOPK * PEER_TOPK)
        cidx = (i1[..., :, None] * PEER_NKEYS + i2[..., None, :]).reshape(chunk, PEER_HEADS, PEER_TOPK * PEER_TOPK)
        sc, pos = lax.top_k(cand, PEER_TOPK)
        eidx = jnp.take_along_axis(cidx, pos, axis=-1)
        g = jax.nn.softmax(sc, axis=-1)
        u = jnp.take(expert_u, eidx, axis=0)
        a = jnp.einsum('thkd,td->thk', u, hc).astype(jnp.float32)
        act = (jax.nn.gelu(a, approximate=False) * g).astype(hc.dtype)
        vv = jnp.take(expert_v, eidx, axis=0)
        return jnp.einsum('thk,thkd->td', act, vv)

    return lax.map(run, hf).reshape(B, S, D)

def first_inputs(seed: int = 0) -> dict:
    key = jax.random.key(seed)
    ks = jax.random.split(key, 20)

    def nrm(k, shape, scale):
        return jax.random.normal(k, shape, jnp.float32) * scale

    def gain(k, shape):
        return 1.0 + 0.05 * jax.random.normal(k, shape, jnp.float32)

    return {
        "x": nrm(ks[0], (BATCH, SEQ, D_MODEL), 1.0),
        "p": nrm(ks[1], (DEPTH, BATCH, SEQ, PLE_DIM), 1.0),
        "norm_mix": gain(ks[2], (DEPTH, D_MODEL)),
        "w_in": nrm(ks[3], (DEPTH, D_MODEL, IN_WIDTH), D_MODEL ** -0.5),
        "qk_norm_na": gain(ks[4], (DEPTH, 2, HEAD_DIM)),
        "na_rel_bias": nrm(ks[5], (DEPTH, NA_HEADS, 2 * NA_WIN_ROWS - 1, 2 * NA_WIN_COLS - 1), 0.2),
        "qk_norm_dil": gain(ks[6], (DEPTH, 2, HEAD_DIM)),
        "w_branch_na": nrm(ks[7], (DEPTH, NA_WIDTH, D_MODEL), NA_WIDTH ** -0.5),
        "w_branch_dil": nrm(ks[8], (DEPTH, DIL_OUT_WIDTH, D_MODEL), DIL_OUT_WIDTH ** -0.5),
        "w_out": nrm(ks[9], (DEPTH, D_MODEL, D_MODEL), D_MODEL ** -0.5),
        "norm_ffn": gain(ks[10], (DEPTH, D_MODEL)),
        "peer_w_query": nrm(ks[11], (DEPTH, D_MODEL, PEER_HEADS * PEER_QDIM), D_MODEL ** -0.5),
        "peer_sub_keys": nrm(ks[12], (DEPTH, 2, PEER_NKEYS, PEER_QDIM // 2), (PEER_QDIM // 2) ** -0.5),
        "peer_expert_u": nrm(ks[13], (DEPTH, PEER_NEXPERTS, D_MODEL), D_MODEL ** -0.5),
        "peer_expert_v": nrm(ks[14], (DEPTH, PEER_NEXPERTS, D_MODEL), PEER_HEADS ** -0.5),
        "norm_ple": gain(ks[15], (DEPTH, D_MODEL)),
        "w_ple_gate": nrm(ks[16], (DEPTH, D_MODEL, D_MODEL), D_MODEL ** -0.5),
        "w_ple": nrm(ks[17], (DEPTH, PLE_DIM, D_MODEL), PLE_DIM ** -0.5),
    }

def first_block(x, p, norm_mix, w_in, qk_norm_na, na_rel_bias, qk_norm_dil, w_branch_na, w_branch_dil,
              w_out, norm_ffn, peer_w_query, peer_sub_keys, peer_expert_u, peer_expert_v,
              norm_ple, w_ple_gate, w_ple):
    B, S, D = x.shape
    pos = jnp.arange(S)
    splits = [int(c) for c in np.cumsum([NA_WIDTH] * 3 + [DIL_WIDTH] * 3 + [D_MODEL])]
    n_dil_heads = DIL_N_GROUPS * DIL_HEADS_PER_GROUP
    for i in range(DEPTH):
        h = rms_norm(x, norm_mix[i])
        proj = h @ w_in[i]
        qa, ka, va, qd, kd, vd, gate_na, gate_dil = jnp.split(proj, splits, axis=-1)

        qa = rms_norm(qa.reshape(B, S, NA_HEADS, HEAD_DIM), qk_norm_na[i, 0])
        ka = rms_norm(ka.reshape(B, S, NA_HEADS, HEAD_DIM), qk_norm_na[i, 1])
        va = va.reshape(B, S, NA_HEADS, HEAD_DIM)
        out_na = neighbourhood_attention(qa, ka, va, na_rel_bias[i])

        qd = partial_rotary(rms_norm(qd.reshape(B, S, n_dil_heads, HEAD_DIM), qk_norm_dil[i, 0]), pos)
        kd = partial_rotary(rms_norm(kd.reshape(B, S, n_dil_heads, HEAD_DIM), qk_norm_dil[i, 1]), pos)
        qd = qd.reshape(B, S, DIL_N_GROUPS, DIL_HEADS_PER_GROUP, HEAD_DIM)
        kd = kd.reshape(B, S, DIL_N_GROUPS, DIL_HEADS_PER_GROUP, HEAD_DIM)
        vd = vd.reshape(B, S, DIL_N_GROUPS, DIL_HEADS_PER_GROUP, HEAD_DIM)
        outs, lses = [], []
        for g, (window, dilation) in enumerate(DIL_CONFIGS):
            o_g, lse_g = dilated_window_attention(qd[:, :, g], kd[:, :, g], vd[:, :, g], window, dilation)
            outs.append(o_g)
            lses.append(lse_g)
        wts = jax.nn.softmax(jnp.stack(lses, axis=2), axis=2)
        out_dil = jnp.sum(wts[..., None] * jnp.stack(outs, axis=2).astype(jnp.float32), axis=2)
        out_dil = out_dil.astype(x.dtype).reshape(B, S, DIL_OUT_WIDTH)

        merged = (jax.nn.sigmoid(gate_na) * (out_na @ w_branch_na[i])
                  + jax.nn.sigmoid(gate_dil) * (out_dil @ w_branch_dil[i]))
        x = x + merged @ w_out[i]

        h = rms_norm(x, norm_ffn[i])
        x = x + peer_ffn(h, peer_w_query[i], peer_sub_keys[i], peer_expert_u[i], peer_expert_v[i])

        h = rms_norm(x, norm_ple[i])
        x = x + jax.nn.sigmoid(h @ w_ple_gate[i]) * (p[i] @ w_ple[i])
    return x


CHUNK = 64
Q_BLOCK = 128
MIX_WIDTH = D_MODEL
POOL_WIDTH = MIX_WIDTH // 2
POOL_WINDOWS = (2, 4, 8, 16)
POOL_GROUPS = len(POOL_WINDOWS)
POOL_GROUP_DIM = POOL_WIDTH // POOL_GROUPS
ATTN_WIDTH = MIX_WIDTH - POOL_WIDTH
DIFF_HEAD_DIM = 64
V_HEAD_DIM = 2 * DIFF_HEAD_DIM
N_DIFF_HEADS = ATTN_WIDTH // V_HEAD_DIM
IN_WIDTH_2 = POOL_WIDTH + 3 * ATTN_WIDTH
D_FF = 2816
CONV_WIDTH = 3
ROPE_THETA_2 = 10000.0
EPS = 1e-6


def rmsnorm(x, g):
    xf = x.astype(jnp.float32)
    y = xf * lax.rsqrt(jnp.mean(xf * xf, axis=-1, keepdims=True) + EPS)
    return (y * g.astype(jnp.float32)).astype(x.dtype)

def rope_tables(positions, dtype):
    inv_freq = ROPE_THETA_2 ** (-jnp.arange(0, DIFF_HEAD_DIM, 2, dtype=jnp.float32) / DIFF_HEAD_DIM)
    ang = positions.astype(jnp.float32)[..., None] * inv_freq
    return (jnp.cos(ang)[:, :, None, None, :].astype(dtype),
            jnp.sin(ang)[:, :, None, None, :].astype(dtype))

def apply_rope(t, cos, sin):
    t1, t2 = jnp.split(t, 2, axis=-1)
    return jnp.concatenate([t1 * cos - t2 * sin, t1 * sin + t2 * cos], axis=-1)

def multiscale_pool(p, pool_w, pool_scale):
    s = p.shape[1]
    pf = p.astype(jnp.float32)
    csum = jnp.pad(jnp.cumsum(pf, axis=1), ((0, 0), (1, 0), (0, 0)))
    t = jnp.arange(s)
    pooled = []
    for g, w in enumerate(POOL_WINDOWS):
        cs = csum[..., g * POOL_GROUP_DIM:(g + 1) * POOL_GROUP_DIM]
        upper = cs[:, 1:]
        lower = jnp.pad(cs[:, :s + 1 - w], ((0, 0), (w - 1, 0), (0, 0)))
        count = jnp.minimum(t + 1, w).astype(jnp.float32)[None, :, None]
        pooled.append((upper - lower) / count)
    d = (jnp.concatenate(pooled, axis=-1) - pf).astype(p.dtype)
    d = d.reshape(p.shape[0], s, POOL_GROUPS, POOL_GROUP_DIM)
    y = jnp.einsum('bsgc,gcd->bsgd', d, pool_w).reshape(p.shape[0], s, POOL_WIDTH)
    return y * pool_scale

def diff_attention(q, k, v, lam, lam_init, head_g):
    b, h, _, s, _ = q.shape
    scale = DIFF_HEAD_DIM ** -0.5
    outs = []
    for i in range(s // Q_BLOCK):
        q0 = i * Q_BLOCK
        end = q0 + Q_BLOCK
        qb = q[:, :, :, q0:end]
        kb = k[:, :, :, :end]
        vb = v[:, :, :end]
        scores = jnp.einsum('bhnqd,bhnkd->bhnqk', qb, kb).astype(jnp.float32) * scale
        q_chunk = (q0 + jnp.arange(Q_BLOCK)) // CHUNK
        k_chunk = jnp.arange(end) // CHUNK
        mask = k_chunk[None, :] <= q_chunk[:, None]
        probs = jax.nn.softmax(jnp.where(mask, scores, -jnp.inf), axis=-1)
        attn = probs[:, :, 0] - lam * probs[:, :, 1]
        outs.append(jnp.einsum('bhqk,bhkd->bhqd', attn.astype(v.dtype), vb))
    o = jnp.concatenate(outs, axis=2)
    o = rmsnorm(o, head_g[None, :, None, :]) * (1.0 - lam_init)
    return o.transpose(0, 2, 1, 3).reshape(b, s, ATTN_WIDTH)

def causal_dwconv(u, w, bias):
    s = u.shape[1]
    upad = jnp.pad(u, ((0, 0), (CONV_WIDTH - 1, 0), (0, 0)))
    out = bias
    for j in range(CONV_WIDTH):
        out = out + w[j] * upad[:, j:j + s]
    return out

def second_inputs(seed: int = 0) -> dict:
    key = jax.random.key(seed)
    ks = jax.random.split(key, 20)
    nrm = lambda k, shape, s: jax.random.normal(k, shape, jnp.float32) * s
    x = jax.random.normal(ks[0], (BATCH, SEQ, D_MODEL), jnp.float32)
    offset = jax.random.randint(ks[1], (BATCH,), 0, 10000, dtype=jnp.int32)
    positions = offset[:, None] + jnp.arange(SEQ, dtype=jnp.int32)[None, :]
    return {
        "x": x,
        "positions": positions,
        "norm_mix_g": 1.0 + nrm(ks[2], (DEPTH, D_MODEL), 0.05),
        "w_in": nrm(ks[3], (DEPTH, D_MODEL, IN_WIDTH_2), D_MODEL ** -0.5),
        "pool_w": nrm(ks[4], (DEPTH, POOL_GROUPS, POOL_GROUP_DIM, POOL_GROUP_DIM), POOL_GROUP_DIM ** -0.5),
        "pool_scale": 1.0 + nrm(ks[5], (DEPTH, POOL_WIDTH), 0.05),
        "lambda_q1": nrm(ks[6], (DEPTH, DIFF_HEAD_DIM), 0.1),
        "lambda_k1": nrm(ks[7], (DEPTH, DIFF_HEAD_DIM), 0.1),
        "lambda_q2": nrm(ks[8], (DEPTH, DIFF_HEAD_DIM), 0.1),
        "lambda_k2": nrm(ks[9], (DEPTH, DIFF_HEAD_DIM), 0.1),
        "attn_norm_g": 1.0 + nrm(ks[10], (DEPTH, N_DIFF_HEADS, V_HEAD_DIM), 0.05),
        "w_o": nrm(ks[11], (DEPTH, MIX_WIDTH, D_MODEL), MIX_WIDTH ** -0.5),
        "norm_ffn_g": 1.0 + nrm(ks[12], (DEPTH, D_MODEL), 0.05),
        "w_up": nrm(ks[13], (DEPTH, D_MODEL, 2 * D_FF), D_MODEL ** -0.5),
        "conv_w": nrm(ks[14], (DEPTH, CONV_WIDTH, 2 * D_FF), CONV_WIDTH ** -0.5),
        "conv_b": nrm(ks[15], (DEPTH, 2 * D_FF), 0.02),
        "w_down": nrm(ks[16], (DEPTH, D_FF, D_MODEL), D_FF ** -0.5),
        "norm_final_g": 1.0 + nrm(ks[17], (D_MODEL,), 0.05),
    }

def second_block(x, positions, norm_mix_g, w_in, pool_w, pool_scale, lambda_q1, lambda_k1,
              lambda_q2, lambda_k2, attn_norm_g, w_o, norm_ffn_g, w_up, conv_w, conv_b,
              w_down, norm_final_g):
    b, s, _ = x.shape
    cos, sin = rope_tables(positions, x.dtype)
    for l in range(DEPTH):
        h = rmsnorm(x, norm_mix_g[l])
        proj = h @ w_in[l]
        p, q, k, v = jnp.split(
            proj, [POOL_WIDTH, POOL_WIDTH + ATTN_WIDTH, POOL_WIDTH + 2 * ATTN_WIDTH], axis=-1)
        pool_out = multiscale_pool(p, pool_w[l], pool_scale[l])
        q = apply_rope(q.reshape(b, s, N_DIFF_HEADS, 2, DIFF_HEAD_DIM), cos, sin)
        k = apply_rope(k.reshape(b, s, N_DIFF_HEADS, 2, DIFF_HEAD_DIM), cos, sin)
        q = q.transpose(0, 2, 3, 1, 4)
        k = k.transpose(0, 2, 3, 1, 4)
        v = v.reshape(b, s, N_DIFF_HEADS, V_HEAD_DIM).transpose(0, 2, 1, 3)
        lam_init = 0.8 - 0.6 * float(np.exp(-0.3 * l))
        lam = (jnp.exp(jnp.sum(lambda_q1[l].astype(jnp.float32) * lambda_k1[l].astype(jnp.float32)))
               - jnp.exp(jnp.sum(lambda_q2[l].astype(jnp.float32) * lambda_k2[l].astype(jnp.float32)))
               + lam_init)
        attn_out = diff_attention(q, k, v, lam, lam_init, attn_norm_g[l])
        mix = jnp.concatenate([pool_out, attn_out], axis=-1) @ w_o[l]
        x = x + mix
        h = rmsnorm(x, norm_ffn_g[l])
        u = causal_dwconv(h @ w_up[l], conv_w[l], conv_b[l])
        gate, val = jnp.split(u, 2, axis=-1)
        x = x + (jax.nn.silu(gate) * val) @ w_down[l]
    return rmsnorm(x, norm_final_g)


def setup_inputs(seed=0):
    out = dict(first_inputs(seed))
    for name, value in second_inputs(seed + 1).items():
        if name != "x":
            out[name + "_2"] = value
    return out


def reference(
    x, p, norm_mix, w_in, qk_norm_na, na_rel_bias, qk_norm_dil, w_branch_na, w_branch_dil,
    w_out, norm_ffn, peer_w_query, peer_sub_keys, peer_expert_u, peer_expert_v, norm_ple,
    w_ple_gate, w_ple, positions_2, norm_mix_g_2, w_in_2, pool_w_2, pool_scale_2, lambda_q1_2,
    lambda_k1_2, lambda_q2_2, lambda_k2_2, attn_norm_g_2, w_o_2, norm_ffn_g_2, w_up_2, conv_w_2,
    conv_b_2, w_down_2, norm_final_g_2,
):
    x = first_block(
        x, p, norm_mix, w_in, qk_norm_na, na_rel_bias, qk_norm_dil, w_branch_na, w_branch_dil,
        w_out, norm_ffn, peer_w_query, peer_sub_keys, peer_expert_u, peer_expert_v, norm_ple,
        w_ple_gate, w_ple,
    )
    return second_block(
        x, positions_2, norm_mix_g_2, w_in_2, pool_w_2, pool_scale_2, lambda_q1_2, lambda_k1_2,
        lambda_q2_2, lambda_k2_2, attn_norm_g_2, w_o_2, norm_ffn_g_2, w_up_2, conv_w_2,
        conv_b_2, w_down_2, norm_final_g_2,
    )


_drawn_inputs = setup_inputs


def setup_inputs(seed=0):
    import zlib

    import numpy as np

    out = dict(_drawn_inputs(seed))
    spreads = {}
    factors = {'qk_norm_na': 3.072,
     'qk_norm_dil': 3.832,
     'norm_ple': 5.058,
     'lambda_q1_2': 2.919,
     'conv_b_2': 5.147,
     'pool_scale_2': 2.752,
     'attn_norm_g_2': 3.005,
     'norm_ffn_g_2': 3.534}
    for name, (base, spread) in spreads.items():
        noise = np.random.default_rng([zlib.crc32(name.encode()), seed]).standard_normal(out[name].shape)
        drawn = base * np.exp(spread * noise) if base else spread * noise
        out[name] = jnp.asarray(drawn.astype(out[name].dtype))
    for name, factor in factors.items():
        out[name] = (out[name] * factor).astype(out[name].dtype)
    return out
```

```python
import math
from contextlib import ExitStack

import numpy as np
import concourse.bass as bass
from concourse import mybir

T = 256
NEG = -1.0e30
ROT_D = 16
NT = 64
STASH = 9
NSLOT = 4
RMS_EPS = 1e-6

COLS = {}
_at = 0
for _n, _w in (("nmix", 8), ("nffn", 8), ("nple", 8), ("nmix2", 8), ("nffn2", 8), ("nfin", 8),
               ("qna", 1), ("kna", 1), ("qdil", 1), ("kdil", 1), ("psc", 4), ("ang", 4),
               ("cw0", 44), ("cw1", 44), ("cw2", 44), ("cb", 44), ("lam", 4)):
    COLS[_n] = (_at, _w)
    _at += _w
NCOL = _at
C0 = {}
_at = 0
for _n, _w in (("ident", 128), ("iota", 128), ("blk", 2), ("o1024", 1), ("o128", 1), ("one", 1),
               ("invf", 1), ("permd", 128), ("permr", 128)):
    C0[_n] = (_at, _w)
    _at += _w
NC0 = _at
C1 = {}
_at = 0
for _n, _w in (("mna", 256), ("mg0", 512), ("mg1", 256), ("mg2", 256), ("cosd", 256), ("sind", 256),
               ("bsel", 1536)):
    C1[_n] = (_at, _w)
    _at += _w
NC1 = _at
C2 = {}
_at = 0
for _n, _w in (("mdf", 384), ("cnt", 1024)):
    C2[_n] = (_at, _w)
    _at += _w
NC2 = _at

DENSE = (("w_in", 8, 46), ("wbna", 4, 8), ("wbdil", 2, 8), ("wout", 8, 8), ("wq", 8, 16),
         ("wpg", 8, 8), ("wple", 2, 8), ("w_in2", 8, 16), ("wo2", 8, 8), ("wup", 8, 44), ("wdn", 22, 8))
SLOT0 = {}
_at = 0
for _n, _k, _m in DENSE:
    SLOT0[_n] = _at
    _at += _k * _m // 16
NDENSE = _at


def load_order():
    order = [("D", i) for i in range(SLOT0["wpg"])]
    order += [("U", j) for j in range(STASH)]
    for j in range(NT):
        order.append(("V", j))
        if j + STASH < NT:
            order.append(("U", j + STASH))
    order += [("D", i) for i in range(SLOT0["wpg"], NDENSE)]
    return order


class Queue:

    def __init__(self, sem):
        self.sem, self.n, self.items, self.seen = sem, 0, [], {}

    def op(self, fn, *waits, sig=True, chain=False):
        need = []
        waits = list(waits) + ([self.last()] if chain else [])
        for w in waits:
            if w is None or w[1] <= 0:
                continue
            if self.seen.get(id(w[0]), 0) >= w[1]:
                continue
            self.seen[id(w[0])] = w[1]
            need.append(w)
        self.items.append((need, fn, self.sem if sig else None, 1))
        if sig:
            self.n += 1
        return self.last()

    def dma(self, fn, sem, *waits):
        need = [w for w in waits if w is not None and w[1] > 0]
        self.items.append((need, fn, sem, 16))

    def last(self):
        return (self.sem, self.n)

    def emit(self, eng):
        for need, fn, sem, by in self.items:
            for s, v in need:
                eng.wait_ge(s, v)
            ins = fn(eng)
            if sem is not None:
                ins.then_inc(sem, by)


class Rot:

    def __init__(self, aps):
        self.aps, self.free, self.i = aps, [[] for _ in aps], 0

    def get(self):
        k = self.i % len(self.aps)
        self.i += 1
        w, self.free[k] = self.free[k], None
        assert w is not None
        return k, self.aps[k], w

    def rel(self, k, *toks):
        self.free[k] = list(toks)


def build(nc, A):
    f32 = mybir.dt.float32
    u32 = mybir.dt.uint32
    i32 = mybir.dt.int32
    ALU = mybir.AluOpType
    ACT = mybir.ActivationFunctionType
    AX = mybir.AxisListType.X
    SC = 0.125

    ctx = ExitStack()
    with ctx:
        def sem(name):
            return ctx.enter_context(nc.semaphore(name))

        def sb(name, w, dt=f32):
            return ctx.enter_context(nc.sbuf_tensor(name, [128, w], dt))

        RING = sb("RING", NSLOT * 2048)
        BIG = sb("BIG", 32768)
        XTt = sb("XT", 2048)
        HTt = sb("HT", 2048)
        CC = sb("CC", NC0)
        CL = sb("CL", NCOL)
        GS = sb("GS", STASH * 2 * 256)
        SM = sb("SM", 256)
        PS = ctx.enter_context(nc.psum_tensor("PS", [128, 4096], f32))
        XT = XTt[:, :].rearrange("p (c t) -> p c t", c=8)
        HT = HTt[:, :].rearrange("p (c t) -> p c t", c=8)

        def bank(i, w=512):
            return PS[:, 512 * i:512 * i + w]

        def col(name, i=0, w=1):
            return CL[:, COLS[name][0] + i:COLS[name][0] + i + w]

        def con(name):
            return CC[:, C0[name][0]:C0[name][0] + C0[name][1]]

        pe = Queue(sem("s_pe"))
        act = Queue(sem("s_act"))
        dve = Queue(sem("s_dve"))
        pool = Queue(sem("s_pool"))
        sp = Queue(sem("s_sp"))
        ident = con("ident")

        def mm(out, lhsT, rhs, *w, start=True, stop=True, sig=True, skip=False):
            return pe.op(lambda e: e.matmul(out, lhsT, rhs, start=start, stop=stop, skip_group_check=skip),
                         *w, sig=sig)

        def tr(out, in_, *w, sig=True):
            return pe.op(lambda e: e.transpose(out, in_, ident), *w, sig=sig)

        def a_act(out, in_, f, *w, chain=False, **kw):
            return act.op(lambda e: e.activation(out, in_, f, **kw), *w, chain=chain)

        def v_tt(out, a, b, op, *w, q=None, chain=False):
            return (q or dve).op(lambda e: e.tensor_tensor(out, a, b, op), *w, chain=chain)

        def v_ts(out, a, s1, s2, op0, op1, *w, q=None, chain=False):
            if op1 is None:
                return (q or dve).op(lambda e: e.tensor_scalar(out, a, s1, None, op0), *w, chain=chain)
            return (q or dve).op(lambda e: e.tensor_scalar(out, a, s1, s2, op0, op1), *w, chain=chain)

        def v_stt(out, a, s, b, op0, op1, *w, chain=False):
            return dve.op(lambda e: e.scalar_tensor_tensor(out, a, s, b, op0, op1), *w, chain=chain)

        def v_cp(out, a, *w, q=None, chain=False):
            return (q or dve).op(lambda e: e.tensor_copy(out, a), *w, chain=chain)

        def v_red(out, a, op, *w, chain=False, negate=None):
            return dve.op(lambda e: e.tensor_reduce(out, a, AX, op, negate=negate), *w, chain=chain)

        def v_rcp(out, a, *w, chain=False):
            return dve.op(lambda e: e.reciprocal(out, a), *w, chain=chain)

        def load(sname, dst, src, *waits, q=None):
            s = sem(sname)
            (q or sp).dma(lambda e: e.dma_start(dst, src), s, *waits)
            return (s, 16)

        t_c0 = load("s_c0", CC[:, :], A["c0"])
        t_cl = load("s_cl", CL[:, :], A["cols"])
        t_x = load("s_x", XTt[:, :], A["xT"])

        order = load_order()
        rsem = [sem(f"s_ring{i}") for i in range(NSLOT)]
        src = {"D": A["dense"], "U": A["eu"], "V": A["ev"]}
        ring = {"used": 0, "blk": 0}

        def issue(n, *waits):
            if n >= len(order):
                return
            kind, j = order[n]
            k = n % NSLOT
            sp.dma(lambda e: e.dma_start(RING[:, k * 2048:(k + 1) * 2048], src[kind][j]), rsem[k], *waits)

        for n in range(NSLOT):
            issue(n)

        def slot(kind):
            n = ring["used"]
            assert order[n][0] == kind
            k = n % NSLOT
            ap = RING[:, k * 2048:(k + 1) * 2048].rearrange("p (b m) -> p b m", b=16)
            return ap, (rsem[k], 16 * (n // NSLOT + 1))

        def slot_done(tok):
            n = ring["used"]
            ring["used"] += 1
            issue(n + NSLOT, tok)

        def barrier():
            toks = [q.last() for q in (pe, act, dve, pool)]
            return toks

        def linear(name, nch, kch, rhs, rhs_w, evac, rot, half=False):
            for n in range(nch):
                if not half or n % 2 == 0:
                    k_, ps, free = rot.get()
                o = ps[:, (n % 2) * 256:(n % 2) * 256 + 256] if half else ps[:, 0:256]
                for kk in range(kch):
                    ap, ld = slot("D")
                    b = ring["blk"] % 16
                    end = b == 15
                    w = (list(free) if kk == 0 else []) + list(rhs_w(kk)) + ([ld] if b == 0 or kk == 0 else [])
                    t = mm(o, ap[:, b, :], rhs(kk), *w, start=kk == 0, stop=kk == kch - 1,
                           sig=end or kk == kch - 1)
                    ring["blk"] += 1
                    if end:
                        slot_done(t)
                free = []
                if half and n % 2 == 0:
                    continue
                rot.rel(k_, *evac(n, ps, t))
                yield

        def linear_nat(nslots, lhs, lhs_w, evac, rot):
            for n in range(nslots):
                ap, ld = slot("D")
                v = ap.rearrange("p (n k) m -> p n k m", n=2)
                assert ring["blk"] % 16 == 0
                ring["blk"] += 16
                for tt in range(2):
                    k_, ps, free = rot.get()
                    o = ps[:, 0:256].rearrange("p (n m) -> p n m", n=2)
                    for kk in range(8):
                        t = mm(o, lhs(kk, tt), v[:, :, kk, :], ld, *free, *lhs_w(kk),
                               start=kk == 0, stop=kk == 7, sig=kk == 7)
                    rot.rel(k_, *evac(n, tt, ps, t))
                slot_done(t)
                yield

        lin = Rot([bank(0), bank(1)])
        scr = Rot([bank(2), bank(3)])
        pvr = Rot([bank(4)])
        trr = Rot([bank(5), bank(6)])
        stat_free = []
        sm_at = [0]

        def small(w):
            a = sm_at[0]
            sm_at[0] += w
            assert sm_at[0] <= 256
            return SM[:, a:a + w]

        def rmsnorm(gname, xw, hw, out=None):
            nonlocal stat_free
            dst = HT if out is None else out
            sq = []
            for c in range(4):
                sq.append(a_act(dst[:, 2 * c:2 * c + 2, :], XT[:, 2 * c:2 * c + 2, :], ACT.Square, *xw, *hw))
            st = bank(7)
            for tt in range(2):
                for c in range(8):
                    t = mm(st[:, tt:tt + 1], dst[:, c, tt * 128:tt * 128 + 128], con("o1024"),
                           sq[c // 2], t_c0, *stat_free, start=c == 0, stop=c == 7, sig=c == 7)
            ms, sd, rs = small(2), small(2), small(2)
            t1 = v_ts(ms, st[:, 0:2], RMS_EPS, None, ALU.add, None, t)
            t2 = a_act(sd, ms, ACT.Sqrt, t1)
            t3 = v_rcp(rs, sd, t2)
            k_, ps, free = lin.get()
            for tt in range(2):
                t = mm(ps[:, tt * 128:tt * 128 + 128], rs[:, tt:tt + 1].to_broadcast([128, 128]), ident,
                       t3, *free, sig=tt == 1)
            out_t = []
            for c in range(8):
                out_t.append(v_stt(dst[:, c, :], XT[:, c, :], col(gname, c), ps[:, 0:256], ALU.mult, ALU.mult,
                                   t, t_cl))
            lin.rel(k_, out_t[-1])
            stat_free = [t1]
            return out_t

        class Arena:
            def __init__(self):
                self.at = 0

            def take(self, w):
                a = self.at
                self.at += w
                assert self.at <= 32768, self.at
                return BIG[:, a:a + w]

        def head_stats(sqs, sts, n, rs, st, st_w, ocol, eps_buf, sd_buf):
            t1 = v_ts(eps_buf, st, RMS_EPS, None, ALU.add, None, *st_w)
            t2 = a_act(sd_buf, eps_buf, ACT.Sqrt, t1)
            return t1, v_rcp(rs, sd_buf, t2)

        ar = Arena()
        c1 = ar.take(NC1)
        bias = ar.take(4096)
        t_c1 = load("s_c1", c1, A["c1"])
        t_bias = load("s_bias", bias, A["nab"])
        c1v = {n: c1[:, a:a + w] for n, (a, w) in C1.items()}
        bias4 = bias.rearrange("p (h a k) -> p h a k", h=8, a=2)
        qka = ar.take(8 * 256).rearrange("p (c t) -> p c t", c=8)
        qkd = ar.take(12 * 256).rearrange("p (c t) -> p c t", c=12)
        va = ar.take(1024).rearrange("p (a n) -> p a n", a=2)
        vd = ar.take(1536).rearrange("p (a n) -> p a n", a=2)
        gates = ar.take(4096).rearrange("p (c t) -> p c t", c=16)
        ona = ar.take(1024).rearrange("p (c t) -> p c t", c=4)
        odl = ar.take(512).rearrange("p (c t) -> p c t", c=2)
        sqr = Rot([ar.take(256) for _ in range(3)])
        sbuf_s = Rot([ar.take(1536) for _ in range(3)])
        sbuf_t = Rot([ar.take(1536) for _ in range(2)])
        qd_m = Rot([ar.take(256) for _ in range(3)])

        t_bm = None
        for h in range(8):
            for a in range(2):
                t_bm = v_tt(bias4[:, h, a, :], bias4[:, h, a, :], c1v["mna"], ALU.add, t_c1, t_bias, q=pool)

        h_t = rmsnorm("nmix", [t_x], [])

        def rhs_h(kk):
            return HT[:, kk, :]

        def w_h(kk):
            return [h_t[kk]]

        ssq = bank(7)[:, 64:64 + 80].rearrange("p (a n) -> p a n", a=2)
        sq_free = []

        def evac_qk(dst, base):
            def f(n, ps, t):
                k_, sq, free = sqr.get()
                t1 = v_cp(dst[:, n, :], ps[:, 0:256], t)
                t2 = a_act(sq, dst[:, n, :], ACT.Square, t1, *free)
                c = 2 * (base + n)
                for tt in range(2):
                    t3 = mm(ssq[:, tt, c:c + 2], sq[:, tt * 128:tt * 128 + 128], con("blk"), t2, *stat_free,
                            sig=tt == 1)
                sqr.rel(k_, t3)
                return [t1]
            return f

        def qk_scale(dst, nq, n, base, gq, gk, rs, trs):
            out = []
            k_, ps, free = lin.get()
            for tt in range(2):
                t = mm(ps[0:2 * n, tt * 128:tt * 128 + 128], rs[:, tt, 2 * base:2 * base + 2 * n], ident,
                       trs, *free, sig=tt == 1)
            tT = v_cp(rsT[0:2 * n, :], ps[0:2 * n, 0:256], t)
            lin.rel(k_, tT)
            bsel = c1v["bsel"]
            for c in range(n):
                k_, ps, free = lin.get()
                t = mm(ps[:, 0:256], bsel[0:2 * n, c * 128:c * 128 + 128], rsT[0:2 * n, :], tT, t_c1, *free)
                g = col(gq) if c < nq else col(gk)
                t = v_stt(dst[:, c, :], dst[:, c, :], g, ps[:, 0:256], ALU.mult, ALU.mult, t)
                lin.rel(k_, t)
                out.append(t)
                yield out

        def run(gen):
            for _ in gen:
                pass

        def weave(main, fill, n=1):
            for _ in main:
                for _ in range(n):
                    next(fill, None)
            run(fill)

        run(linear("w_in", 8, 8, rhs_h, w_h, evac_qk(qka, 0), lin))
        tq = pe.last()
        ms = ar.take(80).rearrange("p (a n) -> p a n", a=2)
        sd = ar.take(80).rearrange("p (a n) -> p a n", a=2)
        rsT = ar.take(256)
        rsq = ar.take(80).rearrange("p (a n) -> p a n", a=2)

        def stats(lo, hi, w):
            nonlocal stat_free
            t1 = v_ts(ms[:, :, lo:hi], ssq[:, :, lo:hi], RMS_EPS, None, ALU.add, None, w)
            stat_free = [t1]
            t2 = a_act(sd[:, :, lo:hi], ms[:, :, lo:hi], ACT.Sqrt, t1)
            return v_rcp(rsq[:, :, lo:hi], sd[:, :, lo:hi], t2)

        trs = stats(0, 16, tq)

        def evac_v(dst):
            def f(n, tt, ps, t):
                return [a_act(dst[:, tt, n * 256:n * 256 + 256], ps[:, 0:256], ACT.Copy, t)]
            return f

        def lhs_h(kk, tt):
            return HT[:, kk, tt * 128:tt * 128 + 128]

        run(linear_nat(2, lhs_h, w_h, evac_v(va), lin))
        run(qk_scale(qka, 4, 8, 0, "qna", "kna", rsq, trs))
        t_qk = dve.last()
        t_va = act.last()

        def softmax(S, W, w):
            nm, z, rz = S["nm"], S["z"], S["rz"]
            t = v_red(nm, S["s"], ALU.max, w, negate=True)
            te = []
            for a in range(2):
                te.append(a_act(S["s"][:, a, :], S["s"][:, a, :], ACT.Exp, t, bias=nm[:, a:a + 1],
                                accum_out=z[:, a:a + 1]))
            t = v_rcp(rz, z, te[1])
            for a in range(2):
                t = v_ts(S["s"][:, a, :], S["s"][:, a, :], rz[:, a:a + 1], None, ALU.mult, None, t)
            return t

        statb = ar.take(12 * 6).rearrange("p (n k) -> p n k", n=12)

        def attention(heads, scores, vlist, put, base):
            st = {}
            for i in range(len(heads) + 2):
                if i < len(heads):
                    h = heads[i]
                    k_, s, free = sbuf_s.get()
                    W, tok = scores(h, s, free)
                    sv = s[:, 0:2 * W].rearrange("p (a w) -> p a w", a=2)
                    b = statb[:, base + i, :]
                    S = {"s": sv, "nm": b[:, 0:2], "z": b[:, 2:4], "rz": b[:, 4:6], "k": k_, "W": W}
                    S["tok"] = softmax(S, W, tok)
                    st[i] = S
                    yield
                if 0 <= i - 1 < len(heads):
                    S = st[i - 1]
                    kt, pt, ptfree = sbuf_t.get()
                    ptv = pt.rearrange("p (c t) -> p c t", t=256)
                    te = []
                    for c in range(S["W"] // 256):
                        k_, ps, free = trr.get()
                        psv = ps.rearrange("p (j t) -> p j t", j=2)
                        for j in range(2):
                            for a in range(2):
                                t = tr(psv[:, j, a * 128:a * 128 + 128],
                                       S["s"][:, a, c * 256 + j * 128:c * 256 + j * 128 + 128],
                                       S["tok"], *free, sig=j == 1 and a == 1)
                        w = list(ptfree) + [t]
                        t2 = a_act(ptv[:, 2 * c:2 * c + 2, :], psv, ACT.Copy, *w)
                        te.append(t2)
                        trr.rel(k_, t2)
                    sbuf_s.rel(S["k"], t)
                    S["pt"], S["ptk"], S["te"] = ptv, kt, te
                    yield
                if 0 <= i - 2:
                    S = st.pop(i - 2)
                    h = heads[i - 2]
                    if (i - 2) % 2 == 0:
                        k_pv, pv, pvfree = pvr.get()
                    r = 64 * (h % 2)
                    n = S["W"] // 128
                    for c in range(n):
                        t = mm(pv[r:r + 64, 0:256], vlist(h, c), S["pt"][:, c, :], S["te"][c // 2], *pvfree,
                               start=c == 0, stop=c == n - 1, sig=c == n - 1)
                    sbuf_t.rel(S["ptk"], t)
                    if (i - 2) % 2 == 1:
                        pvr.rel(k_pv, put(h // 2, pv, t))
                    yield

        def na_scores(h, s, free):
            k_, ps, pf = scr.get()
            r = 64 * (h % 2)
            for a in range(2):
                t = mm(ps[:, a * 256:a * 256 + 256], qka[r:r + 64, h // 2, a * 128:a * 128 + 128],
                       qka[r:r + 64, 4 + h // 2, :], t_qk, *pf, sig=a == 1)
            t = v_stt(s[:, 0:512], ps, SC, bias4[:, h, :, :].rearrange("p a k -> p (a k)"), ALU.mult, ALU.add,
                      t, t_bm, *free)
            scr.rel(k_, t)
            return 256, t

        def put_na(c, pv, t):
            return v_cp(ona[:, c, :], pv[:, 0:256], t)

        def fill1():
            yield from linear("w_in", 12, 8, rhs_h, w_h, evac_qk(qkd, 8), lin)
            yield from linear_nat(3, lhs_h, w_h, evac_v(vd), lin)

        weave(attention(list(range(8)), na_scores, lambda h, c: va[:, c, h * 64:h * 64 + 64], put_na, 0),
              fill1(), 1)
        t_vd = act.last()

        def evac_gate(n, ps, t):
            return [a_act(gates[:, n, :], ps[:, 0:256], ACT.Sigmoid, t)]

        fill = linear("w_in", 16, 8, rhs_h, w_h, evac_gate, lin)
        trs = stats(16, 40, pe.last())
        gen = qk_scale(qkd, 6, 12, 8, "qdil", "kdil", rsq, trs)
        prev = None
        rot_t = []
        for c, toks in enumerate(gen):
            k_, ps, free = scr.get()
            t = mm(ps[:, 0:256], con("permd"), qkd[:, c, :], toks[c], *free)
            k2, m, mf = qd_m.get()
            t1 = v_tt(m, qkd[:, c, :], c1v["cosd"], ALU.mult, toks[c], *mf, q=pool)
            t2 = v_tt(qkd[:, c, :], ps[:, 0:256], c1v["sind"], ALU.mult, t, t1)
            scr.rel(k_, t2)
            t3 = v_tt(qkd[:, c, :], qkd[:, c, :], m, ALU.add, t2)
            qd_m.rel(k2, t3)
            if c % 4 == 3:
                next(fill)
        t_qd = dve.last()

        def dil_scores(hh, s, free):
            s4 = s.rearrange("p (a g k) -> p a g k", a=2, g=3)
            for g in range(3):
                k_, ps, pf = scr.get()
                head = 4 * g + hh
                r = 64 * (head % 2)
                for a in range(2):
                    t = mm(ps[:, a * 256:a * 256 + 256], qkd[r:r + 64, head // 2, a * 128:a * 128 + 128],
                           qkd[r:r + 64, 6 + head // 2, :], t_qd, *pf, sig=a == 1)
                if g == 0:
                    m = c1v["mg0"].rearrange("p (a k) -> p a k", a=2)
                else:
                    m = c1v[f"mg{g}"].unsqueeze(1).to_broadcast([128, 2, 256])
                t = v_stt(s4[:, :, g, :], ps.rearrange("p (a k) -> p a k", a=2), SC, m, ALU.mult, ALU.add,
                          t, t_c1, *free)
                scr.rel(k_, t)
            return 768, t

        def put_dil(c, pv, t):
            return v_cp(odl[:, c, :], pv[:, 0:256], t)

        weave(attention(list(range(4)), dil_scores,
                        lambda h, c: vd[:, c % 2, (4 * (c // 2) + h) * 64:(4 * (c // 2) + h) * 64 + 64],
                        put_dil, 8), fill, 1)
        t_att = dve.last()
        t_gate = act.last()

        mrg = qka
        mt = []

        def evac_na(n, ps, t):
            t1 = v_tt(mrg[:, n, :], ps[:, 0:256], gates[:, n, :], ALU.mult, t, t_gate, pe_att)
            return [t1]

        pe_att = pe.last()
        run(linear("wbna", 8, 4, lambda kk: ona[:, kk, :], lambda kk: [t_att], evac_na, lin))

        def evac_dl(n, ps, t):
            k_, m, mf = qd_m.get()
            t1 = v_tt(m, ps[:, 0:256], gates[:, 8 + n, :], ALU.mult, t, *mf)
            t2 = v_tt(mrg[:, n, :], mrg[:, n, :], m, ALU.add, t1)
            qd_m.rel(k_, t2)
            mt.append(t2)
            return [t1]

        run(linear("wbdil", 8, 2, lambda kk: odl[:, kk, :], lambda kk: [t_att], evac_dl, lin))
        xt = []

        def evac_x(n, ps, t):
            t1 = v_tt(XT[:, n, :], XT[:, n, :], ps[:, 0:256], ALU.add, t)
            xt.append(t1)
            return [t1]

        run(linear("wout", 8, 8, lambda kk: mrg[:, kk, :], lambda kk: [mt[kk]], evac_x, lin))

        fence = barrier()
        ar = Arena()
        h_t = rmsnorm("nffn", [xt[-1]], [pe.last()])
        keysT = ar.take(256).rearrange("p (a n) -> p a n", a=2)
        t_keys = load("s_keys", keysT.rearrange("p a n -> p (a n)"), A["keysT"], *fence)
        qp = ar.take(4096).rearrange("p (c t) -> p c t", c=16)
        Ssc = ar.take(4096).rearrange("p (a c n) -> p a c n", a=2, c=16)
        top = ar.take(2 * 16 * 16).rearrange("p (a c n) -> p a c n", a=2, c=16)
        ixu = ar.take(2 * 16 * 16).bitcast(u32).rearrange("p (a c n) -> p a c n", a=2, c=16)
        ixf = ar.take(2 * 16 * 16).rearrange("p (a c n) -> p a c n", a=2, c=16)
        cand = ar.take(4096).rearrange("p (a h n) -> p a h n", a=2, h=8)
        scv = ar.take(256).rearrange("p (a h n) -> p a h n", a=2, h=8)
        posu = ar.take(256).bitcast(u32).rearrange("p (a h n) -> p a h n", a=2, h=8)
        abu = ar.take(512).bitcast(u32).rearrange("p (b a h n) -> p b a h n", b=2, a=2, h=8)
        abf = ar.take(512).rearrange("p (b a h n) -> p b a h n", b=2, a=2, h=8)
        eq = ar.take(2048).rearrange("p (h k j) -> p h k j", h=8, k=16)
        sel = ar.take(768).rearrange("p (b a n) -> p b a n", b=3, a=2)
        ssum = ar.take(32).rearrange("p (b a h) -> p b a h", b=2, a=2)

        qt_ = []

        def evac_qp(n, ps, t):
            t1 = a_act(qp[:, n, :], ps[:, 0:256], ACT.Copy, t, *fence)
            qt_.append(t1)
            return [t1]

        gq = linear("wq", 16, 8, rhs_h, lambda kk: [h_t[kk]], evac_qp, lin)
        st_tok = {}

        def score_pair(c4):
            for a in range(2):
                k_, ps, free = scr.get()
                for j in range(4):
                    c = 4 * c4 + j
                    t = mm(ps[:, j * 128:j * 128 + 128], qp[:, c, a * 128:a * 128 + 128], keysT[:, c % 2, :],
                           qt_[c], t_keys, *free, sig=j == 3)
                t = a_act(Ssc[:, a, 4 * c4:4 * c4 + 4, :], ps.rearrange("p (c n) -> p c n", c=4), ACT.Copy, t)
                scr.rel(k_, t)
                st_tok[a, c4] = t

        for n in range(17):
            next(gq, None)
            if n % 4 == 0 and n:
                score_pair(n // 4 - 1)
        assert len(qt_) == 16

        upr = Rot([bank(5), bank(6)])
        stash = Rot([GS[:, i * 256:i * 256 + 256] for i in range(2 * STASH)])
        upr.free = [list(f) for f in trr.free]
        ga = {}

        def u_slot(j):
            ap, ld = slot("U")
            for e in range(2):
                k_, ps, free = upr.get()
                ks, g, gf = stash.get()
                for c in range(8):
                    t = mm(ps[:, 0:256], ap[:, 8 * e + c, :], HT[:, c, :], ld, h_t[c], *free,
                           start=c == 0, stop=c == 7, sig=c == 7)
                t2 = a_act(g, ps[:, 0:256], ACT.Gelu, t, *gf)
                upr.rel(k_, t2)
                ga[2 * j + e] = (ks, g, t2)
            slot_done(t)

        def top16(vals, vt, it, w):
            t = dve.op(lambda e: e.max(vt[:, 0:8], vals), *w)
            ti = dve.op(lambda e: e.max_index(it[:, 0:8], vt[:, 0:8], vals), t)
            t = dve.op(lambda e: e.match_replace(vals, vt[:, 0:8], vals, -3.0e38), t, ti)
            t = dve.op(lambda e: e.max(vt[:, 8:16], vals), t)
            return dve.op(lambda e: e.max_index(it[:, 8:16], vt[:, 8:16], vals), t)

        for a in range(2):
            for c in range(16):
                top16(Ssc[:, a, c, :], top[:, a, c, :], ixu[:, a, c, :], [st_tok[a, c // 4], *fence])
            t = dve.last()
            v_cp(ixf[:, a], ixu[:, a], t)
            tv = top[:, a].rearrange("p (h b) n -> p h b n", b=2)
            cv = cand[:, a].rearrange("p h (i j) -> p h i j", i=16)
            t = v_tt(cv, tv[:, :, 0, :].unsqueeze(3).to_broadcast([128, 8, 16, 16]),
                     tv[:, :, 1, :].unsqueeze(2).to_broadcast([128, 8, 16, 16]), ALU.add, t)
            for h in range(8):
                top16(cand[:, a, h, :], scv[:, a, h, :], posu[:, a, h, :], [t])
            t = dve.last()
            ta = dve.op(lambda e, a=a: e.tensor_scalar(abu[:, 0, a], posu[:, a], 4, None,
                                                       ALU.logical_shift_right), t)
            tb = dve.op(lambda e, a=a: e.tensor_scalar(abu[:, 1, a], posu[:, a], 15, None,
                                                       ALU.bitwise_and), t)
            g_ = sel[:, 2, a, :].rearrange("p (h k) -> p h k", h=8)
            t = v_tt(g_, scv[:, a], scv[:, a, :, 0:1].to_broadcast([128, 8, 16]), ALU.subtract, t)
            t = a_act(g_, g_, ACT.Exp, t)
            t = v_red(ssum[:, 0, a], g_, ALU.add, t)
            t = v_rcp(ssum[:, 1, a], ssum[:, 0, a], t)
            t = v_tt(g_, g_, ssum[:, 1, a].unsqueeze(2).to_broadcast([128, 8, 16]), ALU.mult, t)
            t = v_cp(abf[:, :, a], abu[:, :, a], ta, tb)
            for b in range(2):
                ab = abf[:, b, a].unsqueeze(3).to_broadcast([128, 8, 16, 16])
                io = con("iota")[:, 0:16].unsqueeze(1).unsqueeze(1).to_broadcast([128, 8, 16, 16])
                t = v_tt(eq, ab, io, ALU.is_equal, t)
                iv = ixf[:, a].rearrange("p (h b) n -> p h b n", b=2)[:, :, b, :]
                t = v_tt(eq, eq, iv.unsqueeze(2).to_broadcast([128, 8, 16, 16]), ALU.mult, t)
                t = v_red(sel[:, b, a, :].rearrange("p (h k) -> p h k", h=8), eq, ALU.add, t)
        t_sel = dve.last()

        T3 = XF = ctx.enter_context(nc.sbuf_tensor("T3", [128, 768], f32))
        T3v = T3[:, :].rearrange("p (b t) -> p b t", b=3)
        for j in range(STASH):
            u_slot(j)
        for a in range(2):
            k_, ps, free = scr.get()
            for b in range(3):
                t = tr(ps[:, b * 128:b * 128 + 128], sel[:, b, a, :], t_sel, *free, sig=b == 2)
            t = v_cp(T3v[:, :, a * 128:a * 128 + 128], ps[:, 0:384].rearrange("p (b t) -> p b t", b=3), t)
            scr.rel(k_, t)
        t_T3 = t
        fence = barrier()
        G = BIG[:, :].rearrange("p (i t) -> p i t", t=256)
        ohb = ctx.enter_context(nc.sbuf_tensor("ohb", [128, 6 * 256], f32))
        oh = Rot([ohb[:, i * 256:i * 256 + 256] for i in range(6)])
        iota = con("iota")
        gev = Rot([bank(0), bank(1), bank(2), bank(3)])
        g_tok = None
        for t4 in range(64):
            kb, ps, pf = gev.get()
            for j in range(4):
                t_ = 4 * t4 + j
                k_, o, of = oh.get()
                q = pool if j == 3 else dve
                t1 = v_ts(o[:, 0:128], iota, T3v[:, 0, t_:t_ + 1], None, ALU.is_equal, None, t_T3, *of, q=q)
                t2 = v_ts(o[:, 128:256], iota, T3v[:, 1, t_:t_ + 1], T3v[:, 2, t_:t_ + 1], ALU.is_equal,
                          ALU.mult, t_T3, *of)
                t = mm(ps[:, j * 128:j * 128 + 128], o[:, 0:128], o[:, 128:256], t1, t2, *pf)
                oh.rel(k_, t)
            dst = G[:, :, 4 * t4:4 * t4 + 4]
            srcp = ps.rearrange("p (j i) -> p i j", j=4)
            if t4 % 4 == 3:
                g_tok2 = v_cp(dst, srcp, t, *fence)
                gev.rel(kb, g_tok2)
            else:
                g_tok = a_act(dst, srcp, ACT.Copy, t, *fence)
                gev.rel(kb, g_tok)
        t_G = [g_tok, g_tok2]

        for j in range(NT):
            ap, ld = slot("V")
            for e in range(2):
                i2 = 2 * j + e
                ks, g, tg = ga.pop(i2)
                ta = v_tt(G[:, i2, :], g, G[:, i2, :], ALU.mult, tg, *t_G)
                stash.rel(ks, ta)
                for c in range(8):
                    t = mm(bank(c // 2)[:, (c % 2) * 256:(c % 2) * 256 + 256], ap[:, 8 * e + c, :], G[:, i2, :],
                           ld, ta, *t_G, start=i2 == 0 and c % 2 == 0, stop=i2 == 2 * NT - 1 and c % 2 == 1,
                           sig=c == 7, skip=True)
            slot_done(t)
            if j + STASH < NT:
                u_slot(j + STASH)
        xt = []
        for c in range(4):
            xt.append(v_tt(XT[:, 2 * c:2 * c + 2, :], XT[:, 2 * c:2 * c + 2, :],
                           bank(c).rearrange("p (j t) -> p j t", j=2), ALU.add, t))

        fence = barrier()
        lin.free = [[xt[-1]], [xt[-1]]]
        scr.free = [[xt[-1]], [xt[-1]]]
        trr.free = [list(f) for f in upr.free]
        sm_at[0] = 32
        h_t = rmsnorm("nple", [xt[-1]], [pe.last()])
        ar = Arena()
        c2 = ar.take(NC2)
        t_c2 = load("s_c2", c2, A["c2"], *fence)
        pT = ar.take(512).rearrange("p (c t) -> p c t", c=2)
        t_p = load("s_p", pT.rearrange("p c t -> p (c t)"), A["pT"], *fence)
        posi = ar.take(256).bitcast(i32)
        t_pos = load("s_pos", posi, A["pos"].partition_broadcast(128), *fence)
        pg = ar.take(2048).rearrange("p (c t) -> p c t", c=8)
        tg_ = []

        def evac_pg(n, ps, t):
            t1 = a_act(pg[:, n, :], ps[:, 0:256], ACT.Sigmoid, t, *fence)
            tg_.append(t1)
            return [t1]

        run(linear("wpg", 8, 8, rhs_h, lambda kk: [h_t[kk]], evac_pg, lin))
        xt = []

        def evac_ple(n, ps, t):
            t1 = v_tt(pg[:, n, :], ps[:, 0:256], pg[:, n, :], ALU.mult, t, tg_[n])
            xt.append(v_tt(XT[:, n, :], XT[:, n, :], pg[:, n, :], ALU.add, t1))
            return [t1]

        run(linear("wple", 8, 2, lambda kk: pT[:, kk, :], lambda kk: [t_p], evac_ple, lin))

        posf = ar.take(256)
        ang = ar.take(256)
        kq = ar.take(256)
        cosr = ar.take(256)
        sinr = ar.take(256)
        TWO_PI = 2.0 * math.pi
        P1 = 6.28125
        P2 = math.floor((TWO_PI - P1) * 2.0 ** 18) / 2.0 ** 18
        P3 = TWO_PI - P1 - P2
        MAGIC = 12582912.0
        t = v_cp(posf, posi, t_pos, *fence)
        t_ang = v_ts(ang, posf, con("invf"), None, ALU.mult, None, t)
        PI_ = 3.1415925
        for dst, quarter in ((sinr, 0.0), (cosr, 0.25)):
            t = v_ts(kq, ang, 1.0 / TWO_PI, quarter, ALU.mult, ALU.add, t_ang, chain=True)
            t = v_ts(kq, kq, MAGIC, None, ALU.add, None, t)
            t = v_ts(kq, kq, MAGIC, None, ALU.subtract, None, t)
            t = v_stt(dst, kq, -P1, ang, ALU.mult, ALU.add, t)
            t = v_stt(dst, kq, -P2, dst, ALU.mult, ALU.add, t)
            t = v_stt(dst, kq, -P3, dst, ALU.mult, ALU.add, t)
            if quarter:
                t = v_ts(dst, dst, math.pi / 2, None, ALU.add, None, t)
            t = v_ts(dst, dst, PI_, -PI_, ALU.min, ALU.max, t)
            t_sin = a_act(dst, dst, ACT.Sin, t)

        h_t = rmsnorm("nmix2", [xt[-1]], [pe.last()])
        pT_ = ar.take(1024).rearrange("p (c t) -> p c t", c=4)
        qk2 = ar.take(2048).rearrange("p (c t) -> p c t", c=8)
        v2 = ar.take(1024).rearrange("p (a n) -> p a n", a=2)
        mixT = ar.take(2048).rearrange("p (c t) -> p c t", c=8)
        poolw = ar.take(512).rearrange("p (g n) -> p g n", g=4)
        t_pw = load("s_pw", poolw.rearrange("p g n -> p (g n)"), A["poolw"], *fence)
        wa = ar.take(256)
        wb = ar.take(256)
        dT = ar.take(1024).rearrange("p (c t) -> p c t", c=4)
        lm = ar.take(8)

        v_tt(lm[:, 0:1], col("lam", 0), col("lam", 1), ALU.mult, t_cl, *fence)
        t = v_tt(lm[:, 1:2], col("lam", 2), col("lam", 3), ALU.mult)
        st = bank(7)
        t = mm(st[:, 0:2], con("one").to_broadcast([128, 128]), lm[:, 0:2], t, *stat_free)
        t = a_act(lm[:, 2:4], st[:, 0:2], ACT.Exp, t)
        stat_free = [t]
        LAM0 = 0.8 - 0.6 * float(np.exp(-0.0))
        t = v_tt(lm[:, 4:5], lm[:, 2:3], lm[:, 3:4], ALU.subtract, t)
        t = v_ts(lm[:, 5:6], lm[:, 4:5], LAM0, -1.0, ALU.add, ALU.mult, t)

        def evac_p(n, ps, t):
            t = a_act(pT_[:, n, :], ps[:, 0:256], ACT.Copy, t, *fence)
            return [t]

        run(linear("w_in2", 4, 8, rhs_h, lambda kk: [h_t[kk]], evac_p, lin))
        t_pT = act.last()
        qt2 = []

        def evac_q2(n, ps, t):
            t = a_act(qk2[:, n, :], ps[:, 0:256], ACT.Copy, t)
            qt2.append(t)
            return [t]

        def gen_pool():
            for g in range(4):
                cur, tcur = pT_[:, g, :], t_pT
                for lv in range(g + 1):
                    s = 1 << lv
                    nxt = wa if lv % 2 == 0 else wb
                    t1 = v_cp(nxt[:, 0:s], cur[:, 0:s], tcur, chain=True)
                    tcur = v_tt(nxt[:, s:256], cur[:, s:256], cur[:, 0:256 - s], ALU.add, t1)
                    cur = nxt
                cn = c2[:, C2["cnt"][0] + 256 * g:C2["cnt"][0] + 256 * g + 256]
                t1 = v_tt(dT[:, g, :], cur, cn, ALU.mult, tcur, t_c2)
                t1 = v_tt(dT[:, g, :], dT[:, g, :], pT_[:, g, :], ALU.subtract, t1)
                k_, ps, free = trr.get()
                t2 = mm(ps[:, 0:256], poolw[:, g, :], dT[:, g, :], t1, t_pw, *free)
                t3 = a_act(mixT[:, g, :], ps[:, 0:256], ACT.Copy, t2, scale=col("psc", g))
                trr.rel(k_, t3)
                yield

        weave(gen_pool(), linear("w_in2", 8, 8, rhs_h, lambda kk: [h_t[kk]], evac_q2, lin), 2)
        fv = linear_nat(2, lhs_h, lambda kk: [h_t[kk]], evac_v(v2), lin)
        rm = Rot([ar.take(256) for _ in range(2)])
        for c in range(8):
            k_, ps, free = scr.get()
            t = mm(ps[:, 0:256], con("permr"), qk2[:, c, :], qt2[c], *free)
            k2, m, mf = rm.get()
            t1 = v_tt(m, qk2[:, c, :], cosr, ALU.mult, qt2[c], t_sin, *mf, q=pool)
            t2 = v_tt(qk2[:, c, :], ps[:, 0:256], sinr, ALU.mult, t, t1, t_sin)
            scr.rel(k_, t2)
            t3 = v_tt(qk2[:, c, :], qk2[:, c, :], m, ALU.add, t2)
            rm.rel(k2, t3)
            if c % 4 == 3:
                next(fv, None)
        run(fv)
        t_q2 = dve.last()
        t_v2 = act.last()

        sb2 = Rot([ar.take(768) for _ in range(4)])
        sb3 = Rot([ar.take(384) for _ in range(2)])
        osb = ar.take(1024).rearrange("p (c t) -> p c t", c=4)
        osq = ar.take(256)
        sst = ar.take(4 * 12).rearrange("p (h n) -> p h n", h=4)
        mdf = c2[:, 0:384]
        S2 = {}

        def d_scores(h):
            k_, s, free = sb2.get()
            sv = s.rearrange("p (n w) -> p n w", n=2)
            for n in range(2):
                kp, ps, pf = scr.get()
                r = 64 * n
                mm(ps[:, 0:128], qk2[r:r + 64, h, 0:128], qk2[r:r + 64, 4 + h, 0:128], t_q2, *pf, sig=False)
                t = mm(ps[:, 128:384], qk2[r:r + 64, h, 128:256], qk2[r:r + 64, 4 + h, :])
                t = v_stt(sv[:, n, :], ps[:, 0:384], SC, mdf, ALU.mult, ALU.add, t, t_c2, *free)
                scr.rel(kp, t)
            b = sst[:, h, :]
            segs = ((0, 128), (128, 384))
            v_red(b[:, 0:2], sv[:, :, 0:128], ALU.max, t, negate=True)
            t = v_red(b[:, 2:4], sv[:, :, 128:384], ALU.max, t, negate=True)
            for i, (lo, hi) in enumerate(segs):
                for n in range(2):
                    te = a_act(sv[:, n, lo:hi], sv[:, n, lo:hi], ACT.Exp, t,
                               bias=b[:, 2 * i + n:2 * i + n + 1], accum_out=b[:, 4 + 2 * i + n:5 + 2 * i + n])
            t = v_rcp(b[:, 8:12], b[:, 4:8], te)
            for i, (lo, hi) in enumerate(segs):
                t1 = v_ts(b[:, 4 + i:5 + i], b[:, 9 + 2 * i:10 + 2 * i], lm[:, 5:6], None, ALU.mult, None, t)
                t2 = v_ts(sv[:, 0, lo:hi], sv[:, 0, lo:hi], b[:, 8 + 2 * i:9 + 2 * i], None, ALU.mult, None, t)
                t3 = v_stt(sv[:, 0, lo:hi], sv[:, 1, lo:hi], b[:, 4 + i:5 + i], sv[:, 0, lo:hi],
                           ALU.mult, ALU.add, t1, t2)
            S2[h] = (k_, sv, t3)

        def d_tr(h):
            k_, sv, tok = S2[h]
            kp, ps, pf = trr.get()
            for j in range(3):
                t = tr(ps[:, j * 128:j * 128 + 128], sv[:, 0, j * 128:j * 128 + 128], tok, *pf, sig=j == 2)
            sb2.rel(k_, t)
            kt, pt, ptf = sb3.get()
            t = a_act(pt, ps[:, 0:384], ACT.Copy, t, *ptf)
            trr.rel(kp, t)
            S2[h] = (kt, pt, t)

        ssq2 = bank(7)[:, 64:72].rearrange("p (a n) -> p a n", a=2)
        to_ = []

        def d_pv(h):
            kt, pt, tok = S2.pop(h)
            kv, pv, pvf = pvr.get()
            mm(pv[:, 0:256], v2[:, 0, h * 128:h * 128 + 128], pt[:, 0:256], tok, t_v2, *pvf,
               start=True, stop=False, sig=False)
            t = mm(pv[:, 128:256], v2[:, 1, h * 128:h * 128 + 128], pt[:, 256:384], start=False, stop=True)
            sb3.rel(kt, t)
            t1 = v_cp(osb[:, h, :], pv[:, 0:256], t)
            t2 = a_act(osq, osb[:, h, :], ACT.Square, t1, pe.last() if h else None)
            pvr.rel(kv, t1)
            for tt in range(2):
                t = mm(ssq2[:, tt, h:h + 1], osq[:, tt * 128:tt * 128 + 128], con("o128"), t2, *stat_free,
                       sig=tt == 1)
            to_.append((t1, t))

        pvr.free = [[xt[-1]]] if pvr.free[0] is not None else pvr.free
        for h in range(6):
            if h < 4:
                d_scores(h)
            if 0 <= h - 1 < 4:
                d_tr(h - 1)
            if 0 <= h - 2:
                d_pv(h - 2)
        rs2 = ar.take(24).rearrange("p (b a n) -> p b a n", b=3, a=2)
        t = v_ts(rs2[:, 0], ssq2, RMS_EPS, None, ALU.add, None, to_[-1][1])
        stat_free = [t]
        t = a_act(rs2[:, 1], rs2[:, 0], ACT.Sqrt, t)
        t = v_rcp(rs2[:, 2], rs2[:, 1], t)
        t = v_ts(rs2[:, 2], rs2[:, 2], 1.0 - LAM0, None, ALU.mult, None, t)
        tm = []
        for h in range(4):
            k_, ps, free = lin.get()
            for tt in range(2):
                t1 = mm(ps[:, tt * 128:tt * 128 + 128], rs2[:, 2, tt, h:h + 1].to_broadcast([128, 128]), ident,
                        t, *free, sig=tt == 1)
            t1 = v_stt(mixT[:, 4 + h, :], osb[:, h, :], col("ang", h), ps[:, 0:256], ALU.mult, ALU.mult, t1)
            lin.rel(k_, t1)
            tm.append(t1)
        xt = []
        run(linear("wo2", 8, 8, lambda kk: mixT[:, kk, :], lambda kk: [t_v2] if kk < 4 else [tm[kk - 4]],
                   evac_x, lin))
        xt_ = xt if xt else [dve.last()]

        h_t = rmsnorm("nffn2", [dve.last()], [pe.last()])
        actT = ar.take(22 * 256).rearrange("p (c t) -> p c t", c=22)
        ub = Rot([ar.take(512) for _ in range(3)])
        fb = Rot([bank(0), bank(1), bank(2), bank(3)])
        fb.free = [list(f) for f in lin.free] + [list(f) for f in scr.free]
        ta_ = []

        def evac_up(n, ps, t):
            f = n // 2
            k_, u, uf = ub.get()
            uv = u.rearrange("p (j t) -> p j t", j=2)
            pv = ps.rearrange("p (j t) -> p j t", j=2)
            tt_ = []
            for j in range(2):
                c = f + 22 * j
                t1 = a_act(uv[:, j, :], pv[:, j, :], ACT.Identity, t, *uf, scale=col("cw2", c), bias=col("cb", c))
            for j in range(2):
                c = f + 22 * j
                t2 = v_stt(uv[:, j, 1:256], pv[:, j, 0:255], col("cw1", c), uv[:, j, 1:256], ALU.mult, ALU.add, t1)
                t3 = v_stt(uv[:, j, 2:256], pv[:, j, 0:254], col("cw0", c), uv[:, j, 2:256], ALU.mult, ALU.add, t2)
                tt_.append(t3)
            t4 = a_act(uv[:, 0, :], uv[:, 0, :], ACT.Silu, tt_[0])
            t5 = v_tt(actT[:, f, :], uv[:, 0, :], uv[:, 1, :], ALU.mult, t4, tt_[1])
            ub.rel(k_, t5)
            ta_.append(t5)
            return [tt_[1]]

        run(linear("wup", 44, 8, rhs_h, lambda kk: [h_t[kk]], evac_up, fb, half=True))
        xt.clear()
        run(linear("wdn", 8, 22, lambda kk: actT[:, kk, :], lambda kk: [ta_[kk]], evac_x, fb))
        lin.free = [[dve.last()], [dve.last()]]
        y_t = rmsnorm("nfin", [dve.last()], [pe.last()])
        s_out = sem("s_out")
        sp.dma(lambda e: e.dma_start(A["out"], HTt[:, :]), s_out, y_t[-1])
        assert ring["used"] == len(order)

        block = ctx.enter_context(nc.Block())

        @block.sync
        def _(eng):
            sp.emit(eng)
            eng.wait_ge(s_out, 16)

        @block.tensor
        def _(eng):
            pe.emit(eng)

        @block.scalar
        def _(eng):
            act.emit(eng)

        @block.vector
        def _(eng):
            dve.emit(eng)

        @block.gpsimd
        def _(eng):
            pool.emit(eng)


def _blocks(w, order=None):
    k, n = w.shape
    b = w.reshape(k // 128, 128, n // 128, 128).transpose(2, 0, 1, 3)
    if order is not None:
        b = b[np.asarray(order)]
    b = b.reshape(-1, 16, 128, 128).transpose(0, 2, 1, 3)
    return b.reshape(-1, 128, 2048)


def _cols(v):
    return np.asarray(v, np.float32).reshape(-1, 128).T


def _constants():
    c0 = np.zeros((128, NC0), np.float32)

    def put(c, at, name, v):
        a, w = at[name]
        c[:, a:a + w] = v

    p = np.arange(128)
    put(c0, C0, "ident", np.eye(128))
    put(c0, C0, "iota", np.arange(128)[None, :])
    put(c0, C0, "blk", (p[:, None] // 64 == np.arange(2)[None, :]) / 64.0)
    put(c0, C0, "o1024", 1.0 / 1024)
    put(c0, C0, "o128", 1.0 / 128)
    put(c0, C0, "one", 1.0)
    f = np.power(np.float32(10000.0), -(np.arange(0, 64, 2).astype(np.float32)) / np.float32(64))
    put(c0, C0, "invf", f.astype(np.float32)[p % 32][:, None])
    m = np.zeros((128, 128), np.float32)
    r = np.zeros((128, 128), np.float32)
    for b in (0, 64):
        for j in range(8):
            m[b + 8 + j, b + j] = -1.0
            m[b + j, b + 8 + j] = 1.0
        for j in range(32):
            r[b + 32 + j, b + j] = -1.0
            r[b + j, b + 32 + j] = 1.0
    put(c0, C0, "permd", m)
    put(c0, C0, "permr", r)

    c1 = np.zeros((128, NC1), np.float32)
    kcol = np.arange(256) % 64
    cs = np.clip(p % 64 - 8, 0, 48)[:, None]
    ok = (kcol[None, :] >= cs) & (kcol[None, :] < cs + 16)
    put(c1, C1, "mna", np.where(ok, 0.0, NEG))
    q = np.arange(256)
    k = np.arange(256)
    band = np.abs(q[:, None] - k[None, :]) <= 64
    mg0 = np.where(band, 0.0, NEG).reshape(2, 128, 256).transpose(1, 0, 2).reshape(128, 512)
    put(c1, C1, "mg0", mg0)
    put(c1, C1, "mg1", np.where((p[:, None] - k[None, :]) % 4 == 0, 0.0, NEG))
    put(c1, C1, "mg2", np.where((p[:, None] - k[None, :]) % 16 == 0, 0.0, NEG))
    inv = np.power(np.float32(500000.0), -np.arange(8, dtype=np.float32) * np.float32(2.0) / np.float32(16))
    ang = (np.arange(256, dtype=np.float32)[None, :] * inv.astype(np.float32)[:, None]).astype(np.float32)
    cosd = np.ones((128, 256), np.float32)
    sind = np.zeros((128, 256), np.float32)
    for b in (0, 64):
        for j in range(16):
            cosd[b + j] = np.cos(ang[j % 8])
            sind[b + j] = np.sin(ang[j % 8])
    put(c1, C1, "bsel", p[:, None] == np.arange(1536)[None, :] // 64)
    put(c1, C1, "cosd", cosd)
    put(c1, C1, "sind", sind)

    c2 = np.zeros((128, NC2), np.float32)
    md = np.zeros((128, 384), np.float32)
    md[0:64, 64:128] = NEG
    md[0:64, 128 + 192:384] = NEG
    put(c2, C2, "mdf", md)
    cnt = np.concatenate([1.0 / np.minimum(np.arange(256) + 1, w) for w in (2, 4, 8, 16)])
    put(c2, C2, "cnt", cnt[None, :])
    return c0, c1, c2


def _layout(i):
    f = lambda n: np.asarray(i[n])
    x = f("x")[0]
    out = {"xT": x.T.reshape(8, 128, 256).transpose(1, 0, 2).reshape(128, 2048)}
    up = f("w_up_2")[0]
    o = [j for k in range(22) for j in (k, k + 22)]
    out["dense"] = np.concatenate([
        _blocks(f("w_in")[0]), _blocks(f("w_branch_na")[0]), _blocks(f("w_branch_dil")[0]),
        _blocks(f("w_out")[0]), _blocks(f("peer_w_query")[0]), _blocks(f("w_ple_gate")[0]),
        _blocks(f("w_ple")[0]), _blocks(f("w_in_2")[0]), _blocks(f("w_o_2")[0]), _blocks(up, o),
        _blocks(f("w_down_2")[0])])
    out["eu"] = f("peer_expert_u")[0].reshape(128, 64, 2, 8, 128).transpose(1, 4, 2, 3, 0).reshape(64, 128, 2048)
    out["ev"] = f("peer_expert_v")[0].reshape(128, 64, 2048).transpose(1, 0, 2)
    out["keysT"] = f("peer_sub_keys")[0].transpose(2, 0, 1).reshape(128, 256)
    cols = np.zeros((128, NCOL), np.float32)

    def put(name, v):
        a, w = COLS[name]
        cols[0:v.shape[0], a:a + w] = v

    for name, key in (("nmix", "norm_mix"), ("nffn", "norm_ffn"), ("nple", "norm_ple"),
                      ("nmix2", "norm_mix_g_2"), ("nffn2", "norm_ffn_g_2"), ("nfin", "norm_final_g_2")):
        put(name, _cols(f(key)))
    for name, key, j in (("qna", "qk_norm_na", 0), ("kna", "qk_norm_na", 1), ("qdil", "qk_norm_dil", 0),
                         ("kdil", "qk_norm_dil", 1)):
        put(name, np.tile(f(key)[0, j], 2)[:, None])
    put("psc", _cols(f("pool_scale_2")))
    put("ang", f("attn_norm_g_2")[0].T)
    for j in range(3):
        put(f"cw{j}", _cols(f("conv_w_2")[0, j]))
    put("cb", _cols(f("conv_b_2")[0]))
    put("lam", np.stack([f("lambda_q1_2")[0], f("lambda_k1_2")[0], f("lambda_q2_2")[0], f("lambda_k2_2")[0]], 1))
    out["cols"] = cols
    c = np.arange(64)
    dc = np.clip(c[None, :] - c[:, None] + 15, 0, 30)
    r = np.arange(4)
    dr = r[None, :] - r[:, None] + 7
    b = f("na_rel_bias")[0][:, dr[:, None, :, None], dc[None, :, None, :]]
    b = b.reshape(8, 2, 128, 256).transpose(2, 0, 1, 3).reshape(128, 4096)
    out["nab"] = b
    out["pT"] = f("p")[0, 0].T.reshape(2, 128, 256).transpose(1, 0, 2).reshape(128, 512)
    out["poolw"] = f("pool_w_2")[0].transpose(1, 0, 2).reshape(128, 512)
    out["pos"] = f("positions_2").reshape(256)
    out["c0"], out["c1"], out["c2"] = _constants()
    return {k: np.ascontiguousarray(v) for k, v in out.items()}


def program(nc, arrays):
    A = {k: nc.dram_tensor(f"in_{k}", v.shape, mybir.dt.from_np(v.dtype), kind="ExternalInput").ap()
         for k, v in arrays.items()}
    A["out"] = nc.dram_tensor("out_y", (128, 2048), mybir.dt.float32, kind="ExternalOutput").ap()
    build(nc, A)


def kernel(**inputs):
    import concourse.bacc as _bacc
    from concourse.bass_utils import run_bass_kernel_spmd as _run

    arrays = _layout(inputs)
    nc = _bacc.Bacc("TRN2", target_bir_lowering=False, num_devices=1)
    program(nc, arrays)
    r = _run(nc, [{f"in_{k}": v for k, v in arrays.items()}], core_ids=[0])
    y = r.results[0]["out_y"].reshape(128, 8, 256)
    return np.ascontiguousarray(y.transpose(2, 1, 0).reshape(1, 256, 1024))
```

```python
import math
from contextlib import ExitStack

import numpy as np
import concourse.bass as bass
from concourse import mybir

T = 256
NEG = -1.0e30
ROT_D = 16
NE = 128
STASH = 32
LEAD = 3
NRAW = 5
NSPL = 4
RMS_EPS = 1e-6

COLS = {}
_at = 0
for _n, _w in (("nmix", 8), ("nffn", 8), ("nple", 8), ("nmix2", 8), ("nffn2", 8), ("nfin", 8),
               ("qna", 1), ("kna", 1), ("qdil", 1), ("kdil", 1), ("psc", 4), ("ang", 4),
               ("cw0", 44), ("cw1", 44), ("cw2", 44), ("cb", 44), ("lam", 4)):
    COLS[_n] = (_at, _w)
    _at += _w
NCOL = _at
C0 = {}
_at = 0
for _n, _w in (("ident", 128), ("iota", 128), ("blk", 2), ("o1024", 1), ("o128", 1), ("one", 1),
               ("invf", 1), ("permd", 128), ("permr", 128)):
    C0[_n] = (_at, _w)
    _at += _w
NC0 = _at
C1 = {}
_at = 0
for _n, _w in (("mna", 256), ("mg0", 512), ("mg1", 256), ("mg2", 256), ("cosd", 256), ("sind", 256),
               ("bsel", 1536)):
    C1[_n] = (_at, _w)
    _at += _w
NC1 = _at
C2 = {}
_at = 0
for _n, _w in (("mdf", 384), ("cnt", 1024)):
    C2[_n] = (_at, _w)
    _at += _w
NC2 = _at

DENSE = (("w_in", 8, 46), ("wbna", 4, 8), ("wbdil", 2, 8), ("wout", 8, 8), ("wq", 8, 16),
         ("wple", 2, 8), ("wpg", 8, 8), ("w_in2", 8, 16), ("wo2", 8, 8), ("wup", 8, 44), ("wdn", 22, 8))
SLOT0 = {}
_at = 0
for _n, _k, _m in DENSE:
    SLOT0[_n] = _at
    _at += _k * _m // 8
NDENSE = _at


def expert_order():
    order, u = [], 0
    for half in range(2):
        while u < min(half * 64 + STASH, NE):
            order.append(("U", u))
            u += 1
        order.append(("G", half))
        for v in range(half * 64, half * 64 + 64):
            while u < min(v + LEAD, NE):
                order.append(("U", u))
                u += 1
            order.append(("V", v))
    return order


def load_order():
    order = [("D", i) for i in range(SLOT0["wple"])]
    order += [x for x in expert_order() if x[0] != "G"]
    order += [("D", i) for i in range(SLOT0["wple"], NDENSE)]
    return order


class Queue:

    def __init__(self, sem):
        self.sem, self.n, self.items, self.seen = sem, 0, [], {}

    def op(self, fn, *waits, sig=True, chain=False):
        need = []
        waits = list(waits) + ([self.last()] if chain else [])
        for w in waits:
            if w is None or w[1] <= 0:
                continue
            if self.seen.get(id(w[0]), 0) >= w[1]:
                continue
            self.seen[id(w[0])] = w[1]
            need.append(w)
        self.items.append((need, fn, self.sem if sig else None, 1))
        if sig:
            self.n += 1
        return self.last()

    def dma(self, fn, sem, *waits):
        need = [w for w in waits if w is not None and w[1] > 0]
        self.items.append((need, fn, sem, 16))

    def last(self):
        return (self.sem, self.n)

    def emit(self, eng):
        for need, fn, sem, by in self.items:
            for s, v in need:
                eng.wait_ge(s, v)
            ins = fn(eng)
            if sem is not None:
                ins.then_inc(sem, by)


class Rot:

    def __init__(self, aps):
        self.aps, self.free, self.i = aps, [[] for _ in aps], 0

    def get(self):
        k = self.i % len(self.aps)
        self.i += 1
        w, self.free[k] = self.free[k], None
        assert w is not None
        return k, self.aps[k], w

    def rel(self, k, *toks):
        self.free[k] = list(toks)


class Later:

    def __init__(self, depth):
        self.depth, self.fns = depth, []

    def put(self, fn):
        self.fns.append(fn)
        while len(self.fns) > self.depth:
            self.fns.pop(0)()

    def flush(self):
        while self.fns:
            self.fns.pop(0)()


def build(nc, A):
    f32 = mybir.dt.float32
    u32 = mybir.dt.uint32
    i32 = mybir.dt.int32
    ALU = mybir.AluOpType
    ACT = mybir.ActivationFunctionType
    AX = mybir.AxisListType.X
    SC = 0.125

    ctx = ExitStack()
    with ctx:
        def sem(name):
            return ctx.enter_context(nc.semaphore(name))

        def sb(name, w, dt=f32):
            return ctx.enter_context(nc.sbuf_tensor(name, [128, w], dt))

        f32r = mybir.dt.float32r
        RAW = sb("RAW", NRAW * 1024)
        SPL = sb("SPL", NSPL * 2048, f32r)
        XTt = sb("XT", 2048)
        HFt = sb("HF", 2048)
        HSt = sb("HS", 4096, f32r)
        CC = sb("CC", NC0)
        CL = sb("CL", NCOL)
        SM = sb("SM", 64)
        PS = ctx.enter_context(nc.psum_tensor("PS", [128, 4096], f32))
        XT = XTt[:, :].rearrange("p (c t) -> p c t", c=8)
        HF = HFt[:, :].rearrange("p (c t) -> p c t", c=8)
        HS = HSt[:, :].rearrange("p (s c t) -> p s c t", s=2, c=8)

        def bank(i, w=512):
            return PS[:, 512 * i:512 * i + w]

        def col(name, i=0, w=1):
            return CL[:, COLS[name][0] + i:COLS[name][0] + i + w]

        def con(name):
            return CC[:, C0[name][0]:C0[name][0] + C0[name][1]]

        pe = Queue(sem("s_pe"))
        act = Queue(sem("s_act"))
        dve = Queue(sem("s_dve"))
        pool = Queue(sem("s_pool"))
        sp = Queue(sem("s_sp"))
        ident = con("ident")

        def mm(out, lhsT, rhs, *w, start=True, stop=True, sig=True, skip=False):
            return pe.op(lambda e: e.matmul(out, lhsT, rhs, start=start, stop=stop, skip_group_check=skip),
                         *w, sig=sig)

        def tr(out, in_, *w, sig=True):
            return pe.op(lambda e: e.transpose(out, in_, ident), *w, sig=sig)

        def a_act(out, in_, f, *w, chain=False, **kw):
            return act.op(lambda e: e.activation(out, in_, f, **kw), *w, chain=chain)

        def v_tt(out, a, b, op, *w, q=None, chain=False):
            return (q or dve).op(lambda e: e.tensor_tensor(out, a, b, op), *w, chain=chain)

        def v_ts(out, a, s1, s2, op0, op1, *w, q=None, chain=False):
            if op1 is None:
                return (q or dve).op(lambda e: e.tensor_scalar(out, a, s1, None, op0), *w, chain=chain)
            return (q or dve).op(lambda e: e.tensor_scalar(out, a, s1, s2, op0, op1), *w, chain=chain)

        def v_stt(out, a, s, b, op0, op1, *w, chain=False):
            return dve.op(lambda e: e.scalar_tensor_tensor(out, a, s, b, op0, op1), *w, chain=chain)

        def v_cp(out, a, *w, q=None, chain=False):
            return (q or dve).op(lambda e: e.tensor_copy(out, a), *w, chain=chain)

        def v_red(out, a, op, *w, chain=False, negate=None):
            return dve.op(lambda e: e.tensor_reduce(out, a, AX, op, negate=negate), *w, chain=chain)

        def v_rcp(out, a, *w, chain=False):
            return dve.op(lambda e: e.reciprocal(out, a), *w, chain=chain)

        def load(sname, dst, src, *waits, q=None):
            s = sem(sname)
            (q or sp).dma(lambda e: e.dma_start(dst, src), s, *waits)
            return (s, 16)

        sm_set = dve.op(lambda e: e.memset(SM[:, 62:63], 0.0))
        eps_set = dve.op(lambda e: e.memset(SM[:, 63:64], RMS_EPS))
        t_c0 = load("s_c0", CC[:, :], A["c0"])
        t_cl = load("s_cl", CL[:, :], A["cols"])
        t_x = [load(f"s_x{i}", XTt[:, 512 * i:512 * i + 512], A["xT"][:, 512 * i:512 * i + 512]) for i in range(4)]

        order = load_order()
        rsem = [sem(f"s_raw{i}") for i in range(NRAW)]
        src = {"D": A["dense"], "U": A["eu"], "V": A["ev"]}
        ring = {"used": 0, "blk": 0}
        split_t = {}
        rest_on = [pool]

        def raw(n):
            k = n % NRAW
            return RAW[:, k * 1024:(k + 1) * 1024]

        def issue(n, *waits):
            if n >= len(order):
                return
            kind, j = order[n]
            sp.dma(lambda e: e.dma_start(raw(n), src[kind][j]), rsem[n % NRAW], *waits)

        def spl(n):
            k = n % NSPL
            return SPL[:, k * 2048:k * 2048 + 1024], SPL[:, k * 2048 + 1024:k * 2048 + 2048]

        def split(n, *waits):
            if n >= len(order):
                return
            hi, lo = spl(n)
            t1 = act.op(lambda e: e.activation(hi, raw(n), ACT.Copy), (rsem[n % NRAW], 16 * (n // NRAW + 1)), *waits)
            t2 = rest_on[n % len(rest_on)].op(lambda e: e.tensor_tensor(lo, raw(n), hi.bitcast(f32), ALU.subtract), t1, *waits)
            split_t[n] = (t1, t2)
            issue(n + NRAW, t2)

        for n in range(NRAW):
            issue(n)
        for n in range(NSPL):
            split(n)

        def slot(kind):
            n = ring["used"]
            assert order[n][0] == kind
            hi, lo = spl(n)
            return (hi.rearrange("p (b m) -> p b m", b=8), lo.rearrange("p (b m) -> p b m", b=8)), split_t[n]

        def slot_done(tok):
            n = ring["used"]
            ring["used"] += 1
            split(n + NSPL, tok)

        def mm3(out, l, r, *w, start, stop, sig=False, skip=False):
            mm(out, l[0], r[0], *w, start=start, stop=False, sig=False, skip=skip)
            mm(out, l[0], r[1], start=False, stop=False, sig=False, skip=skip)
            return mm(out, l[1], r[0], start=False, stop=stop, sig=sig, skip=skip)

        def parts(hi, lo, x, *w, eng=None):
            if eng is act:
                t = a_act(hi, x, ACT.Copy, *w)
            else:
                t = v_cp(hi, x, *w)
            return v_tt(lo, x, hi.bitcast(f32), ALU.subtract, t, *w)

        def barrier():
            toks = [q.last() for q in (pe, act, dve, pool)]
            return toks

        def linear(name, nch, kch, rhs, rhs_w, evac, rot, half=False):
            for n in range(nch):
                if not half or n % 2 == 0:
                    k_, ps, free = rot.get()
                o = ps[:, (n % 2) * 256:(n % 2) * 256 + 256] if half else ps[:, 0:256]
                for kk in range(kch):
                    (hi, lo), ld = slot("D")
                    b = ring["blk"] % 8
                    end = b == 7
                    w = (list(free) if kk == 0 else []) + list(rhs_w(kk)) + (list(ld) if b == 0 else [])
                    t = mm3(o, (hi[:, b, :], lo[:, b, :]), rhs(kk), *w, start=kk == 0, stop=kk == kch - 1,
                            sig=end or kk == kch - 1)
                    ring["blk"] += 1
                    if end:
                        slot_done(t)
                free = []
                if half and n % 2 == 0:
                    continue
                rot.rel(k_, *evac(n, ps, t))
                yield

        def linear_nat(npairs, lhs, lhs_w, evac, rot):
            for n in range(npairs):
                bufs = [rot.get() for _ in range(2)]
                for half in range(2):
                    (hi, lo), ld = slot("D")
                    assert ring["blk"] % 8 == 0
                    ring["blk"] += 8
                    for b in range(4):
                        kk = 4 * half + b
                        wh = hi[:, 2 * b:2 * b + 2, :].rearrange("p n m -> p (n m)")
                        wl = lo[:, 2 * b:2 * b + 2, :].rearrange("p n m -> p (n m)")
                        for tt in range(2):
                            l = lhs(kk, tt)
                            t = mm3(bufs[tt][1][:, 0:256], l, (wh, wl), *ld, *bufs[tt][2], *lhs_w(kk),
                                    start=kk == 0, stop=kk == 7, sig=b == 3)
                    slot_done(t)
                for tt in range(2):
                    rot.rel(bufs[tt][0], *evac(n, tt, bufs[tt][1], t))
                yield

        lin = Rot([bank(0), bank(1)])
        scr = Rot([bank(2), bank(3)])
        pvr = Rot([bank(4)])
        trr = Rot([bank(5), bank(6)])
        stat_free = []
        sm_at = [0]

        def small(w):
            a = sm_at[0]
            sm_at[0] += w
            assert sm_at[0] <= 52
            return SM[:, a:a + w]

        later = Later(2)
        nsum = {"t": []}

        def square(c, *w, on_dve=False):
            if on_dve:
                tq = v_tt(HF[:, c, :], XT[:, c, :], XT[:, c, :], ALU.mult, *w)
            else:
                tq = a_act(HF[:, c, :], XT[:, c, :], ACT.Square, *w)
            nsum["t"].append(None)

            def sums():
                for tt in range(2):
                    t = mm(bank(7)[:, tt:tt + 1], HF[:, c, tt * 128:tt * 128 + 128], con("o1024"), tq, t_c0,
                           *stat_free, start=c == 0 and tt == 0, stop=c == 7 and tt == 1, sig=tt == 1, skip=True)
                nsum["t"][c] = t

            later.put(sums)

        warm_t = {}

        def warm(f):
            a_act(SM[0:1, 60:61], SM[0:1, 62:63], f, sm_set)

        def rmsnorm(gname, xw, hw, split_=True):
            nonlocal stat_free
            for c in range(len(nsum["t"]), 8):
                square(c, *xw, on_dve=c % 2 == 1)
            later.flush()
            t = nsum["t"][-1]
            nsum["t"] = []
            sd, rs = small(2), small(2)
            t1 = t2 = a_act(sd, bank(7)[:, 0:2], ACT.Sqrt, t, eps_set, bias=SM[:, 63:64])
            t3 = v_rcp(rs, sd, t2)
            k_, ps, free = lin.get()
            for tt in range(2):
                t = mm(ps[:, tt * 128:tt * 128 + 128], rs[:, tt:tt + 1].to_broadcast([128, 128]), ident,
                       t3, *free, sig=tt == 1)
            out_t = []
            for c in range(8):
                t1_ = v_stt(HF[:, c, :], XT[:, c, :], col(gname, c), ps[:, 0:256], ALU.mult, ALU.mult, t, t_cl)
                if split_:
                    out_t.append(parts(HS[:, 0, c, :], HS[:, 1, c, :], HF[:, c, :], t1_, *hw, eng=act))
                else:
                    out_t.append(t1_)
            lin.rel(k_, t1_)
            stat_free = [t1]
            return out_t

        names = [0]

        class Arena:

            def __init__(self):
                self.ctx = ExitStack()

            def take(self, w, dt=f32):
                names[0] += 1
                return self.ctx.enter_context(nc.sbuf_tensor(f"t{names[0]}", [128, w], dt))[:, :]

            def close(self):
                self.ctx.close()

        ao = Arena()
        gates = ao.take(4096).rearrange("p (c t) -> p c t", c=16)
        ona = ao.take(2048, f32r).rearrange("p (s c t) -> p s c t", s=2, c=4)
        odl = ao.take(1024, f32r).rearrange("p (s c t) -> p s c t", s=2, c=2)
        ar = Arena()
        c1 = ar.take(NC1)
        bias = ar.take(4096)
        t_c1 = load("s_c1", c1, A["c1"])
        t_bias = load("s_bias", bias, A["nab"])
        c1v = {n: c1[:, a:a + w] for n, (a, w) in C1.items()}
        bias4 = bias.rearrange("p (h a k) -> p h a k", h=8, a=2)
        qka = ar.take(8 * 256).rearrange("p (c t) -> p c t", c=8)
        qkd = ar.take(12 * 256).rearrange("p (c t) -> p c t", c=12)
        va = ar.take(1024).rearrange("p (a n) -> p a n", a=2)
        vd = ar.take(1536).rearrange("p (a n) -> p a n", a=2)
        sqr = Rot([ar.take(256) for _ in range(4)])
        sbuf_s = Rot([ar.take(1536) for _ in range(2)])
        sbuf_t = Rot([ar.take(1536) for _ in range(2)])
        qd_m = Rot([ar.take(256) for _ in range(3)])

        t_bm = None
        for h in range(8):
            for a in range(2):
                t_bm = v_tt(bias4[:, h, a, :], bias4[:, h, a, :], c1v["mna"], ALU.add, t_c1, t_bias, q=pool)

        lm = SM[:, 52:60]
        v_tt(lm[:, 0:1], col("lam", 0), col("lam", 1), ALU.mult, t_cl)
        t = v_tt(lm[:, 1:2], col("lam", 2), col("lam", 3), ALU.mult)
        st = bank(7)
        t = mm(st[:, 0:2], con("one").to_broadcast([128, 128]), lm[:, 0:2], t, *stat_free)
        t = a_act(lm[:, 2:4], st[:, 0:2], ACT.Exp, t)
        stat_free = [t]
        LAM0 = 0.8 - 0.6 * float(np.exp(-0.0))
        t = v_tt(lm[:, 4:5], lm[:, 2:3], lm[:, 3:4], ALU.subtract, t)
        t = v_ts(lm[:, 5:6], lm[:, 4:5], LAM0, -1.0, ALU.add, ALU.mult, t)

        warm(ACT.Sqrt)
        for c in range(8):
            square(c, t_x[c // 2], on_dve=c % 2 == 1)
        h_t = rmsnorm("nmix", [], [])

        def rhs_h(kk):
            return HS[:, 0, kk, :], HS[:, 1, kk, :]

        def w_h(kk):
            return [h_t[kk]]

        ssq = bank(7)[:, 64:64 + 80].rearrange("p (a n) -> p a n", a=2)
        sq_free = []

        def evac_qk(dst, base):
            def f(n, ps, t):
                k_, sq, free = sqr.get()
                t1 = v_cp(dst[:, n, :], ps[:, 0:256], t)
                t2 = a_act(sq, dst[:, n, :], ACT.Square, t1, *free)
                c = 2 * (base + n)

                def sums():
                    for tt in range(2):
                        t3 = mm(ssq[:, tt, c:c + 2], sq[:, tt * 128:tt * 128 + 128], con("blk"), t2, *stat_free,
                                sig=tt == 1)
                    sqr.rel(k_, t3)

                later.put(sums)
                return [t1]
            return f

        def qk_scale(dst, nq, n, base, gq, gk, rs, trs):
            out = []
            k_, ps, free = lin.get()
            for tt in range(2):
                t = mm(ps[0:2 * n, tt * 128:tt * 128 + 128], rs[:, tt, 2 * base:2 * base + 2 * n], ident,
                       trs, *free, sig=tt == 1)
            tT = v_cp(rsT[0:2 * n, :], ps[0:2 * n, 0:256], t)
            lin.rel(k_, tT)
            bsel = c1v["bsel"]
            for c in range(n):
                k_, ps, free = lin.get()
                t = mm(ps[:, 0:256], bsel[0:2 * n, c * 128:c * 128 + 128], rsT[0:2 * n, :], tT, t_c1, *free)
                g = col(gq) if c < nq else col(gk)
                t = v_stt(dst[:, c, :], dst[:, c, :], g, ps[:, 0:256], ALU.mult, ALU.mult, t)
                lin.rel(k_, t)
                out.append(t)
                yield out

        def run(gen):
            for _ in gen:
                pass

        def weave(main, fill, n=(1, 1)):
            for w in main:
                for _ in range(n[w or 0]):
                    next(fill, None)
            run(fill)

        run(linear("w_in", 8, 8, rhs_h, w_h, evac_qk(qka, 0), lin))
        later.flush()
        tq = pe.last()
        ms = ar.take(80).rearrange("p (a n) -> p a n", a=2)
        sd = ar.take(80).rearrange("p (a n) -> p a n", a=2)
        rsT = ar.take(256)
        rsq = ar.take(80).rearrange("p (a n) -> p a n", a=2)

        def stats(lo, hi, w):
            nonlocal stat_free
            t1 = v_ts(ms[:, :, lo:hi], ssq[:, :, lo:hi], RMS_EPS, None, ALU.add, None, w)
            stat_free = [t1]
            t2 = a_act(sd[:, :, lo:hi], ms[:, :, lo:hi], ACT.Sqrt, t1)
            return v_rcp(rsq[:, :, lo:hi], sd[:, :, lo:hi], t2)

        trs = stats(0, 16, tq)

        def evac_v(dst):
            def f(n, tt, ps, t):
                return [a_act(dst[:, tt, n * 256:n * 256 + 256], ps[:, 0:256], ACT.Copy, t)]
            return f

        def lhs_h(kk, tt):
            return HS[:, 0, kk, tt * 128:tt * 128 + 128], HS[:, 1, kk, tt * 128:tt * 128 + 128]

        run(linear_nat(2, lhs_h, w_h, evac_v(va), lin))
        run(qk_scale(qka, 4, 8, 0, "qna", "kna", rsq, trs))
        t_qk = dve.last()
        t_va = act.last()

        def softmax(S, W, w):
            nm, z, rz = S["nm"], S["z"], S["rz"]
            t = v_red(nm, S["s"], ALU.max, w, negate=True)
            te = []
            for a in range(2):
                te.append(a_act(S["s"][:, a, :], S["s"][:, a, :], ACT.Exp, t, bias=nm[:, a:a + 1],
                                accum_out=z[:, a:a + 1]))
            t = v_rcp(rz, z, te[1])
            for a in range(2):
                t = v_ts(S["s"][:, a, :], S["s"][:, a, :], rz[:, a:a + 1], None, ALU.mult, None, t)
            return t

        statb = ar.take(12 * 6).rearrange("p (n k) -> p n k", n=12)

        def attention(heads, scores, vlist, put, base):
            st = {}
            for i in range(len(heads) + 2):
                if i < len(heads):
                    h = heads[i]
                    k_, s, free = sbuf_s.get()
                    W, tok = scores(h, s, free)
                    sv = s[:, 0:2 * W].rearrange("p (a w) -> p a w", a=2)
                    b = statb[:, base + i, :]
                    S = {"s": sv, "nm": b[:, 0:2], "z": b[:, 2:4], "rz": b[:, 4:6], "k": k_, "W": W}
                    S["tok"] = softmax(S, W, tok)
                    st[i] = S
                if 0 <= i - 2:
                    S = st.pop(i - 2)
                    h = heads[i - 2]
                    if (i - 2) % 2 == 0:
                        k_pv, pv, pvfree = pvr.get()
                    r = 64 * (h % 2)
                    n = S["W"] // 128
                    for c in range(n):
                        t = mm(pv[r:r + 64, 0:256], vlist(h, c), S["pt"][:, c, :], S["te"][c // 2], *pvfree,
                               start=c == 0, stop=c == n - 1, sig=c == n - 1)
                    sbuf_t.rel(S["ptk"], t)
                    if (i - 2) % 2 == 1:
                        pvr.rel(k_pv, *put(h // 2, pv, t))
                yield 0
                if 0 <= i - 1 < len(heads):
                    S = st[i - 1]
                    kt, pt, ptfree = sbuf_t.get()
                    ptv = pt.rearrange("p (c t) -> p c t", t=256)
                    te = []
                    for c in range(S["W"] // 256):
                        k_, ps, free = trr.get()
                        psv = ps.rearrange("p (j t) -> p j t", j=2)
                        for j in range(2):
                            for a in range(2):
                                t = tr(psv[:, j, a * 128:a * 128 + 128],
                                       S["s"][:, a, c * 256 + j * 128:c * 256 + j * 128 + 128],
                                       S["tok"], *free, sig=j == 1 and a == 1)
                        w = list(ptfree) + [t]
                        t2 = a_act(ptv[:, 2 * c:2 * c + 2, :], psv, ACT.Copy, *w)
                        te.append(t2)
                        trr.rel(k_, t2)
                    sbuf_s.rel(S["k"], t)
                    S["pt"], S["ptk"], S["te"] = ptv, kt, te
                yield 1

        def na_scores(h, s, free):
            k_, ps, pf = scr.get()
            r = 64 * (h % 2)
            for a in range(2):
                t = mm(ps[:, a * 256:a * 256 + 256], qka[r:r + 64, h // 2, a * 128:a * 128 + 128],
                       qka[r:r + 64, 4 + h // 2, :], t_qk, *pf, sig=a == 1)
            t = v_stt(s[:, 0:512], ps, SC, bias4[:, h, :, :].rearrange("p a k -> p (a k)"), ALU.mult, ALU.add,
                      t, t_bm, *free)
            scr.rel(k_, t)
            return 256, t

        def put_na(c, pv, t):
            return [parts(ona[:, 0, c, :], ona[:, 1, c, :], pv[:, 0:256], t)]

        def fill1():
            yield from linear("w_in", 12, 8, rhs_h, w_h, evac_qk(qkd, 8), lin)
            later.flush()
            yield from linear_nat(3, lhs_h, w_h, evac_v(vd), lin)

        weave(attention(list(range(8)), na_scores, lambda h, c: va[:, c, h * 64:h * 64 + 64], put_na, 0),
              fill1(), (1, 1))
        t_vd = act.last()

        def evac_gate(n, ps, t):
            return [a_act(gates[:, n, :], ps[:, 0:256], ACT.Sigmoid, t)]

        fill = linear("w_in", 16, 8, rhs_h, w_h, evac_gate, lin)
        trs = stats(16, 40, pe.last())
        gen = qk_scale(qkd, 6, 12, 8, "qdil", "kdil", rsq, trs)
        prev = None
        rot_t = []
        rot_l = Later(1)
        for c, toks in enumerate(gen):
            def rotary(c=c, tok=toks[c]):
                k_, ps, free = scr.get()
                t = mm(ps[:, 0:256], con("permd"), qkd[:, c, :], tok, *free)
                k2, m, mf = qd_m.get()
                t1 = v_tt(m, qkd[:, c, :], c1v["cosd"], ALU.mult, tok, *mf, q=pool)
                t2 = v_tt(qkd[:, c, :], ps[:, 0:256], c1v["sind"], ALU.mult, t, t1)
                scr.rel(k_, t2)
                t3 = v_tt(qkd[:, c, :], qkd[:, c, :], m, ALU.add, t2)
                qd_m.rel(k2, t3)

            rot_l.put(rotary)
            if c % 2 == 1:
                next(fill)
        rot_l.flush()
        t_qd = dve.last()

        def dil_scores(hh, s, free):
            s4 = s.rearrange("p (a g k) -> p a g k", a=2, g=3)
            for g in range(3):
                k_, ps, pf = scr.get()
                head = 4 * g + hh
                r = 64 * (head % 2)
                for a in range(2):
                    t = mm(ps[:, a * 256:a * 256 + 256], qkd[r:r + 64, head // 2, a * 128:a * 128 + 128],
                           qkd[r:r + 64, 6 + head // 2, :], t_qd, *pf, sig=a == 1)
                if g == 0:
                    m = c1v["mg0"].rearrange("p (a k) -> p a k", a=2)
                else:
                    m = c1v[f"mg{g}"].unsqueeze(1).to_broadcast([128, 2, 256])
                t = v_stt(s4[:, :, g, :], ps.rearrange("p (a k) -> p a k", a=2), SC, m, ALU.mult, ALU.add,
                          t, t_c1, *free)
                scr.rel(k_, t)
            return 768, t

        def put_dil(c, pv, t):
            return [parts(odl[:, 0, c, :], odl[:, 1, c, :], pv[:, 0:256], t)]

        weave(attention(list(range(4)), dil_scores,
                        lambda h, c: vd[:, c % 2, (4 * (c // 2) + h) * 64:(4 * (c // 2) + h) * 64 + 64],
                        put_dil, 8), fill, (2, 1))
        t_att = dve.last()
        t_gate = act.last()

        ar.close()
        ar = Arena()
        mrf = ar.take(2048).rearrange("p (c t) -> p c t", c=8)
        mrg = ar.take(4096, f32r).rearrange("p (s c t) -> p s c t", s=2, c=8)
        qd_m = Rot([ar.take(256) for _ in range(3)])
        fence = barrier()
        mt = []

        def evac_na(n, ps, t):
            t1 = v_tt(mrf[:, n, :], ps[:, 0:256], gates[:, n, :], ALU.mult, t, t_gate, *fence)
            return [t1]

        run(linear("wbna", 8, 4, lambda kk: (ona[:, 0, kk, :], ona[:, 1, kk, :]), lambda kk: [t_att], evac_na, lin))

        def evac_dl(n, ps, t):
            k_, m, mf = qd_m.get()
            t1 = v_tt(m, ps[:, 0:256], gates[:, 8 + n, :], ALU.mult, t, *mf)
            t2 = v_tt(mrf[:, n, :], mrf[:, n, :], m, ALU.add, t1)
            qd_m.rel(k_, t2)
            mt.append(parts(mrg[:, 0, n, :], mrg[:, 1, n, :], mrf[:, n, :], t2))
            return [t1]

        run(linear("wbdil", 8, 2, lambda kk: (odl[:, 0, kk, :], odl[:, 1, kk, :]), lambda kk: [t_att], evac_dl, lin))
        xt = []

        def evac_x(n, ps, t):
            t1 = v_tt(XT[:, n, :], XT[:, n, :], ps[:, 0:256], ALU.add, t)
            xt.append(t1)
            if n == 0:
                warm(ACT.Sqrt)
            square(n, t1)
            return [t1]

        run(linear("wout", 8, 8, lambda kk: (mrg[:, 0, kk, :], mrg[:, 1, kk, :]), lambda kk: [mt[kk]], evac_x, lin))

        ar.close()
        ao.close()
        fence = barrier()
        ex = Arena()
        GS = ex.take(STASH * 256)
        T3 = ex.take(768)
        ar = Arena()
        h_t = rmsnorm("nffn", [xt[-1]], [pe.last()])
        keysT = ar.take(256).rearrange("p (a n) -> p a n", a=2)
        t_keys = load("s_keys", keysT.rearrange("p a n -> p (a n)"), A["keysT"], *fence)
        qpc = ar.take(4096)
        qp = qpc.rearrange("p (c t) -> p c t", c=16)
        Ssc = ar.take(4096).rearrange("p (a c n) -> p a c n", a=2, c=16)
        top = ar.take(2 * 16 * 16).rearrange("p (a c n) -> p a c n", a=2, c=16)
        ixu = ar.take(2 * 16 * 16).bitcast(u32).rearrange("p (a c n) -> p a c n", a=2, c=16)
        ixf = ar.take(2 * 16 * 16).rearrange("p (a c n) -> p a c n", a=2, c=16)
        cand = qpc.rearrange("p (a h n) -> p a h n", a=2, h=8)
        scv = ar.take(256).rearrange("p (a h n) -> p a h n", a=2, h=8)
        posu = ar.take(256).bitcast(u32).rearrange("p (a h n) -> p a h n", a=2, h=8)
        abu = ar.take(512).bitcast(u32).rearrange("p (b a h n) -> p b a h n", b=2, a=2, h=8)
        abf = ar.take(512).rearrange("p (b a h n) -> p b a h n", b=2, a=2, h=8)
        eq = ar.take(2048).rearrange("p (h k j) -> p h k j", h=8, k=16)
        sel = ar.take(768).rearrange("p (b a n) -> p b a n", b=3, a=2)
        ssum = ar.take(32).rearrange("p (b a h) -> p b a h", b=2, a=2)

        qt_ = []

        def evac_qp(n, ps, t):
            t1 = a_act(qp[:, n, :], ps[:, 0:256], ACT.Copy, t, *fence)
            qt_.append(t1)
            return [t1]

        gq = linear("wq", 16, 8, rhs_h, lambda kk: [h_t[kk]], evac_qp, lin)
        st_tok = {}

        def score_pair(c4):
            for a in range(2):
                k_, ps, free = scr.get()
                for j in range(4):
                    c = 4 * c4 + j
                    t = mm(ps[:, j * 128:j * 128 + 128], qp[:, c, a * 128:a * 128 + 128], keysT[:, c % 2, :],
                           qt_[c], t_keys, *free, sig=j == 3)
                t = a_act(Ssc[:, a, 4 * c4:4 * c4 + 4, :], ps.rearrange("p (c n) -> p c n", c=4), ACT.Copy, t)
                scr.rel(k_, t)
                st_tok[a, c4] = t

        for n in range(17):
            next(gq, None)
            if n % 4 == 0 and n:
                score_pair(n // 4 - 1)
        assert len(qt_) == 16

        upr = Rot([bank(5), bank(6)])
        stash = Rot([GS[:, i * 256:i * 256 + 256] for i in range(STASH)])
        upr.free = [list(f) for f in trr.free]
        ga = {}

        def u_slot(j):
            (hi, lo), ld = slot("U")
            k_, ps, free = upr.get()
            ks, g, gf = stash.get()
            for c in range(8):
                t = mm3(ps[:, 0:256], (hi[:, c, :], lo[:, c, :]), rhs_h(c), *ld, h_t[c], *free,
                        start=c == 0, stop=c == 7, sig=c == 7)
            slot_done(t)
            t2 = a_act(g, ps[:, 0:256], ACT.Gelu, t, *gf, *fence)
            upr.rel(k_, t2)
            ga[j] = (ks, g, t2)

        def top16(probs, w):
            st = [[dve.op(lambda e, v=v, vt=vt: e.max(vt[:, 0:8], v), *w)] for v, vt, it in probs]
            for i, (v, vt, it) in enumerate(probs):
                st[i].append(dve.op(lambda e, v=v, vt=vt, it=it: e.max_index(it[:, 0:8], vt[:, 0:8], v), st[i][0]))
            for i, (v, vt, it) in enumerate(probs):
                st[i].append(dve.op(lambda e, v=v, vt=vt: e.match_replace(v, vt[:, 0:8], v, -3.0e38), st[i][1]))
            for i, (v, vt, it) in enumerate(probs):
                st[i].append(dve.op(lambda e, v=v, vt=vt: e.max(vt[:, 8:16], v), st[i][2]))
            for i, (v, vt, it) in enumerate(probs):
                t = dve.op(lambda e, v=v, vt=vt, it=it: e.max_index(it[:, 8:16], vt[:, 8:16], v), st[i][3])
            return t

        def route():
            for a in range(2):
                for c in range(0, 16, 4):
                    top16([(Ssc[:, a, c + i, :], top[:, a, c + i, :], ixu[:, a, c + i, :]) for i in range(4)],
                          [st_tok[a, c // 4], *fence])
                    yield 4
                t = dve.last()
                v_cp(ixf[:, a], ixu[:, a], t)
                tv = top[:, a].rearrange("p (h b) n -> p h b n", b=2)
                cv = cand[:, a].rearrange("p h (i j) -> p h i j", i=16)
                t = v_tt(cv, tv[:, :, 0, :].unsqueeze(3).to_broadcast([128, 8, 16, 16]),
                         tv[:, :, 1, :].unsqueeze(2).to_broadcast([128, 8, 16, 16]), ALU.add, t, qp_done)
                yield 2
                for h in range(0, 8, 2):
                    top16([(cand[:, a, h + i, :], scv[:, a, h + i, :], posu[:, a, h + i, :]) for i in range(2)], [t])
                    yield 4
                t = dve.last()
                ta = dve.op(lambda e, a=a: e.tensor_scalar(abu[:, 0, a], posu[:, a], 4, None,
                                                           ALU.logical_shift_right), t)
                tb = dve.op(lambda e, a=a: e.tensor_scalar(abu[:, 1, a], posu[:, a], 15, None,
                                                           ALU.bitwise_and), t)
                g_ = sel[:, 2, a, :].rearrange("p (h k) -> p h k", h=8)
                t = v_tt(g_, scv[:, a], scv[:, a, :, 0:1].to_broadcast([128, 8, 16]), ALU.subtract, t)
                t = a_act(g_, g_, ACT.Exp, t)
                t = v_red(ssum[:, 0, a], g_, ALU.add, t)
                t = v_rcp(ssum[:, 1, a], ssum[:, 0, a], t)
                t = v_tt(g_, g_, ssum[:, 1, a].unsqueeze(2).to_broadcast([128, 8, 16]), ALU.mult, t)
                t = v_cp(abf[:, :, a], abu[:, :, a], ta, tb)
                yield 2
                for b in range(2):
                    ab = abf[:, b, a].unsqueeze(3).to_broadcast([128, 8, 16, 16])
                    io = con("iota")[:, 0:16].unsqueeze(1).unsqueeze(1).to_broadcast([128, 8, 16, 16])
                    t = v_tt(eq, ab, io, ALU.is_equal, t)
                    yield 2
                    iv = ixf[:, a].rearrange("p (h b) n -> p h b n", b=2)[:, :, b, :]
                    t = v_tt(eq, eq, iv.unsqueeze(2).to_broadcast([128, 8, 16, 16]), ALU.mult, t)
                    yield 2
                    t = v_red(sel[:, b, a, :].rearrange("p (h k) -> p h k", h=8), eq, ALU.add, t)
                    yield 2

        exo = expert_order()
        step = 0
        credit = 0.0
        qp_done = pe.last()
        for cost in route():
            credit += cost
            while credit >= 4 and exo[step][0] == "U" and step < STASH - 4:
                credit -= 4
                u_slot(exo[step][1])
                step += 1
        t_sel = dve.last()

        T3v = T3.rearrange("p (b t) -> p b t", b=3)
        for a in range(2):
            k_, ps, free = scr.get()
            for b in range(3):
                t = tr(ps[:, b * 128:b * 128 + 128], sel[:, b, a, :], t_sel, *free, sig=b == 2)
            t = v_cp(T3v[:, :, a * 128:a * 128 + 128], ps[:, 0:384].rearrange("p (b t) -> p b t", b=3), t)
            scr.rel(k_, t)
        t_T3 = t
        ar.close()
        ar = Arena()
        fence = barrier()
        G = ar.take(64 * 256).rearrange("p (i t) -> p i t", t=256)
        oh = Rot([ar.take(1536) for _ in range(2)])
        asp = Rot([ar.take(512, f32r) for _ in range(4)])
        iota = con("iota")
        gev = Rot([scr.aps[0], scr.aps[1]])
        gev.free = [list(f) for f in scr.free]
        gtok = {}
        acc = [bank(0), bank(1), bank(4), bank(7)]
        acc_free = lin.free[0] + lin.free[1] + pvr.free[0] + stat_free

        def gates_of(half):
            gw = list(fence) + ([dve.last(), pe.last()] if half else [])

            def marks(t8):
                k_, o, of = oh.get()
                i1 = T3v[:, 0, 8 * t8:8 * t8 + 8].unsqueeze(2).to_broadcast([128, 8, 128])
                i2 = T3v[:, 1, 8 * t8:8 * t8 + 8].unsqueeze(2).to_broadcast([128, 8, 64])
                gt = T3v[:, 2, 8 * t8:8 * t8 + 8].unsqueeze(2).to_broadcast([128, 8, 64])
                w1 = o[:, 0:1024].rearrange("p (j i) -> p j i", j=8)
                w2 = o[:, 1024:1536].rearrange("p (j i) -> p j i", j=8)
                it = iota[:, 64 * half:64 * half + 64].unsqueeze(1).to_broadcast([128, 8, 64])
                t2 = v_tt(w2, it, i2, ALU.is_equal, t_T3, *of, *gw)
                t2 = v_tt(w2, w2, gt, ALU.mult, t2, q=dve if half else pool)
                t1 = v_tt(w1, iota.unsqueeze(1).to_broadcast([128, 8, 128]), i1, ALU.is_equal, t_T3, *of, *gw)
                return k_, w1, w2, t1, t2

            ready = marks(0)
            for t8 in range(32):
                now = ready
                if t8 + 1 < 32:
                    ready = marks(t8 + 1)
                kb, ps, pf = gev.get()
                k_, w1, w2, tok1, tok2 = now
                for j in range(8):
                    t = mm(ps[:, j * 64:j * 64 + 64], w1[:, j, :], w2[:, j, :], tok1, tok2, *pf, sig=j == 7)
                oh.rel(k_, t)
                t = a_act(G[:, :, 8 * t8:8 * t8 + 8], ps.rearrange("p (j i) -> p i j", j=8), ACT.Copy, t, *gw)
                gev.rel(kb, t)
                yield
            gtok[half] = t

        def v_slot(i2):
            (hi, lo), ld = slot("V")
            g_ = G[:, i2 % 64, :]
            ap_ = a_parts.pop(i2)
            for c in range(8):
                t = mm3(acc[c // 2][:, (c % 2) * 256:(c % 2) * 256 + 256], (hi[:, c, :], lo[:, c, :]),
                        (ap_[1][:, 0:256], ap_[1][:, 256:512]), *ld, ap_[2], *acc_free,
                        start=i2 == 0 and c % 2 == 0, stop=i2 == NE - 1 and c % 2 == 1, sig=c == 7, skip=True)
            asp.rel(ap_[0], t)
            slot_done(t)

        a_parts = {}

        def a_of(i2):
            ks, g, tg = ga.pop(i2)
            t = v_tt(g, g, G[:, i2 % 64, :], ALU.mult, tg, gtok[i2 // 64])
            k_, sp_, free = asp.get()
            t = parts(sp_[:, 0:256], sp_[:, 256:512], g, t, *free, eng=act)
            stash.rel(ks, t)
            a_parts[i2] = (k_, sp_, t)

        ahead = 0
        while step < len(exo):
            kind, j = exo[step]
            rest_on[:] = [dve, pool] if kind == "V" else [pool]
            if kind == "G":
                nxt = step
                gg = gates_of(j)
                for n, _ in enumerate(gg):
                    pass
                step += 1
                continue
            if kind == "U":
                if exo[step][1] + 0 < NE and (j < STASH or (64 <= j + 0 and j < 64 + STASH)):
                    last = j
                    k2 = step
                    todo = []
                    while exo[k2][0] == "U":
                        todo.append(exo[k2][1])
                        k2 += 1
                    if exo[k2][0] == "G" and len(todo) > 0:
                        gg = gates_of(exo[k2][1])
                        per = 32 / len(todo)
                        at = 0.0
                        for u in todo:
                            at += per
                            u_slot(u)
                            while at >= 1 and next(gg, 1) is None:
                                at -= 1
                        for _ in gg:
                            pass
                        step = k2 + 1
                        continue
                u_slot(j)
                step += 1
                continue
            while ahead < min(j + 3, (j // 64 + 1) * 64) and ahead in ga:
                a_of(ahead)
                ahead += 1
            v_slot(j)
            step += 1
        xt = []
        for c in range(4):
            xt.append(v_tt(XT[:, 2 * c:2 * c + 2, :], XT[:, 2 * c:2 * c + 2, :],
                           acc[c].rearrange("p (j t) -> p j t", j=2), ALU.add, pe.last()))
        ar.close()
        ex.close()

        rest_on[:] = [pool, dve]
        fence = barrier()
        lin.free = [[xt[-1]], [xt[-1]]]
        scr.free = [list(f) for f in gev.free]
        pvr.free = [[xt[-1]]]
        stat_free = [xt[-1]]
        trr.free = [list(f) for f in upr.free]
        sm_at[0] = 16
        xt0, fence_pe = list(xt), pe.last()
        t_sin = None
        ar = Arena()
        c2 = ar.take(NC2)
        t_c2 = load("s_c2", c2, A["c2"], *fence)
        pF = ar.take(512)
        t_p = load("s_p", pF, A["pT"], *fence)
        pS = ar.take(1024, f32r)
        t_p = parts(pS[:, 0:512], pS[:, 512:1024], pF, t_p, *fence, eng=act)
        pS = pS.rearrange("p (s c t) -> p s c t", s=2, c=2)
        posi = ar.take(256).bitcast(i32)
        t_pos = load("s_pos", posi, A["pos"].partition_broadcast(128), *fence)
        pg = ar.take(2048).rearrange("p (c t) -> p c t", c=8)
        tg_ = []

        posf = ar.take(256)
        ang = ar.take(256)
        kq = ar.take(256)
        cosr = ar.take(256)
        sinr = ar.take(256)

        def rotary_tables():
            nonlocal t_sin
            TWO_PI = 2.0 * math.pi
            P1 = 6.28125
            P2 = math.floor((TWO_PI - P1) * 2.0 ** 18) / 2.0 ** 18
            P3 = TWO_PI - P1 - P2
            MAGIC = 12582912.0
            t = v_cp(posf, posi, t_pos, *fence)
            t_ang = v_ts(ang, posf, con("invf"), None, ALU.mult, None, t)
            PI_ = 3.1415925
            for dst, quarter in ((sinr, 0.0), (cosr, 0.25)):
                t = v_ts(kq, ang, 1.0 / TWO_PI, quarter, ALU.mult, ALU.add, t_ang, chain=True)
                t = v_ts(kq, kq, MAGIC, None, ALU.add, None, t)
                t = v_ts(kq, kq, MAGIC, None, ALU.subtract, None, t)
                t = v_stt(dst, kq, -P1, ang, ALU.mult, ALU.add, t)
                t = v_stt(dst, kq, -P2, dst, ALU.mult, ALU.add, t)
                t = v_stt(dst, kq, -P3, dst, ALU.mult, ALU.add, t)
                if quarter:
                    t = v_ts(dst, dst, math.pi / 2, None, ALU.add, None, t)
                t = v_ts(dst, dst, PI_, -PI_, ALU.min, ALU.max, t)
                t_sin = a_act(dst, dst, ACT.Sin, t)


        pw = ar.take(2048).rearrange("p (c t) -> p c t", c=8)

        def evac_ple(n, ps, t):
            t1 = v_cp(pw[:, n, :], ps[:, 0:256], t, *fence)
            tg_.append(t1)
            return [t1]

        run(linear("wple", 8, 2, lambda kk: (pS[:, 0, kk, :], pS[:, 1, kk, :]), lambda kk: [t_p], evac_ple, lin))
        h_t = rmsnorm("nple", xt0, [fence_pe])
        rotary_tables()
        xt = []

        def evac_pg(n, ps, t):
            t0 = a_act(pg[:, n, :], ps[:, 0:256], ACT.Sigmoid, t, *fence)
            t1 = v_tt(pg[:, n, :], pg[:, n, :], pw[:, n, :], ALU.mult, t0, tg_[n])
            xt.append(v_tt(XT[:, n, :], XT[:, n, :], pg[:, n, :], ALU.add, t1))
            if n == 7:
                warm(ACT.Sqrt)
            square(n, xt[-1])
            return [t0]

        run(linear("wpg", 8, 8, rhs_h, lambda kk: [h_t[kk]], evac_pg, lin))

        h_t = rmsnorm("nmix2", [xt[-1]], [pe.last()])
        pT_ = ar.take(1024).rearrange("p (c t) -> p c t", c=4)
        qk2 = ar.take(2048).rearrange("p (c t) -> p c t", c=8)
        v2 = ar.take(1024).rearrange("p (a n) -> p a n", a=2)
        mxf = Rot([ar.take(256) for _ in range(3)])
        mixT = ar.take(4096, f32r).rearrange("p (s c t) -> p s c t", s=2, c=8)
        poolw = ar.take(512).rearrange("p (g n) -> p g n", g=4)
        t_pw = load("s_pw", poolw.rearrange("p g n -> p (g n)"), A["poolw"], *fence)
        wa = ar.take(256)
        wb, wc, wd = ar.take(256), ar.take(256), ar.take(256)
        dT = ar.take(1024).rearrange("p (c t) -> p c t", c=4)
        qt2 = []

        def evac_q2(n, ps, t):
            t = a_act(qk2[:, n, :], ps[:, 0:256], ACT.Copy, t)
            qt2.append(t)
            return [t]

        run(linear("w_in2", 8, 8, rhs_h, lambda kk: [h_t[kk]], evac_q2, lin))
        fv = linear_nat(2, lhs_h, lambda kk: [h_t[kk]], evac_v(v2), lin)
        rm = Rot([ar.take(256) for _ in range(2)])
        for c in range(8):
            k_, ps, free = scr.get()
            t = mm(ps[:, 0:256], con("permr"), qk2[:, c, :], qt2[c], *free)
            k2, m, mf = rm.get()
            t1 = v_tt(m, qk2[:, c, :], cosr, ALU.mult, qt2[c], t_sin, *mf, q=pool)
            t2 = v_tt(qk2[:, c, :], ps[:, 0:256], sinr, ALU.mult, t, t1, t_sin)
            scr.rel(k_, t2)
            t3 = v_tt(qk2[:, c, :], qk2[:, c, :], m, ALU.add, t2)
            rm.rel(k2, t3)
            if c % 4 == 3:
                next(fv, None)
        run(fv)
        t_q2 = dve.last()
        t_v2 = act.last()

        sb2 = Rot([ar.take(768) for _ in range(4)])
        sb3 = Rot([ar.take(384) for _ in range(2)])
        osb = ar.take(1024).rearrange("p (c t) -> p c t", c=4)
        osqr = Rot([ar.take(256) for _ in range(4)])
        sst = ar.take(4 * 12).rearrange("p (h n) -> p h n", h=4)
        mdf = c2[:, 0:384]
        S2 = {}

        def d_scores(h):
            k_, s, free = sb2.get()
            sv = s.rearrange("p (n w) -> p n w", n=2)
            for n in range(2):
                kp, ps, pf = scr.get()
                r = 64 * n
                mm(ps[:, 0:128], qk2[r:r + 64, h, 0:128], qk2[r:r + 64, 4 + h, 0:128], t_q2, *pf, sig=False)
                t = mm(ps[:, 128:384], qk2[r:r + 64, h, 128:256], qk2[r:r + 64, 4 + h, :])
                t = v_stt(sv[:, n, :], ps[:, 0:384], SC, mdf, ALU.mult, ALU.add, t, t_c2, *free)
                scr.rel(kp, t)
            b = sst[:, h, :]
            segs = ((0, 128), (128, 384))
            v_red(b[:, 0:2], sv[:, :, 0:128], ALU.max, t, negate=True)
            t = v_red(b[:, 2:4], sv[:, :, 128:384], ALU.max, t, negate=True)
            for i, (lo, hi) in enumerate(segs):
                for n in range(2):
                    te = a_act(sv[:, n, lo:hi], sv[:, n, lo:hi], ACT.Exp, t,
                               bias=b[:, 2 * i + n:2 * i + n + 1], accum_out=b[:, 4 + 2 * i + n:5 + 2 * i + n])
            t = v_rcp(b[:, 8:12], b[:, 4:8], te)
            for i, (lo, hi) in enumerate(segs):
                t1 = v_ts(b[:, 4 + i:5 + i], b[:, 9 + 2 * i:10 + 2 * i], lm[:, 5:6], None, ALU.mult, None, t)
                t2 = v_ts(sv[:, 0, lo:hi], sv[:, 0, lo:hi], b[:, 8 + 2 * i:9 + 2 * i], None, ALU.mult, None, t)
                t3 = v_stt(sv[:, 0, lo:hi], sv[:, 1, lo:hi], b[:, 4 + i:5 + i], sv[:, 0, lo:hi],
                           ALU.mult, ALU.add, t1, t2)
            S2[h] = (k_, sv, t3)

        def d_tr(h):
            k_, sv, tok = S2[h]
            kp, ps, pf = trr.get()
            for j in range(3):
                t = tr(ps[:, j * 128:j * 128 + 128], sv[:, 0, j * 128:j * 128 + 128], tok, *pf, sig=j == 2)
            sb2.rel(k_, t)
            kt, pt, ptf = sb3.get()
            t = a_act(pt, ps[:, 0:384], ACT.Copy, t, *ptf)
            trr.rel(kp, t)
            S2[h] = (kt, pt, t)

        ssq2 = bank(7)[:, 64:72].rearrange("p (a n) -> p a n", a=2)
        to_ = []

        def d_pv(h):
            kt, pt, tok = S2.pop(h)
            kv, pv, pvf = pvr.get()
            mm(pv[:, 0:256], v2[:, 0, h * 128:h * 128 + 128], pt[:, 0:256], tok, t_v2, *pvf,
               start=True, stop=False, sig=False)
            t = mm(pv[:, 128:256], v2[:, 1, h * 128:h * 128 + 128], pt[:, 256:384], start=False, stop=True)
            sb3.rel(kt, t)
            t1 = v_cp(osb[:, h, :], pv[:, 0:256], t)
            ko, oq, of = osqr.get()
            t2 = a_act(oq, osb[:, h, :], ACT.Square, t1, *of)
            pvr.rel(kv, t1)

            def sums():
                for tt in range(2):
                    t = mm(ssq2[:, tt, h:h + 1], oq[:, tt * 128:tt * 128 + 128], con("o128"), t2, *stat_free,
                           sig=tt == 1)
                osqr.rel(ko, t)
                to_.append((t1, t))

            later.put(sums)

        t_pT = []
        def evac_p(n, ps, t):
            t = a_act(pT_[:, n, :], ps[:, 0:256], ACT.Copy, t, *fence)
            t_pT.append(t)
            return [t]

        tpool = []

        def gen_pool():
            for g in range(4):
                cur, tcur = pT_[:, g, :], t_pT[g]
                on = pool if g >= 2 else dve
                bufs = (wa, wb) if g >= 2 else (wc, wd)
                for lv in range(g + 1):
                    s = 1 << lv
                    nxt = bufs[lv % 2]
                    t1 = v_cp(nxt[:, 0:s], cur[:, 0:s], tcur, q=on, chain=True)
                    tcur = v_tt(nxt[:, s:256], cur[:, s:256], cur[:, 0:256 - s], ALU.add, t1, q=on)
                    cur = nxt
                cn = c2[:, C2["cnt"][0] + 256 * g:C2["cnt"][0] + 256 * g + 256]
                t1 = v_tt(dT[:, g, :], cur, cn, ALU.mult, tcur, t_c2, q=on)
                t1 = v_tt(dT[:, g, :], dT[:, g, :], pT_[:, g, :], ALU.subtract, t1, q=on)
                yield
                k_, ps, free = trr.get()
                t2 = mm(ps[:, 0:256], poolw[:, g, :], dT[:, g, :], t1, t_pw, *free)
                km, m, mf = mxf.get()
                t3 = a_act(m, ps[:, 0:256], ACT.Copy, t2, *mf, scale=col("psc", g))
                trr.rel(k_, t3)
                t3 = parts(mixT[:, 0, g, :], mixT[:, 1, g, :], m, t3)
                mxf.rel(km, t3)
                tpool.append(t3)
                yield

        def fill2():
            gl = linear("w_in2", 4, 8, rhs_h, lambda kk: [h_t[kk]], evac_p, lin)
            next(gl)
            yield
            gp = gen_pool()
            next(gp)
            for _ in range(3):
                next(gl)
                yield
                next(gp)
                next(gp)
                yield
            run(gl)
            run(gp)

        fl = fill2()
        for h in range(6):
            if h < 4:
                d_scores(h)
            if 0 <= h - 2:
                d_pv(h - 2)
            next(fl, None)
            if 0 <= h - 1 < 4:
                d_tr(h - 1)
            next(fl, None)
        run(fl)
        later.flush()
        rs2 = ar.take(24).rearrange("p (b a n) -> p b a n", b=3, a=2)
        t = v_ts(rs2[:, 0], ssq2, RMS_EPS, None, ALU.add, None, to_[-1][1])
        stat_free = [t]
        t = a_act(rs2[:, 1], rs2[:, 0], ACT.Sqrt, t)
        t = v_rcp(rs2[:, 2], rs2[:, 1], t)
        t = v_ts(rs2[:, 2], rs2[:, 2], 1.0 - LAM0, None, ALU.mult, None, t)
        tm = []
        for h in range(4):
            k_, ps, free = lin.get()
            for tt in range(2):
                t1 = mm(ps[:, tt * 128:tt * 128 + 128], rs2[:, 2, tt, h:h + 1].to_broadcast([128, 128]), ident,
                        t, *free, sig=tt == 1)
            t1 = v_stt(osb[:, h, :], osb[:, h, :], col("ang", h), ps[:, 0:256], ALU.mult, ALU.mult, t1)
            lin.rel(k_, t1)
            tm.append(parts(mixT[:, 0, 4 + h, :], mixT[:, 1, 4 + h, :], osb[:, h, :], t1, eng=act))
        xt = []
        run(linear("wo2", 8, 8, lambda kk: (mixT[:, 0, kk, :], mixT[:, 1, kk, :]),
                   lambda kk: [tpool[kk]] if kk < 4 else [tm[kk - 4]],
                   evac_x, lin))

        h_t = rmsnorm("nffn2", [dve.last()], [pe.last()])
        ar.close()
        ar = Arena()
        fence = barrier()
        actT = ar.take(44 * 256, f32r).rearrange("p (s c t) -> p s c t", s=2, c=22)
        ub = Rot([ar.take(512) for _ in range(3)])
        fb = Rot([bank(0), bank(1), bank(2), bank(3)])
        fb.free = [list(f) for f in lin.free] + [list(f) for f in scr.free]
        ta_ = []

        def evac_up(n, ps, t):
            f = n // 2
            k_, u, uf = ub.get()
            uv = u.rearrange("p (j t) -> p j t", j=2)
            pv = ps.rearrange("p (j t) -> p j t", j=2)
            tt_ = []
            for j in range(2):
                c = f + 22 * j
                t1 = a_act(uv[:, j, :], pv[:, j, :], ACT.Identity, t, *uf, *fence, scale=col("cw2", c), bias=col("cb", c))
            for j in range(2):
                c = f + 22 * j
                t2 = v_stt(uv[:, j, 1:256], pv[:, j, 0:255], col("cw1", c), uv[:, j, 1:256], ALU.mult, ALU.add, t1)
                t3 = v_stt(uv[:, j, 2:256], pv[:, j, 0:254], col("cw0", c), uv[:, j, 2:256], ALU.mult, ALU.add, t2)
                tt_.append(t3)
            t4 = a_act(uv[:, 0, :], uv[:, 0, :], ACT.Silu, tt_[0])
            t5 = v_tt(uv[:, 0, :], uv[:, 0, :], uv[:, 1, :], ALU.mult, t4, tt_[1])
            t5 = parts(actT[:, 0, f, :], actT[:, 1, f, :], uv[:, 0, :], t5, eng=act)
            ub.rel(k_, t5)
            ta_.append(t5)
            return [tt_[1]]

        run(linear("wup", 44, 8, rhs_h, lambda kk: [h_t[kk]], evac_up, fb, half=True))
        xt.clear()
        run(linear("wdn", 8, 22, lambda kk: (actT[:, 0, kk, :], actT[:, 1, kk, :]), lambda kk: [ta_[kk]], evac_x, fb))
        lin.free = [[dve.last()], [dve.last()]]
        y_t = rmsnorm("nfin", [dve.last()], [pe.last()], split_=False)
        s_out = sem("s_out")
        sp.dma(lambda e: e.dma_start(A["out"], HFt[:, :]), s_out, y_t[-1])
        assert ring["used"] == len(order)
        ar.close()

        block = ctx.enter_context(nc.Block())

        @block.sync
        def _(eng):
            sp.emit(eng)
            eng.wait_ge(s_out, 16)

        @block.tensor
        def _(eng):
            pe.emit(eng)

        @block.scalar
        def _(eng):
            act.emit(eng)

        @block.vector
        def _(eng):
            dve.emit(eng)

        @block.gpsimd
        def _(eng):
            pool.emit(eng)


def _blocks(w, order=None, wide=()):
    k, n = w.shape
    b = w.reshape(k // 128, 128, n // 128, 128).transpose(2, 0, 1, 3)
    if order is not None:
        b = b[np.asarray(order)]
    if wide:
        b = b.copy()
        for c in wide:
            pair = b[c:c + 2].transpose(1, 0, 2, 3).reshape(2, k // 128, 128, 128).copy()
            b[c:c + 2] = pair
    b = b.reshape(-1, 8, 128, 128).transpose(0, 2, 1, 3)
    return b.reshape(-1, 128, 1024)


def _cols(v):
    return np.asarray(v, np.float32).reshape(-1, 128).T


def _constants():
    c0 = np.zeros((128, NC0), np.float32)

    def put(c, at, name, v):
        a, w = at[name]
        c[:, a:a + w] = v

    p = np.arange(128)
    put(c0, C0, "ident", np.eye(128))
    put(c0, C0, "iota", np.arange(128)[None, :])
    put(c0, C0, "blk", (p[:, None] // 64 == np.arange(2)[None, :]) / 64.0)
    put(c0, C0, "o1024", 1.0 / 1024)
    put(c0, C0, "o128", 1.0 / 128)
    put(c0, C0, "one", 1.0)
    f = np.power(np.float32(10000.0), -(np.arange(0, 64, 2).astype(np.float32)) / np.float32(64))
    put(c0, C0, "invf", f.astype(np.float32)[p % 32][:, None])
    m = np.zeros((128, 128), np.float32)
    r = np.zeros((128, 128), np.float32)
    for b in (0, 64):
        for j in range(8):
            m[b + 8 + j, b + j] = -1.0
            m[b + j, b + 8 + j] = 1.0
        for j in range(32):
            r[b + 32 + j, b + j] = -1.0
            r[b + j, b + 32 + j] = 1.0
    put(c0, C0, "permd", m)
    put(c0, C0, "permr", r)

    c1 = np.zeros((128, NC1), np.float32)
    kcol = np.arange(256) % 64
    cs = np.clip(p % 64 - 8, 0, 48)[:, None]
    ok = (kcol[None, :] >= cs) & (kcol[None, :] < cs + 16)
    put(c1, C1, "mna", np.where(ok, 0.0, NEG))
    q = np.arange(256)
    k = np.arange(256)
    band = np.abs(q[:, None] - k[None, :]) <= 64
    mg0 = np.where(band, 0.0, NEG).reshape(2, 128, 256).transpose(1, 0, 2).reshape(128, 512)
    put(c1, C1, "mg0", mg0)
    put(c1, C1, "mg1", np.where((p[:, None] - k[None, :]) % 4 == 0, 0.0, NEG))
    put(c1, C1, "mg2", np.where((p[:, None] - k[None, :]) % 16 == 0, 0.0, NEG))
    inv = np.power(np.float32(500000.0), -np.arange(8, dtype=np.float32) * np.float32(2.0) / np.float32(16))
    ang = (np.arange(256, dtype=np.float32)[None, :] * inv.astype(np.float32)[:, None]).astype(np.float32)
    cosd = np.ones((128, 256), np.float32)
    sind = np.zeros((128, 256), np.float32)
    for b in (0, 64):
        for j in range(16):
            cosd[b + j] = np.cos(ang[j % 8])
            sind[b + j] = np.sin(ang[j % 8])
    put(c1, C1, "bsel", p[:, None] == np.arange(1536)[None, :] // 64)
    put(c1, C1, "cosd", cosd)
    put(c1, C1, "sind", sind)

    c2 = np.zeros((128, NC2), np.float32)
    md = np.zeros((128, 384), np.float32)
    md[0:64, 64:128] = NEG
    md[0:64, 128 + 192:384] = NEG
    put(c2, C2, "mdf", md)
    cnt = np.concatenate([1.0 / np.minimum(np.arange(256) + 1, w) for w in (2, 4, 8, 16)])
    put(c2, C2, "cnt", cnt[None, :])
    return c0, c1, c2


def _layout(i):
    f = lambda n: np.asarray(i[n])
    x = f("x")[0]
    out = {"xT": x.T.reshape(8, 128, 256).transpose(1, 0, 2).reshape(128, 2048)}
    up = f("w_up_2")[0]
    o = [j for k in range(22) for j in (k, k + 22)]
    out["dense"] = np.concatenate([
        _blocks(f("w_in")[0], None, (8, 10, 24, 26, 28)), _blocks(f("w_branch_na")[0]), _blocks(f("w_branch_dil")[0]),
        _blocks(f("w_out")[0]), _blocks(f("peer_w_query")[0]), _blocks(f("w_ple")[0]),
        _blocks(f("w_ple_gate")[0]), _blocks(f("w_in_2")[0], [*range(4, 16), *range(4)], (8, 10)), _blocks(f("w_o_2")[0]), _blocks(up, o),
        _blocks(f("w_down_2")[0])])
    out["eu"] = f("peer_expert_u")[0].reshape(128, 128, 8, 128).transpose(1, 3, 2, 0).reshape(128, 128, 1024)
    out["ev"] = f("peer_expert_v")[0].reshape(128, 128, 1024).transpose(1, 0, 2)
    out["keysT"] = f("peer_sub_keys")[0].transpose(2, 0, 1).reshape(128, 256)
    cols = np.zeros((128, NCOL), np.float32)

    def put(name, v):
        a, w = COLS[name]
        cols[0:v.shape[0], a:a + w] = v

    for name, key in (("nmix", "norm_mix"), ("nffn", "norm_ffn"), ("nple", "norm_ple"),
                      ("nmix2", "norm_mix_g_2"), ("nffn2", "norm_ffn_g_2"), ("nfin", "norm_final_g_2")):
        put(name, _cols(f(key)))
    for name, key, j in (("qna", "qk_norm_na", 0), ("kna", "qk_norm_na", 1), ("qdil", "qk_norm_dil", 0),
                         ("kdil", "qk_norm_dil", 1)):
        put(name, np.tile(f(key)[0, j], 2)[:, None])
    put("psc", _cols(f("pool_scale_2")))
    put("ang", f("attn_norm_g_2")[0].T)
    for j in range(3):
        put(f"cw{j}", _cols(f("conv_w_2")[0, j]))
    put("cb", _cols(f("conv_b_2")[0]))
    put("lam", np.stack([f("lambda_q1_2")[0], f("lambda_k1_2")[0], f("lambda_q2_2")[0], f("lambda_k2_2")[0]], 1))
    out["cols"] = cols
    c = np.arange(64)
    dc = np.clip(c[None, :] - c[:, None] + 15, 0, 30)
    r = np.arange(4)
    dr = r[None, :] - r[:, None] + 7
    b = f("na_rel_bias")[0][:, dr[:, None, :, None], dc[None, :, None, :]]
    b = b.reshape(8, 2, 128, 256).transpose(2, 0, 1, 3).reshape(128, 4096)
    out["nab"] = b
    out["pT"] = f("p")[0, 0].T.reshape(2, 128, 256).transpose(1, 0, 2).reshape(128, 512)
    out["poolw"] = f("pool_w_2")[0].transpose(1, 0, 2).reshape(128, 512)
    out["pos"] = f("positions_2").reshape(256)
    out["c0"], out["c1"], out["c2"] = _constants()
    return {k: np.ascontiguousarray(v) for k, v in out.items()}


def program(nc, arrays):
    A = {k: nc.dram_tensor(f"in_{k}", v.shape, mybir.dt.from_np(v.dtype), kind="ExternalInput").ap()
         for k, v in arrays.items()}
    A["out"] = nc.dram_tensor("out_y", (128, 2048), mybir.dt.float32, kind="ExternalOutput").ap()
    build(nc, A)


def kernel(**inputs):
    import concourse.bacc as _bacc
    from concourse.bass_utils import run_bass_kernel_spmd as _run

    arrays = _layout(inputs)
    nc = _bacc.Bacc("TRN2", target_bir_lowering=False, num_devices=1)
    program(nc, arrays)
    r = _run(nc, [{f"in_{k}": v for k, v in arrays.items()}], core_ids=[0])
    y = r.results[0]["out_y"].reshape(128, 8, 256)
    return np.ascontiguousarray(y.transpose(2, 1, 0).reshape(1, 256, 1024))
```

```python
import math
from contextlib import ExitStack

import numpy as np
import concourse.bass as bass
from concourse import mybir

T = 256
NEG = -1.0e30
ROT_D = 16
NE = 128
STASH = 28
QUART = 32
NRAW = 5
NSPL = 4
RMS_EPS = 1e-6

COLS = {}
_at = 0
for _n, _w in (("nmix", 8), ("nffn", 8), ("nple", 8), ("nmix2", 8), ("nffn2", 8), ("nfin", 8),
               ("qna", 1), ("kna", 1), ("qdil", 1), ("kdil", 1), ("psc", 4), ("ang", 4),
               ("cw0", 44), ("cw1", 44), ("cw2", 44), ("cb", 44), ("lam", 4)):
    COLS[_n] = (_at, _w)
    _at += _w
NCOL = _at
C0 = {}
_at = 0
for _n, _w in (("ident", 128), ("iota", 128), ("blk", 2), ("o1024", 1), ("o128", 1), ("one", 1),
               ("invf", 1), ("permd", 128), ("permr", 128)):
    C0[_n] = (_at, _w)
    _at += _w
NC0 = _at
C1 = {}
_at = 0
for _n, _w in (("mna", 256), ("mg0", 512), ("mg1", 256), ("mg2", 256), ("cosd", 256), ("sind", 256),
               ("bsel", 1536)):
    C1[_n] = (_at, _w)
    _at += _w
NC1 = _at
C2 = {}
_at = 0
for _n, _w in (("mdf", 384), ("cnt", 1024)):
    C2[_n] = (_at, _w)
    _at += _w
NC2 = _at

DENSE = (("w_in", 8, 46), ("wbna", 4, 8), ("wbdil", 2, 8), ("wout", 8, 8), ("wq", 8, 16),
         ("wple", 2, 8), ("wpg", 8, 8), ("w_in2", 8, 16), ("wo2", 8, 8), ("wup", 8, 44), ("wdn", 22, 8))
SLOT0 = {}
_at = 0
for _n, _k, _m in DENSE:
    SLOT0[_n] = _at
    _at += _k * _m // 8
NDENSE = _at


def expert_order():
    order = [("U", u) for u in range(STASH)]
    for v in range(NE):
        order.append(("V", v))
        if v + STASH < NE:
            order.append(("U", v + STASH))
    return order


def load_order():
    order = [("D", i) for i in range(SLOT0["wple"])]
    order += expert_order()
    order += [("D", i) for i in range(SLOT0["wple"], NDENSE)]
    return order


class Queue:

    def __init__(self, sem):
        self.sem, self.n, self.items, self.seen = sem, 0, [], {}

    def op(self, fn, *waits, sig=True, chain=False):
        need = []
        waits = list(waits) + ([self.last()] if chain else [])
        for w in waits:
            if w is None or w[1] <= 0:
                continue
            if self.seen.get(id(w[0]), 0) >= w[1]:
                continue
            self.seen[id(w[0])] = w[1]
            need.append(w)
        self.items.append((need, fn, self.sem if sig else None, 1))
        if sig:
            self.n += 1
        return self.last()

    def dma(self, fn, sem, *waits):
        need = [w for w in waits if w is not None and w[1] > 0]
        self.items.append((need, fn, sem, 16))

    def last(self):
        return (self.sem, self.n)

    def emit(self, eng):
        for need, fn, sem, by in self.items:
            for s, v in need:
                eng.wait_ge(s, v)
            ins = fn(eng)
            if sem is not None:
                ins.then_inc(sem, by)


class Rot:

    def __init__(self, aps):
        self.aps, self.free, self.i = aps, [[] for _ in aps], 0

    def get(self):
        k = self.i % len(self.aps)
        self.i += 1
        w, self.free[k] = self.free[k], None
        assert w is not None
        return k, self.aps[k], w

    def rel(self, k, *toks):
        self.free[k] = list(toks)


class Later:

    def __init__(self, depth):
        self.depth, self.fns = depth, []

    def put(self, fn):
        self.fns.append(fn)
        while len(self.fns) > self.depth:
            self.fns.pop(0)()

    def flush(self):
        while self.fns:
            self.fns.pop(0)()


def build(nc, A):
    f32 = mybir.dt.float32
    u32 = mybir.dt.uint32
    bf16 = mybir.dt.bfloat16
    i32 = mybir.dt.int32
    ALU = mybir.AluOpType
    ACT = mybir.ActivationFunctionType
    AX = mybir.AxisListType.X
    SC = 0.125

    ctx = ExitStack()
    with ctx:
        def sem(name):
            return ctx.enter_context(nc.semaphore(name))

        def sb(name, w, dt=f32):
            return ctx.enter_context(nc.sbuf_tensor(name, [128, w], dt))

        f32r = mybir.dt.float32r
        RAW = sb("RAW", NRAW * 1024)
        SPL = sb("SPL", NSPL * 2048, f32r)
        XTt = sb("XT", 2048)
        HFt = sb("HF", 2048)
        HSt = sb("HS", 4096, f32r)
        CC = sb("CC", NC0)
        CL = sb("CL", NCOL)
        SM = sb("SM", 64)
        RS = sb("RS", 256)
        PS = ctx.enter_context(nc.psum_tensor("PS", [128, 4096], f32))
        XT = XTt[:, :].rearrange("p (c t) -> p c t", c=8)
        HF = HFt[:, :].rearrange("p (c t) -> p c t", c=8)
        HS = HSt[:, :].rearrange("p (s c t) -> p s c t", s=2, c=8)

        def bank(i, w=512):
            return PS[:, 512 * i:512 * i + w]

        def col(name, i=0, w=1):
            return CL[:, COLS[name][0] + i:COLS[name][0] + i + w]

        def con(name):
            return CC[:, C0[name][0]:C0[name][0] + C0[name][1]]

        pe = Queue(sem("s_pe"))
        act = Queue(sem("s_act"))
        dve = Queue(sem("s_dve"))
        pool = Queue(sem("s_pool"))
        sp = Queue(sem("s_sp"))
        ident = con("ident")

        def mm(out, lhsT, rhs, *w, start=True, stop=True, sig=True, skip=False):
            return pe.op(lambda e: e.matmul(out, lhsT, rhs, start=start, stop=stop, skip_group_check=skip),
                         *w, sig=sig)

        def tr(out, in_, *w, sig=True):
            return pe.op(lambda e: e.transpose(out, in_, ident), *w, sig=sig)

        def a_act(out, in_, f, *w, chain=False, **kw):
            return act.op(lambda e: e.activation(out, in_, f, **kw), *w, chain=chain)

        def v_tt(out, a, b, op, *w, q=None, chain=False):
            return (q or dve).op(lambda e: e.tensor_tensor(out, a, b, op), *w, chain=chain)

        def v_ts(out, a, s1, s2, op0, op1, *w, q=None, chain=False):
            if op1 is None:
                return (q or dve).op(lambda e: e.tensor_scalar(out, a, s1, None, op0), *w, chain=chain)
            return (q or dve).op(lambda e: e.tensor_scalar(out, a, s1, s2, op0, op1), *w, chain=chain)

        def v_stt(out, a, s, b, op0, op1, *w, chain=False):
            return dve.op(lambda e: e.scalar_tensor_tensor(out, a, s, b, op0, op1), *w, chain=chain)

        def v_cp(out, a, *w, q=None, chain=False):
            return (q or dve).op(lambda e: e.tensor_copy(out, a), *w, chain=chain)

        def v_red(out, a, op, *w, chain=False, negate=None):
            return dve.op(lambda e: e.tensor_reduce(out, a, AX, op, negate=negate), *w, chain=chain)

        def v_rcp(out, a, *w, chain=False):
            return dve.op(lambda e: e.reciprocal(out, a), *w, chain=chain)

        def load(sname, dst, src, *waits, q=None):
            s = sem(sname)
            (q or sp).dma(lambda e: e.dma_start(dst, src), s, *waits)
            return (s, 16)

        sm_set = dve.op(lambda e: e.memset(SM[:, 62:63], 0.0))
        eps_set = dve.op(lambda e: e.memset(SM[:, 63:64], RMS_EPS))
        t_c0 = load("s_c0", CC[:, :], A["c0"])
        t_cl = load("s_cl", CL[:, :], A["cols"])
        t_x = [load(f"s_x{i}", XTt[:, 512 * i:512 * i + 512], A["xT"][:, 512 * i:512 * i + 512]) for i in range(4)]

        order = load_order()
        rsem = [sem(f"s_raw{i}") for i in range(NRAW)]
        src = {"D": A["dense"], "U": A["eu"], "V": A["ev"]}
        ring = {"used": 0, "blk": 0}
        split_t = {}
        rest_on = [pool]

        def raw(n):
            k = n % NRAW
            return RAW[:, k * 1024:(k + 1) * 1024]

        def issue(n, *waits):
            if n >= len(order):
                return
            kind, j = order[n]
            sp.dma(lambda e: e.dma_start(raw(n), src[kind][j]), rsem[n % NRAW], *waits)

        def spl(n):
            k = n % NSPL
            return SPL[:, k * 2048:k * 2048 + 1024], SPL[:, k * 2048 + 1024:k * 2048 + 2048]

        def split(n, *waits):
            if n >= len(order):
                return
            hi, lo = spl(n)
            t1 = act.op(lambda e: e.activation(hi, raw(n), ACT.Copy), (rsem[n % NRAW], 16 * (n // NRAW + 1)), *waits)
            t2 = rest_on[n % len(rest_on)].op(lambda e: e.tensor_tensor(lo, raw(n), hi.bitcast(f32), ALU.subtract), t1, *waits)
            split_t[n] = (t1, t2)
            issue(n + NRAW, t2)

        for n in range(NRAW):
            issue(n)

        def slot(kind):
            n = ring["used"]
            assert order[n][0] == kind
            hi, lo = spl(n)
            return (hi.rearrange("p (b m) -> p b m", b=8), lo.rearrange("p (b m) -> p b m", b=8)), split_t[n]

        def slot_done(tok):
            n = ring["used"]
            ring["used"] += 1
            split(n + NSPL, tok)

        def mm3(out, l, r, *w, start, stop, sig=False, skip=False):
            mm(out, l[0], r[0], *w, start=start, stop=False, sig=False, skip=skip)
            mm(out, l[0], r[1], start=False, stop=False, sig=False, skip=skip)
            return mm(out, l[1], r[0], start=False, stop=stop, sig=sig, skip=skip)

        def parts(hi, lo, x, *w, eng=None):
            if eng is act:
                t = a_act(hi, x, ACT.Copy, *w)
            else:
                t = v_cp(hi, x, *w)
            return v_tt(lo, x, hi.bitcast(f32), ALU.subtract, t, *w)

        def barrier():
            toks = [q.last() for q in (pe, act, dve, pool)]
            return toks

        def linear(name, nch, kch, rhs, rhs_w, evac, rot, half=False):
            for n in range(nch):
                if not half or n % 2 == 0:
                    k_, ps, free = rot.get()
                o = ps[:, (n % 2) * 256:(n % 2) * 256 + 256] if half else ps[:, 0:256]
                for kk in range(kch):
                    (hi, lo), ld = slot("D")
                    b = ring["blk"] % 8
                    end = b == 7
                    w = (list(free) if kk == 0 else []) + list(rhs_w(kk)) + (list(ld) if b == 0 else [])
                    t = mm3(o, (hi[:, b, :], lo[:, b, :]), rhs(kk), *w, start=kk == 0, stop=kk == kch - 1,
                            sig=end or kk == kch - 1)
                    ring["blk"] += 1
                    if end:
                        slot_done(t)
                free = []
                if half and n % 2 == 0:
                    continue
                rot.rel(k_, *evac(n, ps, t))
                yield

        def linear_nat(npairs, lhs, lhs_w, evac, rot):
            for n in range(npairs):
                bufs = [rot.get() for _ in range(2)]
                for half in range(2):
                    (hi, lo), ld = slot("D")
                    assert ring["blk"] % 8 == 0
                    ring["blk"] += 8
                    for b in range(4):
                        kk = 4 * half + b
                        wh = hi[:, 2 * b:2 * b + 2, :].rearrange("p n m -> p (n m)")
                        wl = lo[:, 2 * b:2 * b + 2, :].rearrange("p n m -> p (n m)")
                        for tt in range(2):
                            l = lhs(kk, tt)
                            t = mm3(bufs[tt][1][:, 0:256], l, (wh, wl), *ld, *bufs[tt][2], *lhs_w(kk),
                                    start=kk == 0, stop=kk == 7, sig=b == 3)
                    slot_done(t)
                for tt in range(2):
                    rot.rel(bufs[tt][0], *evac(n, tt, bufs[tt][1], t))
                yield

        lin = Rot([bank(0), bank(1)])
        scr = Rot([bank(2), bank(3)])
        pvr = Rot([bank(4)])
        trr = Rot([bank(5), bank(6)])
        stat_free = []
        later = Later(2)
        nsum = {"t": []}

        def square(c, *w, on_dve=False):
            if on_dve:
                tq = v_tt(HF[:, c, :], XT[:, c, :], XT[:, c, :], ALU.mult, *w)
            else:
                tq = a_act(HF[:, c, :], XT[:, c, :], ACT.Square, *w)
            nsum["t"].append(None)

            def sums():
                t = mm(bank(7)[:, 0:256], con("o1024").to_broadcast([128, 128]), HF[:, c, :], tq, t_c0, *stat_free,
                       start=c == 0, stop=c == 7)
                nsum["t"][c] = t

            later.put(sums)

        def warm(f):
            a_act(SM[0:1, 60:61], SM[0:1, 62:63], f, sm_set)

        out_h = {}

        def rest_of(c, *w):
            return v_tt(HS[:, 1, c, :], HF[:, c, :], HS[:, 0, c, :].bitcast(f32), ALU.subtract, out_h[c], *w,
                        q=pool if c % 2 and norms else dve)

        norms = 0
        rs_free = []

        def rmsnorm(gname, xw, hw, split_=True):
            nonlocal stat_free, norms
            for c in range(len(nsum["t"]), 8):
                square(c, *xw, on_dve=c % 2 == 1)
            later.flush()
            t = nsum["t"][-1]
            nsum["t"] = []
            t1 = a_act(RS[:, :], bank(7)[:, 0:256], ACT.Sqrt, t, eps_set, *rs_free, bias=SM[:, 63:64])
            t = v_rcp(RS[:, :], RS[:, :], t1)
            out_t = []
            for c in range(8):
                t1_ = v_stt(HF[:, c, :], XT[:, c, :], col(gname, c), RS[:, :], ALU.mult, ALU.mult, t, t_cl)
                out_t.append(t1_)
                if split_:
                    th = a_act(HS[:, 0, c, :], HF[:, c, :], ACT.Copy, t1_, *hw)
                    if c:
                        out_t[c - 1] = rest_of(c - 1, *hw)
                    out_h[c] = th
            if split_:
                out_t[7] = rest_of(7, *hw)
            norms += 1
            rs_free[:] = [t1_]
            stat_free = [t1]
            return out_t

        names = [0]

        class Arena:

            def __init__(self):
                self.ctx = ExitStack()

            def take(self, w, dt=f32):
                names[0] += 1
                return self.ctx.enter_context(nc.sbuf_tensor(f"t{names[0]}", [128, w], dt))[:, :]

            def close(self):
                self.ctx.close()

        ao = Arena()
        gates = ao.take(4096).rearrange("p (c t) -> p c t", c=16)
        ona = ao.take(2048, f32r).rearrange("p (s c t) -> p s c t", s=2, c=4)
        odl = ao.take(1024, f32r).rearrange("p (s c t) -> p s c t", s=2, c=2)
        ar = Arena()
        c1 = ar.take(NC1)
        bias = ar.take(4096)
        t_c1 = load("s_c1", c1, A["c1"])
        t_bias = load("s_bias", bias, A["nab"])
        c1v = {n: c1[:, a:a + w] for n, (a, w) in C1.items()}
        bias4 = bias.rearrange("p (h a k) -> p h a k", h=8, a=2)
        qka = ar.take(8 * 256).rearrange("p (c t) -> p c t", c=8)
        qkd = ar.take(12 * 256).rearrange("p (c t) -> p c t", c=12)
        va = ar.take(1024).rearrange("p (a n) -> p a n", a=2)
        vd = ar.take(1536).rearrange("p (a n) -> p a n", a=2)
        sqr = Rot([ar.take(256) for _ in range(3)])
        sbuf_s = Rot([ar.take(1536) for _ in range(2)])
        sbuf_t = Rot([ar.take(1536) for _ in range(2)])
        qd_m = Rot([ar.take(256) for _ in range(3)])

        warm(ACT.Sqrt)
        for c in range(8):
            square(c, t_x[c // 2], on_dve=c % 2 == 1)
        rest_on[:] = [pool, dve]
        split(0)
        split(1)
        h_t = rmsnorm("nmix", [], [])
        split(2)
        split(3)
        rest_on[:] = [pool]


        def rhs_h(kk):
            return HS[:, 0, kk, :], HS[:, 1, kk, :]

        def w_h(kk):
            return [h_t[kk]]

        ssq = bank(7)[:, 64:64 + 80].rearrange("p (a n) -> p a n", a=2)
        sq_free = []

        def evac_qk(dst, base):
            def f(n, ps, t):
                k_, sq, free = sqr.get()
                t1 = v_cp(dst[:, n, :], ps[:, 0:256], t)
                t2 = a_act(sq, dst[:, n, :], ACT.Square, t1, *free)
                c = 2 * (base + n)

                def sums():
                    for tt in range(2):
                        t3 = mm(ssq[:, tt, c:c + 2], sq[:, tt * 128:tt * 128 + 128], con("blk"), t2, *stat_free,
                                sig=tt == 1)
                    sqr.rel(k_, t3)

                later.put(sums)
                return [t1]
            return f

        def qk_scale(dst, nq, n, base, gq, gk, rs, trs):
            out = []
            k_, ps, free = lin.get()
            for tt in range(2):
                t = mm(ps[0:2 * n, tt * 128:tt * 128 + 128], rs[:, tt, 2 * base:2 * base + 2 * n], ident,
                       trs, *free, sig=tt == 1)
            tT = v_cp(rsT[0:2 * n, :], ps[0:2 * n, 0:256], t)
            lin.rel(k_, tT)
            bsel = c1v["bsel"]
            for c in range(n):
                k_, ps, free = lin.get()
                t = mm(ps[:, 0:256], bsel[0:2 * n, c * 128:c * 128 + 128], rsT[0:2 * n, :], tT, t_c1, *free)
                g = col(gq) if c < nq else col(gk)
                t = v_stt(dst[:, c, :], dst[:, c, :], g, ps[:, 0:256], ALU.mult, ALU.mult, t)
                lin.rel(k_, t)
                out.append(t)
                yield out

        def run(gen):
            for _ in gen:
                pass

        def weave(main, fill, n=(1, 1)):
            for w in main:
                for _ in range(n[w or 0]):
                    next(fill, None)
            run(fill)

        run(linear("w_in", 8, 8, rhs_h, w_h, evac_qk(qka, 0), lin))
        later.flush()
        t_bm = None
        for h in range(8):
            for a in range(2):
                t_bm = v_tt(bias4[:, h, a, :], bias4[:, h, a, :], c1v["mna"], ALU.add, t_c1, t_bias, q=pool)
        tq = pe.last()
        ms = ar.take(80).rearrange("p (a n) -> p a n", a=2)
        sd = ar.take(80).rearrange("p (a n) -> p a n", a=2)
        rsT = ar.take(256)
        rsq = ar.take(80).rearrange("p (a n) -> p a n", a=2)

        def stats(lo, hi, w):
            nonlocal stat_free
            t1 = v_ts(ms[:, :, lo:hi], ssq[:, :, lo:hi], RMS_EPS, None, ALU.add, None, w)
            stat_free = [t1]
            t2 = a_act(sd[:, :, lo:hi], ms[:, :, lo:hi], ACT.Sqrt, t1)
            return v_rcp(rsq[:, :, lo:hi], sd[:, :, lo:hi], t2)

        trs = stats(0, 16, tq)

        def evac_v(dst):
            def f(n, tt, ps, t):
                return [a_act(dst[:, tt, n * 256:n * 256 + 256], ps[:, 0:256], ACT.Copy, t)]
            return f

        def lhs_h(kk, tt):
            return HS[:, 0, kk, tt * 128:tt * 128 + 128], HS[:, 1, kk, tt * 128:tt * 128 + 128]

        run(linear_nat(2, lhs_h, w_h, evac_v(va), lin))
        run(qk_scale(qka, 4, 8, 0, "qna", "kna", rsq, trs))
        t_qk = dve.last()
        t_va = act.last()

        lm = SM[:, 52:60]
        v_tt(lm[:, 0:1], col("lam", 0), col("lam", 1), ALU.mult, t_cl)
        t = v_tt(lm[:, 1:2], col("lam", 2), col("lam", 3), ALU.mult)
        k_, st, free = lin.get()
        t = mm(st[:, 0:2], con("one").to_broadcast([128, 128]), lm[:, 0:2], t, *free)
        t = a_act(lm[:, 2:4], st[:, 0:2], ACT.Exp, t)
        lin.rel(k_, t)
        LAM0 = 0.8 - 0.6 * float(np.exp(-0.0))
        t = v_tt(lm[:, 4:5], lm[:, 2:3], lm[:, 3:4], ALU.subtract, t)
        t = v_ts(lm[:, 5:6], lm[:, 4:5], LAM0, -1.0, ALU.add, ALU.mult, t)


        def softmax(S, W, w):
            nm, z, rz = S["nm"], S["z"], S["rz"]
            t = v_red(nm, S["s"], ALU.max, w, negate=True)
            te = []
            for a in range(2):
                te.append(a_act(S["s"][:, a, :], S["s"][:, a, :], ACT.Exp, t, bias=nm[:, a:a + 1],
                                accum_out=z[:, a:a + 1]))
            t = v_rcp(rz, z, te[1])
            for a in range(2):
                t = v_ts(S["s"][:, a, :], S["s"][:, a, :], rz[:, a:a + 1], None, ALU.mult, None, t)
            return t

        statb = ar.take(12 * 6).rearrange("p (n k) -> p n k", n=12)

        def attention(heads, scores, vlist, put, base):
            st = {}
            for i in range(len(heads) + 2):
                if i < len(heads):
                    h = heads[i]
                    k_, s, free = sbuf_s.get()
                    W, tok = scores(h, s, free)
                    sv = s[:, 0:2 * W].rearrange("p (a w) -> p a w", a=2)
                    b = statb[:, base + i, :]
                    S = {"s": sv, "nm": b[:, 0:2], "z": b[:, 2:4], "rz": b[:, 4:6], "k": k_, "W": W}
                    S["tok"] = softmax(S, W, tok)
                    st[i] = S
                if 0 <= i - 2:
                    S = st.pop(i - 2)
                    h = heads[i - 2]
                    if (i - 2) % 2 == 0:
                        k_pv, pv, pvfree = pvr.get()
                    r = 64 * (h % 2)
                    n = S["W"] // 128
                    for c in range(n):
                        t = mm(pv[r:r + 64, 0:256], vlist(h, c), S["pt"][:, c, :], S["te"][c // 2], *pvfree,
                               start=c == 0, stop=c == n - 1, sig=c == n - 1)
                    sbuf_t.rel(S["ptk"], t)
                    if (i - 2) % 2 == 1:
                        pvr.rel(k_pv, *put(h // 2, pv, t))
                yield 0
                if 0 <= i - 1 < len(heads):
                    S = st[i - 1]
                    kt, pt, ptfree = sbuf_t.get()
                    ptv = pt.rearrange("p (c t) -> p c t", t=256)
                    te = []
                    for c in range(S["W"] // 256):
                        k_, ps, free = trr.get()
                        psv = ps.rearrange("p (j t) -> p j t", j=2)
                        for j in range(2):
                            for a in range(2):
                                t = tr(psv[:, j, a * 128:a * 128 + 128],
                                       S["s"][:, a, c * 256 + j * 128:c * 256 + j * 128 + 128],
                                       S["tok"], *free, sig=j == 1 and a == 1)
                        w = list(ptfree) + [t]
                        t2 = a_act(ptv[:, 2 * c:2 * c + 2, :], psv, ACT.Copy, *w)
                        te.append(t2)
                        trr.rel(k_, t2)
                    sbuf_s.rel(S["k"], t)
                    S["pt"], S["ptk"], S["te"] = ptv, kt, te
                yield 1

        def na_scores(h, s, free):
            k_, ps, pf = scr.get()
            r = 64 * (h % 2)
            for a in range(2):
                t = mm(ps[:, a * 256:a * 256 + 256], qka[r:r + 64, h // 2, a * 128:a * 128 + 128],
                       qka[r:r + 64, 4 + h // 2, :], t_qk, *pf, sig=a == 1)
            t = v_stt(s[:, 0:512], ps, SC, bias4[:, h, :, :].rearrange("p a k -> p (a k)"), ALU.mult, ALU.add,
                      t, t_bm, *free)
            scr.rel(k_, t)
            return 256, t

        def put_na(c, pv, t):
            return [parts(ona[:, 0, c, :], ona[:, 1, c, :], pv[:, 0:256], t)]

        def fill1():
            yield from linear("w_in", 12, 8, rhs_h, w_h, evac_qk(qkd, 8), lin)
            later.flush()
            yield from linear_nat(3, lhs_h, w_h, evac_v(vd), lin)

        weave(attention(list(range(8)), na_scores, lambda h, c: va[:, c, h * 64:h * 64 + 64], put_na, 0),
              fill1(), (1, 1))
        t_vd = act.last()

        def evac_gate(n, ps, t):
            return [a_act(gates[:, n, :], ps[:, 0:256], ACT.Sigmoid, t)]

        fill = linear("w_in", 16, 8, rhs_h, w_h, evac_gate, lin)
        trs = stats(16, 40, pe.last())
        gen = qk_scale(qkd, 6, 12, 8, "qdil", "kdil", rsq, trs)
        prev = None
        rot_t = []
        rot_l = Later(1)
        for c, toks in enumerate(gen):
            def rotary(c=c, tok=toks[c]):
                k_, ps, free = scr.get()
                t = mm(ps[:, 0:256], con("permd"), qkd[:, c, :], tok, *free)
                k2, m, mf = qd_m.get()
                t1 = v_tt(m, qkd[:, c, :], c1v["cosd"], ALU.mult, tok, *mf, q=pool)
                t2 = v_tt(qkd[:, c, :], ps[:, 0:256], c1v["sind"], ALU.mult, t, t1)
                scr.rel(k_, t2)
                t3 = v_tt(qkd[:, c, :], qkd[:, c, :], m, ALU.add, t2)
                qd_m.rel(k2, t3)

            rot_l.put(rotary)
            if c % 2 == 1:
                next(fill)
        rot_l.flush()
        t_qd = dve.last()

        def dil_scores(hh, s, free):
            s4 = s.rearrange("p (a g k) -> p a g k", a=2, g=3)
            for g in range(3):
                k_, ps, pf = scr.get()
                head = 4 * g + hh
                r = 64 * (head % 2)
                for a in range(2):
                    t = mm(ps[:, a * 256:a * 256 + 256], qkd[r:r + 64, head // 2, a * 128:a * 128 + 128],
                           qkd[r:r + 64, 6 + head // 2, :], t_qd, *pf, sig=a == 1)
                if g == 0:
                    m = c1v["mg0"].rearrange("p (a k) -> p a k", a=2)
                else:
                    m = c1v[f"mg{g}"].unsqueeze(1).to_broadcast([128, 2, 256])
                t = v_stt(s4[:, :, g, :], ps.rearrange("p (a k) -> p a k", a=2), SC, m, ALU.mult, ALU.add,
                          t, t_c1, *free)
                scr.rel(k_, t)
            return 768, t

        def put_dil(c, pv, t):
            return [parts(odl[:, 0, c, :], odl[:, 1, c, :], pv[:, 0:256], t)]

        weave(attention(list(range(4)), dil_scores,
                        lambda h, c: vd[:, c % 2, (4 * (c // 2) + h) * 64:(4 * (c // 2) + h) * 64 + 64],
                        put_dil, 8), fill, (2, 1))
        t_att = dve.last()
        t_gate = act.last()

        ar.close()
        ar = Arena()
        mrf = ar.take(2048).rearrange("p (c t) -> p c t", c=8)
        mrg = ar.take(4096, f32r).rearrange("p (s c t) -> p s c t", s=2, c=8)
        qd_m = Rot([ar.take(256) for _ in range(3)])
        fence = barrier()
        mt = []

        def evac_na(n, ps, t):
            t1 = v_tt(mrf[:, n, :], ps[:, 0:256], gates[:, n, :], ALU.mult, t, t_gate, *fence)
            return [t1]

        run(linear("wbna", 8, 4, lambda kk: (ona[:, 0, kk, :], ona[:, 1, kk, :]), lambda kk: [t_att], evac_na, lin))

        def evac_dl(n, ps, t):
            k_, m, mf = qd_m.get()
            t1 = v_tt(m, ps[:, 0:256], gates[:, 8 + n, :], ALU.mult, t, *mf)
            t2 = v_tt(mrf[:, n, :], mrf[:, n, :], m, ALU.add, t1)
            qd_m.rel(k_, t2)
            mt.append(parts(mrg[:, 0, n, :], mrg[:, 1, n, :], mrf[:, n, :], t2))
            return [t1]

        run(linear("wbdil", 8, 2, lambda kk: (odl[:, 0, kk, :], odl[:, 1, kk, :]), lambda kk: [t_att], evac_dl, lin))
        xt = []

        def evac_x(n, ps, t):
            t1 = v_tt(XT[:, n, :], XT[:, n, :], ps[:, 0:256], ALU.add, t)
            xt.append(t1)
            if n == 0:
                warm(ACT.Sqrt)
            square(n, t1)
            return [t1]

        run(linear("wout", 8, 8, lambda kk: (mrg[:, 0, kk, :], mrg[:, 1, kk, :]), lambda kk: [mt[kk]], evac_x, lin))

        ar.close()
        ao.close()
        fence = barrier()
        ex = Arena()
        GS = ex.take(STASH * 256)
        T3 = ex.take(5 * 256, bf16)
        IOB = ex.take(1024, bf16)
        PLr = ex.take(1024, f32r)
        ar = Arena()
        h_t = rmsnorm("nffn", [xt[-1]], [pe.last()])
        keysT = ar.take(256).rearrange("p (a n) -> p a n", a=2)
        t_keys = load("s_keys", keysT.rearrange("p a n -> p (a n)"), A["keysT"], *fence)
        qpc = ar.take(4096)
        qp = qpc.rearrange("p (c t) -> p c t", c=16)
        Ssc = ar.take(4096).rearrange("p (a c n) -> p a c n", a=2, c=16)
        top = ar.take(2 * 16 * 16).rearrange("p (a c n) -> p a c n", a=2, c=16)
        ixu = ar.take(2 * 16 * 16).bitcast(u32).rearrange("p (a c n) -> p a c n", a=2, c=16)
        ixf = ar.take(2 * 16 * 16).rearrange("p (a c n) -> p a c n", a=2, c=16)
        cand = qpc[:, 0:1792].rearrange("p (a h n) -> p a h n", a=2, h=8)
        scv = ar.take(256).rearrange("p (a h n) -> p a h n", a=2, h=8)
        posu = ar.take(256).bitcast(u32).rearrange("p (a h n) -> p a h n", a=2, h=8)
        abu = ar.take(1024).bitcast(u32).rearrange("p (b a h n) -> p b a h n", b=4, a=2, h=8)
        abf = ar.take(1024).rearrange("p (b a h n) -> p b a h n", b=4, a=2, h=8)
        far = ar.take(256).rearrange("p (a h n) -> p a h n", a=2, h=8)
        eqs = [ar.take(2048).rearrange("p (h k j) -> p h k j", h=8, k=16) for _ in range(2)]
        sel = ar.take(768).rearrange("p (b a n) -> p b a n", b=3, a=2)
        ssum = ar.take(32).rearrange("p (b a h) -> p b a h", b=2, a=2)

        qt_ = []

        def evac_qp(n, ps, t):
            t1 = a_act(qp[:, n, :], ps[:, 0:256], ACT.Copy, t, *fence)
            qt_.append(t1)
            return [t1]

        gq = linear("wq", 16, 8, rhs_h, lambda kk: [h_t[kk]], evac_qp, lin)
        st_tok = {}

        def score_pair(c4):
            for a in range(2):
                k_, ps, free = scr.get()
                for j in range(4):
                    c = 4 * c4 + j
                    t = mm(ps[:, j * 128:j * 128 + 128], qp[:, c, a * 128:a * 128 + 128], keysT[:, c % 2, :],
                           qt_[c], t_keys, *free, sig=j == 3)
                t = a_act(Ssc[:, a, 4 * c4:4 * c4 + 4, :], ps.rearrange("p (c n) -> p c n", c=4), ACT.Copy, t)
                scr.rel(k_, t)
                st_tok[a, c4] = t

        for n in range(17):
            next(gq, None)
            if n % 4 == 0 and n:
                score_pair(n // 4 - 1)
        assert len(qt_) == 16

        upr = Rot([bank(5), bank(6)])
        stash = Rot([GS[:, i * 256:i * 256 + 256] for i in range(STASH)])
        upr.free = [list(f) for f in trr.free]
        ga = {}

        def u_slot(j):
            (hi, lo), ld = slot("U")
            k_, ps, free = upr.get()
            ks, g, gf = stash.get()
            for c in range(8):
                t = mm3(ps[:, 0:256], (hi[:, c, :], lo[:, c, :]), rhs_h(c), *ld, h_t[c], *free,
                        start=c == 0, stop=c == 7, sig=c == 7)
            slot_done(t)
            t2 = a_act(g, ps[:, 0:256], ACT.Gelu, t, *gf, *fence)
            upr.rel(k_, t2)
            ga[j] = (ks, g, t2)

        def top16(probs, w):
            st = [[dve.op(lambda e, v=v, vt=vt: e.max(vt[:, 0:8], v), *w)] for v, vt, it in probs]
            for i, (v, vt, it) in enumerate(probs):
                st[i].append(dve.op(lambda e, v=v, vt=vt, it=it: e.max_index(it[:, 0:8], vt[:, 0:8], v), st[i][0]))
            for i, (v, vt, it) in enumerate(probs):
                st[i].append(dve.op(lambda e, v=v, vt=vt: e.match_replace(v, vt[:, 0:8], v, -3.0e38), st[i][1]))
            for i, (v, vt, it) in enumerate(probs):
                st[i].append(dve.op(lambda e, v=v, vt=vt: e.max(vt[:, 8:16], v), st[i][2]))
            for i, (v, vt, it) in enumerate(probs):
                t = dve.op(lambda e, v=v, vt=vt, it=it: e.max_index(it[:, 8:16], vt[:, 8:16], v), st[i][3])
            return t

        def route():
            t_exp, t_ab, t_eq = {}, {}, {}

            def look_up(a, on_dve):
                for b in range(2):
                    eq = eqs[b]
                    ab = abf[:, b, a].unsqueeze(3).to_broadcast([128, 8, 16, 16])
                    io = con("iota")[:, 0:16].unsqueeze(1).unsqueeze(1).to_broadcast([128, 8, 16, 16])
                    t = v_tt(eq, ab, io, ALU.is_equal, t_ab[a])
                    iv = ixf[:, a].rearrange("p (h b) n -> p h b n", b=2)[:, :, b, :]
                    t_eq[b] = v_tt(eq, eq, iv.unsqueeze(2).to_broadcast([128, 8, 16, 16]), ALU.mult, t,
                                   q=dve if b in on_dve else pool)

            def found(a):
                for b in (1, 0):
                    v_red(sel[:, b, a, :].rearrange("p (h k) -> p h k", h=8), eqs[b], ALU.add, t_eq[b])
                g_ = sel[:, 2, a, :].rearrange("p (h k) -> p h k", h=8)
                t = v_red(ssum[:, 0, a], g_, ALU.add, t_exp[a])
                t = v_rcp(ssum[:, 1, a], ssum[:, 0, a], t)
                v_tt(g_, g_, ssum[:, 1, a].unsqueeze(2).to_broadcast([128, 8, 16]), ALU.mult, t)

            for c in range(0, 16, 4):
                for a in range(2):
                    top16([(Ssc[:, a, c + i, :], top[:, a, c + i, :], ixu[:, a, c + i, :]) for i in range(4)],
                          [st_tok[a, c // 4], *fence])
                    yield 4 if c >= 8 else 0
            t = dve.last()
            for a in range(2):
                v_cp(ixf[:, a], ixu[:, a], t)
                tv = top[:, a].rearrange("p (h b) n -> p h b n", b=2)
                cv = cand[:, a, :, 0:64].rearrange("p h (i j) -> p h i j", i=4)
                v_tt(cv, tv[:, :, 0, 0:4].unsqueeze(3).to_broadcast([128, 8, 4, 16]),
                     tv[:, :, 1, :].unsqueeze(2).to_broadcast([128, 8, 4, 16]), ALU.add, t, qp_done)
                cv = cand[:, a, :, 64:112].rearrange("p h (i j) -> p h i j", i=12)
                t = v_tt(cv, tv[:, :, 0, 4:16].unsqueeze(3).to_broadcast([128, 8, 12, 4]),
                         tv[:, :, 1, 0:4].unsqueeze(2).to_broadcast([128, 8, 12, 4]), ALU.add, t, qp_done)
                yield 2
                if a:
                    look_up(0, [])
                    yield 4
                for h in range(0, 8, 2):
                    top16([(cand[:, a, h + i, :], scv[:, a, h + i, :], posu[:, a, h + i, :]) for i in range(2)], [t])
                    yield 4
                t = dve.last()
                if a:
                    found(0)
                    yield 5
                for i, (n_, op_) in enumerate(((4, ALU.logical_shift_right), (15, ALU.bitwise_and),
                                               (2, ALU.logical_shift_right), (3, ALU.bitwise_and))):
                    ta = dve.op(lambda e, a=a, i=i, n_=n_, op_=op_: e.tensor_scalar(abu[:, i, a], posu[:, a], n_, None,
                                                                                    op_), t)
                g_ = sel[:, 2, a, :].rearrange("p (h k) -> p h k", h=8)
                t = v_tt(g_, scv[:, a], scv[:, a, :, 0:1].to_broadcast([128, 8, 16]), ALU.subtract, t)
                t_exp[a] = a_act(g_, g_, ACT.Exp, t)
                t = v_cp(abf[:, :, a], abu[:, :, a], ta)
                t = v_ts(far[:, a], abf[:, 0, a], 4.0, None, ALU.is_ge, None, t)
                t = v_tt(abf[:, 2:4, a], abf[:, 2:4, a], abf[:, 0:2, a], ALU.subtract, t)
                t = v_tt(abf[:, 2:4, a], abf[:, 2:4, a], far[:, a].unsqueeze(1).to_broadcast([128, 2, 8, 16]), ALU.mult, t)
                t = v_tt(abf[:, 0:2, a], abf[:, 0:2, a], abf[:, 2:4, a], ALU.add, t)
                t = v_stt(abf[:, 0, a], far[:, a], -12.0, abf[:, 0, a], ALU.mult, ALU.add, t)
                t_ab[a] = t
                yield 2
            look_up(1, [1])
            yield 6
            found(1)

        ahead_u = 0
        credit = 0.0
        qp_done = pe.last()
        for cost in route():
            credit += cost
            while credit >= 4 and ahead_u < STASH - 4:
                credit -= 4
                u_slot(ahead_u)
                ahead_u += 1
        t_sel = dve.last()

        T3f = eqs[0].rearrange("p h k j -> p (h k j)")[:, 0:768].rearrange("p (b t) -> p b t", b=3)
        rest = eqs[0].rearrange("p h k j -> p (h k j)")[:, 768:1280].rearrange("p (b t) -> p b t", b=2)
        for a in range(2):
            k_, ps, free = scr.get()
            for b in range(3):
                t = tr(ps[:, b * 128:b * 128 + 128], sel[:, b, a, :], t_sel, *free, sig=b == 2)
            t = v_cp(T3f[:, :, a * 128:a * 128 + 128], ps[:, 0:384].rearrange("p (b t) -> p b t", b=3), t)
            scr.rel(k_, t)
        T3v = T3.rearrange("p (b t) -> p b t", b=5)
        v_cp(T3v[:, 0:3, :], T3f, t)
        t = dve.last()
        for k in range(2):
            t = v_tt(rest[:, k, :], rest[:, k - 1, :] if k else T3f[:, 2, :], T3v[:, 2 + k, :], ALU.subtract, t)
            t = v_cp(T3v[:, 3 + k, :], rest[:, k, :], t)
        iota8 = IOB.rearrange("p (i j) -> p i j", j=8)
        v_cp(iota8, con("iota").unsqueeze(2).to_broadcast([128, 128, 8]), *fence)
        t_T3 = dve.last()
        ar.close()
        ar = Arena()
        fence = barrier()
        G = ar.take(64 * 256).rearrange("p (i t) -> p i t", t=256)
        oh = Rot([ar.take(1024 + 24 * QUART, bf16) for _ in range(3)])
        asp = Rot([ar.take(512, f32r) for _ in range(4)])
        iota = con("iota")
        gev = Rot([scr.aps[0], scr.aps[1]])
        gev.free = [list(f) for f in scr.free]
        gtok = {}
        acc = [bank(0), bank(1), bank(4), bank(7)]
        acc_free = lin.free[0] + lin.free[1] + pvr.free[0] + stat_free

        def gates_of(q):
            gw = list(fence) + [dve.last()]
            Gq = G[:, QUART * (q % 2):QUART * (q % 2) + QUART, :]

            def marks(n):
                k_, o, of = oh.get()
                at = [T3v[:, b, 8 * n:8 * n + 8] for b in range(5)]
                w1 = o[:, 0:1024].rearrange("p (i j) -> p i j", j=8)
                w2 = o[:, 1024:1024 + 24 * QUART].rearrange("p (k i j) -> p k i j", k=3, j=8)
                te = v_tt(w2[:, 2], iota8[:, QUART * q:QUART * q + QUART, :],
                     at[1].unsqueeze(1).to_broadcast([128, QUART, 8]), ALU.is_equal, t_T3, *of, *gw)
                v_tt(w1, iota8, at[0].unsqueeze(1).to_broadcast([128, 128, 8]), ALU.is_equal, t_T3, *of, *gw)
                for k in range(3):
                    tm = v_tt(w2[:, k], w2[:, 2], at[2 + k].unsqueeze(1).to_broadcast([128, QUART, 8]), ALU.mult, te)
                return k_, w1, w2, tm

            ready = [marks(0), marks(1)]
            for n in range(32):
                if n + 2 < 32:
                    ready.append(marks(n + 2))
                k_, w1, w2, tok = ready.pop(0)
                kb, ps, pf = gev.get()
                for j in range(8):
                    for k in range(3):
                        t = mm(ps[:, j * QUART:j * QUART + QUART], w1[:, :, j], w2[:, k, :, j], tok, *pf,
                               start=k == 0, stop=k == 2, sig=j == 7 and k == 2)
                oh.rel(k_, t)
                t = a_act(Gq[:, :, 8 * n:8 * n + 8], ps[:, 0:8 * QUART].rearrange("p (j i) -> p i j", j=8),
                          ACT.Copy, t, *gw)
                gev.rel(kb, t)
                if n == 31:
                    gtok[q] = t
                yield

        def v_slot(i2):
            (hi, lo), ld = slot("V")
            g_ = G[:, i2 % 64, :]
            ap_ = a_parts.pop(i2)
            for c in range(8):
                t = mm3(acc[c // 2][:, (c % 2) * 256:(c % 2) * 256 + 256], (hi[:, c, :], lo[:, c, :]),
                        (ap_[1][:, 0:256], ap_[1][:, 256:512]), *ld, ap_[2], *acc_free,
                        start=i2 == 0 and c % 2 == 0, stop=i2 == NE - 1 and c % 2 == 1, sig=c == 7, skip=True)
            asp.rel(ap_[0], t)
            slot_done(t)

        a_parts = {}

        def a_of(i2):
            ks, g, tg = ga.pop(i2)
            t = v_tt(g, g, G[:, i2 % 64, :], ALU.mult, tg, gtok[i2 // QUART])
            k_, sp_, free = asp.get()
            t = parts(sp_[:, 0:256], sp_[:, 256:512], g, t, *free)
            stash.rel(ks, t)
            a_parts[i2] = (k_, sp_, t)

        beside = ahead_u
        for n, _ in enumerate(gates_of(0)):
            while ahead_u < STASH and (STASH - ahead_u) * 32 >= (31 - n) * (STASH - beside):
                u_slot(ahead_u)
                ahead_u += 1
        ahead, credit, gg = 0, 0.0, iter(())
        late = None
        pF, pS = GS[:, 0:512], PLr
        pw = GS[:, 2048:4096].rearrange("p (c t) -> p c t", c=8)
        for j in range(NE):
            if j == NE - STASH:
                rest_on[:] = [pool, dve]
            if j % QUART == 0 and j + QUART < NE:
                gg, credit = gates_of(j // QUART + 1), 0.0
            while ahead < min(j + 3, NE) and ahead // QUART in gtok:
                a_of(ahead)
                ahead += 1
            if ahead == NE and late is None:
                late = [dve.last(), act.last()]
                t_p = load("s_p", pF, A["pT"], *late)
                t_p = parts(pS[:, 0:512], pS[:, 512:1024], pF, t_p, *late)
                pS = pS.rearrange("p (s c t) -> p s c t", s=2, c=2)
            v_slot(j)
            credit += 32 / 28
            while credit >= 1:
                credit -= 1
                next(gg, None)
            if j + STASH < NE:
                u_slot(ahead_u)
                ahead_u += 1
        v_end = pe.last()
        xt = []
        for c in range(4):
            xt.append(v_tt(XT[:, 2 * c:2 * c + 2, :], XT[:, 2 * c:2 * c + 2, :],
                           acc[c].rearrange("p (j t) -> p j t", j=2), ALU.add, v_end))
        stat_free = [xt[-1]]
        warm(ACT.Sqrt)
        tg_ = []

        def evac_ple(n, ps, t):
            t1 = a_act(pw[:, n, :], ps[:, 0:256], ACT.Copy, t, *late)
            tg_.append(t1)
            square(n, xt[n // 2], on_dve=True)
            return [t1]

        run(linear("wple", 8, 2, lambda kk: (pS[:, 0, kk, :], pS[:, 1, kk, :]), lambda kk: [t_p], evac_ple, upr))
        ar.close()

        rest_on[:] = [pool, dve]
        fence = barrier()
        lin.free = [[xt[-1]], [xt[-1]]]
        scr.free = [list(f) for f in gev.free]
        pvr.free = [[xt[-1]]]
        trr.free = [list(f) for f in upr.free]
        xt0, fence_pe = list(xt), pe.last()
        t_sin = None
        ar = Arena()
        c2 = ar.take(NC2)
        t_c2 = load("s_c2", c2, A["c2"], *fence)
        posi = ar.take(256).bitcast(i32)
        t_pos = load("s_pos", posi, A["pos"].partition_broadcast(128), *fence)
        pg = ar.take(2048).rearrange("p (c t) -> p c t", c=8)

        posf = ar.take(256)
        ang = ar.take(256)
        kq = ar.take(256)
        cosr = ar.take(256)
        sinr = ar.take(256)

        def rotary_tables():
            nonlocal t_sin
            TWO_PI = 2.0 * math.pi
            P1 = 6.28125
            P2 = math.floor((TWO_PI - P1) * 2.0 ** 18) / 2.0 ** 18
            P3 = TWO_PI - P1 - P2
            MAGIC = 12582912.0
            t = v_cp(posf, posi, t_pos, *fence)
            t_ang = v_ts(ang, posf, con("invf"), None, ALU.mult, None, t)
            PI_ = 3.1415925
            for dst, quarter in ((sinr, 0.0), (cosr, 0.25)):
                t = v_ts(kq, ang, 1.0 / TWO_PI, quarter, ALU.mult, ALU.add, t_ang, chain=True)
                t = v_ts(kq, kq, MAGIC, None, ALU.add, None, t)
                t = v_ts(kq, kq, MAGIC, None, ALU.subtract, None, t)
                t = v_stt(dst, kq, -P1, ang, ALU.mult, ALU.add, t)
                t = v_stt(dst, kq, -P2, dst, ALU.mult, ALU.add, t)
                t = v_stt(dst, kq, -P3, dst, ALU.mult, ALU.add, t)
                if quarter:
                    t = v_ts(dst, dst, math.pi / 2, None, ALU.add, None, t)
                t = v_ts(dst, dst, PI_, -PI_, ALU.min, ALU.max, t)
                t_sin = a_act(dst, dst, ACT.Sin, t)


        h_t = rmsnorm("nple", xt0, [fence_pe])
        rotary_tables()
        xt = []

        def evac_pg(n, ps, t):
            t0 = a_act(pg[:, n, :], ps[:, 0:256], ACT.Sigmoid, t, *fence)
            t1 = v_tt(pg[:, n, :], pg[:, n, :], pw[:, n, :], ALU.mult, t0, tg_[n])
            xt.append(v_tt(XT[:, n, :], XT[:, n, :], pg[:, n, :], ALU.add, t1))
            if n == 7:
                warm(ACT.Sqrt)
            square(n, xt[-1])
            return [t0]

        run(linear("wpg", 8, 8, rhs_h, lambda kk: [h_t[kk]], evac_pg, lin))

        h_t = rmsnorm("nmix2", [xt[-1]], [pe.last()])
        pT_ = ar.take(1024).rearrange("p (c t) -> p c t", c=4)
        qk2 = ar.take(2048).rearrange("p (c t) -> p c t", c=8)
        v2 = ar.take(1024).rearrange("p (a n) -> p a n", a=2)
        mxf = Rot([ar.take(256) for _ in range(3)])
        mixT = ar.take(4096, f32r).rearrange("p (s c t) -> p s c t", s=2, c=8)
        poolw = ar.take(512).rearrange("p (g n) -> p g n", g=4)
        t_pw = load("s_pw", poolw.rearrange("p g n -> p (g n)"), A["poolw"], *fence)
        wa = ar.take(256)
        wb, wc, wd = ar.take(256), ar.take(256), ar.take(256)
        dT = ar.take(1024).rearrange("p (c t) -> p c t", c=4)
        qt2 = []

        def evac_q2(n, ps, t):
            t = a_act(qk2[:, n, :], ps[:, 0:256], ACT.Copy, t)
            qt2.append(t)
            return [t]

        run(linear("w_in2", 8, 8, rhs_h, lambda kk: [h_t[kk]], evac_q2, lin))
        fv = linear_nat(2, lhs_h, lambda kk: [h_t[kk]], evac_v(v2), lin)
        rm = Rot([ar.take(256) for _ in range(2)])
        for c in range(8):
            k_, ps, free = scr.get()
            t = mm(ps[:, 0:256], con("permr"), qk2[:, c, :], qt2[c], *free)
            k2, m, mf = rm.get()
            t1 = v_tt(m, qk2[:, c, :], cosr, ALU.mult, qt2[c], t_sin, *mf, q=pool)
            t2 = v_tt(qk2[:, c, :], ps[:, 0:256], sinr, ALU.mult, t, t1, t_sin)
            scr.rel(k_, t2)
            t3 = v_tt(qk2[:, c, :], qk2[:, c, :], m, ALU.add, t2)
            rm.rel(k2, t3)
            if c % 4 == 3:
                next(fv, None)
        run(fv)
        t_q2 = dve.last()
        t_v2 = act.last()

        sb2 = Rot([ar.take(768) for _ in range(4)])
        sb3 = Rot([ar.take(384) for _ in range(2)])
        osb = GS[:, 4096:5120].rearrange("p (c t) -> p c t", c=4)
        osqr = Rot([GS[:, 5120 + 256 * i:5376 + 256 * i] for i in range(3)])
        sst = ar.take(4 * 12).rearrange("p (h n) -> p h n", h=4)
        mdf = c2[:, 0:384]
        S2 = {}

        def d_scores(h):
            k_, s, free = sb2.get()
            sv = s.rearrange("p (n w) -> p n w", n=2)
            for n in range(2):
                kp, ps, pf = scr.get()
                r = 64 * n
                mm(ps[:, 0:128], qk2[r:r + 64, h, 0:128], qk2[r:r + 64, 4 + h, 0:128], t_q2, *pf, sig=False)
                t = mm(ps[:, 128:384], qk2[r:r + 64, h, 128:256], qk2[r:r + 64, 4 + h, :])
                t = v_stt(sv[:, n, :], ps[:, 0:384], SC, mdf, ALU.mult, ALU.add, t, t_c2, *free)
                scr.rel(kp, t)
            b = sst[:, h, :]
            segs = ((0, 128), (128, 384))
            v_red(b[:, 0:2], sv[:, :, 0:128], ALU.max, t, negate=True)
            t = v_red(b[:, 2:4], sv[:, :, 128:384], ALU.max, t, negate=True)
            for i, (lo, hi) in enumerate(segs):
                for n in range(2):
                    te = a_act(sv[:, n, lo:hi], sv[:, n, lo:hi], ACT.Exp, t,
                               bias=b[:, 2 * i + n:2 * i + n + 1], accum_out=b[:, 4 + 2 * i + n:5 + 2 * i + n])
            t = v_rcp(b[:, 8:12], b[:, 4:8], te)
            for i, (lo, hi) in enumerate(segs):
                t1 = v_ts(b[:, 4 + i:5 + i], b[:, 9 + 2 * i:10 + 2 * i], lm[:, 5:6], None, ALU.mult, None, t)
                t2 = v_ts(sv[:, 0, lo:hi], sv[:, 0, lo:hi], b[:, 8 + 2 * i:9 + 2 * i], None, ALU.mult, None, t)
                t3 = v_stt(sv[:, 0, lo:hi], sv[:, 1, lo:hi], b[:, 4 + i:5 + i], sv[:, 0, lo:hi],
                           ALU.mult, ALU.add, t1, t2)
            S2[h] = (k_, sv, t3)

        def d_tr(h):
            k_, sv, tok = S2[h]
            kp, ps, pf = trr.get()
            for j in range(3):
                t = tr(ps[:, j * 128:j * 128 + 128], sv[:, 0, j * 128:j * 128 + 128], tok, *pf, sig=j == 2)
            sb2.rel(k_, t)
            kt, pt, ptf = sb3.get()
            t = a_act(pt, ps[:, 0:384], ACT.Copy, t, *ptf)
            trr.rel(kp, t)
            S2[h] = (kt, pt, t)

        ssq2 = bank(7)[:, 64:72].rearrange("p (a n) -> p a n", a=2)
        to_ = []

        def d_pv(h):
            kt, pt, tok = S2.pop(h)
            kv, pv, pvf = pvr.get()
            mm(pv[:, 0:256], v2[:, 0, h * 128:h * 128 + 128], pt[:, 0:256], tok, t_v2, *pvf,
               start=True, stop=False, sig=False)
            t = mm(pv[:, 128:256], v2[:, 1, h * 128:h * 128 + 128], pt[:, 256:384], start=False, stop=True)
            sb3.rel(kt, t)
            t1 = v_cp(osb[:, h, :], pv[:, 0:256], t)
            ko, oq, of = osqr.get()
            t2 = a_act(oq, osb[:, h, :], ACT.Square, t1, *of)
            pvr.rel(kv, t1)

            def sums():
                for tt in range(2):
                    t = mm(ssq2[:, tt, h:h + 1], oq[:, tt * 128:tt * 128 + 128], con("o128"), t2, *stat_free,
                           sig=tt == 1)
                osqr.rel(ko, t)
                to_.append((t1, t))

            later.put(sums)

        t_pT = []
        def evac_p(n, ps, t):
            t = a_act(pT_[:, n, :], ps[:, 0:256], ACT.Copy, t, *fence)
            t_pT.append(t)
            return [t]

        tpool = []

        def gen_pool():
            for g in range(4):
                cur, tcur = pT_[:, g, :], t_pT[g]
                on = pool if g >= 2 else dve
                bufs = (wa, wb) if g >= 2 else (wc, wd)
                for lv in range(g + 1):
                    s = 1 << lv
                    nxt = bufs[lv % 2]
                    t1 = v_cp(nxt[:, 0:s], cur[:, 0:s], tcur, q=on, chain=True)
                    tcur = v_tt(nxt[:, s:256], cur[:, s:256], cur[:, 0:256 - s], ALU.add, t1, q=on)
                    cur = nxt
                cn = c2[:, C2["cnt"][0] + 256 * g:C2["cnt"][0] + 256 * g + 256]
                t1 = v_tt(dT[:, g, :], cur, cn, ALU.mult, tcur, t_c2, q=on)
                t1 = v_tt(dT[:, g, :], dT[:, g, :], pT_[:, g, :], ALU.subtract, t1, q=on)
                yield
                k_, ps, free = trr.get()
                t2 = mm(ps[:, 0:256], poolw[:, g, :], dT[:, g, :], t1, t_pw, *free)
                km, m, mf = mxf.get()
                t3 = a_act(m, ps[:, 0:256], ACT.Copy, t2, *mf, scale=col("psc", g))
                trr.rel(k_, t3)
                t3 = parts(mixT[:, 0, g, :], mixT[:, 1, g, :], m, t3)
                mxf.rel(km, t3)
                tpool.append(t3)
                yield

        def fill2():
            gl = linear("w_in2", 4, 8, rhs_h, lambda kk: [h_t[kk]], evac_p, lin)
            next(gl)
            yield
            next(gp)
            for _ in range(3):
                next(gl)
                yield
                next(gp)
                next(gp)
                yield
            run(gl)

        gp = gen_pool()
        fl = fill2()
        for h in range(6):
            if h < 4:
                d_scores(h)
            if 0 <= h - 2:
                d_pv(h - 2)
            next(fl, None)
            if 0 <= h - 1 < 4:
                d_tr(h - 1)
            next(fl, None)
        run(fl)
        later.flush()
        rs2 = ar.take(24).rearrange("p (b a n) -> p b a n", b=3, a=2)
        t = v_ts(rs2[:, 0], ssq2, RMS_EPS, None, ALU.add, None, to_[-1][1])
        stat_free = [t]
        t = a_act(rs2[:, 1], rs2[:, 0], ACT.Sqrt, t)
        t = v_rcp(rs2[:, 2], rs2[:, 1], t)
        t = v_ts(rs2[:, 2], rs2[:, 2], 1.0 - LAM0, None, ALU.mult, None, t)
        tm = []
        for h in range(4):
            k_, ps, free = lin.get()
            for tt in range(2):
                t1 = mm(ps[:, tt * 128:tt * 128 + 128], rs2[:, 2, tt, h:h + 1].to_broadcast([128, 128]), ident,
                        t, *free, sig=tt == 1)
            t1 = v_stt(osb[:, h, :], osb[:, h, :], col("ang", h), ps[:, 0:256], ALU.mult, ALU.mult, t1)
            lin.rel(k_, t1)
            tm.append(parts(mixT[:, 0, 4 + h, :], mixT[:, 1, 4 + h, :], osb[:, h, :], t1, eng=act))
        run(gp)
        xt = []
        run(linear("wo2", 8, 8, lambda kk: (mixT[:, 0, kk, :], mixT[:, 1, kk, :]),
                   lambda kk: [tpool[kk]] if kk < 4 else [tm[kk - 4]],
                   evac_x, lin))

        h_t = rmsnorm("nffn2", [dve.last()], [pe.last()])
        ar.close()
        ex.close()
        ar = Arena()
        fence = barrier()
        actT = ar.take(44 * 256, f32r).rearrange("p (s c t) -> p s c t", s=2, c=22)
        ub = Rot([ar.take(512) for _ in range(3)])
        fb = Rot([bank(2), bank(3), bank(0), bank(1)])
        fb.free = [list(f) for f in scr.free] + [list(f) for f in lin.free]
        ta_ = []

        def evac_up(n, ps, t):
            f = n // 2
            k_, u, uf = ub.get()
            uv = u.rearrange("p (j t) -> p j t", j=2)
            pv = ps.rearrange("p (j t) -> p j t", j=2)
            tt_ = []
            for j in range(2):
                c = f + 22 * j
                t1 = a_act(uv[:, j, :], pv[:, j, :], ACT.Identity, t, *uf, *fence, scale=col("cw2", c), bias=col("cb", c))
            for j in range(2):
                c = f + 22 * j
                t2 = v_stt(uv[:, j, 1:256], pv[:, j, 0:255], col("cw1", c), uv[:, j, 1:256], ALU.mult, ALU.add, t1)
                t3 = v_stt(uv[:, j, 2:256], pv[:, j, 0:254], col("cw0", c), uv[:, j, 2:256], ALU.mult, ALU.add, t2)
                tt_.append(t3)
            t4 = a_act(uv[:, 0, :], uv[:, 0, :], ACT.Silu, tt_[0])
            t5 = v_tt(uv[:, 0, :], uv[:, 0, :], uv[:, 1, :], ALU.mult, t4, tt_[1])
            t5 = parts(actT[:, 0, f, :], actT[:, 1, f, :], uv[:, 0, :], t5, eng=act)
            ub.rel(k_, t5)
            ta_.append(t5)
            return [tt_[1]]

        run(linear("wup", 44, 8, rhs_h, lambda kk: [h_t[kk]], evac_up, fb, half=True))
        xt.clear()
        run(linear("wdn", 8, 22, lambda kk: (actT[:, 0, kk, :], actT[:, 1, kk, :]), lambda kk: [ta_[kk]], evac_x, fb))
        lin.free = [[dve.last()], [dve.last()]]
        y_t = rmsnorm("nfin", [dve.last()], [pe.last()], split_=False)
        s_out = sem("s_out")
        sp.dma(lambda e: e.dma_start(A["out"], HFt[:, :]), s_out, y_t[-1])
        assert ring["used"] == len(order)
        ar.close()

        block = ctx.enter_context(nc.Block())

        @block.sync
        def _(eng):
            sp.emit(eng)
            eng.wait_ge(s_out, 16)

        @block.tensor
        def _(eng):
            pe.emit(eng)

        @block.scalar
        def _(eng):
            act.emit(eng)

        @block.vector
        def _(eng):
            dve.emit(eng)

        @block.gpsimd
        def _(eng):
            pool.emit(eng)


def _blocks(w, order=None, wide=()):
    k, n = w.shape
    b = w.reshape(k // 128, 128, n // 128, 128).transpose(2, 0, 1, 3)
    if order is not None:
        b = b[np.asarray(order)]
    if wide:
        b = b.copy()
        for c in wide:
            pair = b[c:c + 2].transpose(1, 0, 2, 3).reshape(2, k // 128, 128, 128).copy()
            b[c:c + 2] = pair
    b = b.reshape(-1, 8, 128, 128).transpose(0, 2, 1, 3)
    return b.reshape(-1, 128, 1024)


def _cols(v):
    return np.asarray(v, np.float32).reshape(-1, 128).T


def _constants():
    c0 = np.zeros((128, NC0), np.float32)

    def put(c, at, name, v):
        a, w = at[name]
        c[:, a:a + w] = v

    p = np.arange(128)
    put(c0, C0, "ident", np.eye(128))
    put(c0, C0, "iota", np.arange(128)[None, :])
    put(c0, C0, "blk", (p[:, None] // 64 == np.arange(2)[None, :]) / 64.0)
    put(c0, C0, "o1024", 1.0 / 1024)
    put(c0, C0, "o128", 1.0 / 128)
    put(c0, C0, "one", 1.0)
    f = np.power(np.float32(10000.0), -(np.arange(0, 64, 2).astype(np.float32)) / np.float32(64))
    put(c0, C0, "invf", f.astype(np.float32)[p % 32][:, None])
    m = np.zeros((128, 128), np.float32)
    r = np.zeros((128, 128), np.float32)
    for b in (0, 64):
        for j in range(8):
            m[b + 8 + j, b + j] = -1.0
            m[b + j, b + 8 + j] = 1.0
        for j in range(32):
            r[b + 32 + j, b + j] = -1.0
            r[b + j, b + 32 + j] = 1.0
    put(c0, C0, "permd", m)
    put(c0, C0, "permr", r)

    c1 = np.zeros((128, NC1), np.float32)
    kcol = np.arange(256) % 64
    cs = np.clip(p % 64 - 8, 0, 48)[:, None]
    ok = (kcol[None, :] >= cs) & (kcol[None, :] < cs + 16)
    put(c1, C1, "mna", np.where(ok, 0.0, NEG))
    q = np.arange(256)
    k = np.arange(256)
    band = np.abs(q[:, None] - k[None, :]) <= 64
    mg0 = np.where(band, 0.0, NEG).reshape(2, 128, 256).transpose(1, 0, 2).reshape(128, 512)
    put(c1, C1, "mg0", mg0)
    put(c1, C1, "mg1", np.where((p[:, None] - k[None, :]) % 4 == 0, 0.0, NEG))
    put(c1, C1, "mg2", np.where((p[:, None] - k[None, :]) % 16 == 0, 0.0, NEG))
    inv = np.power(np.float32(500000.0), -np.arange(8, dtype=np.float32) * np.float32(2.0) / np.float32(16))
    ang = (np.arange(256, dtype=np.float32)[None, :] * inv.astype(np.float32)[:, None]).astype(np.float32)
    cosd = np.ones((128, 256), np.float32)
    sind = np.zeros((128, 256), np.float32)
    for b in (0, 64):
        for j in range(16):
            cosd[b + j] = np.cos(ang[j % 8])
            sind[b + j] = np.sin(ang[j % 8])
    put(c1, C1, "bsel", p[:, None] == np.arange(1536)[None, :] // 64)
    put(c1, C1, "cosd", cosd)
    put(c1, C1, "sind", sind)

    c2 = np.zeros((128, NC2), np.float32)
    md = np.zeros((128, 384), np.float32)
    md[0:64, 64:128] = NEG
    md[0:64, 128 + 192:384] = NEG
    put(c2, C2, "mdf", md)
    cnt = np.concatenate([1.0 / np.minimum(np.arange(256) + 1, w) for w in (2, 4, 8, 16)])
    put(c2, C2, "cnt", cnt[None, :])
    return c0, c1, c2


def _layout(i):
    f = lambda n: np.asarray(i[n])
    x = f("x")[0]
    out = {"xT": x.T.reshape(8, 128, 256).transpose(1, 0, 2).reshape(128, 2048)}
    up = f("w_up_2")[0]
    o = [j for k in range(22) for j in (k, k + 22)]
    out["dense"] = np.concatenate([
        _blocks(f("w_in")[0], None, (8, 10, 24, 26, 28)), _blocks(f("w_branch_na")[0]), _blocks(f("w_branch_dil")[0]),
        _blocks(f("w_out")[0]), _blocks(f("peer_w_query")[0]), _blocks(f("w_ple")[0]),
        _blocks(f("w_ple_gate")[0]), _blocks(f("w_in_2")[0], [*range(4, 16), *range(4)], (8, 10)), _blocks(f("w_o_2")[0]), _blocks(up, o),
        _blocks(f("w_down_2")[0])])
    out["eu"] = f("peer_expert_u")[0].reshape(128, 128, 8, 128).transpose(1, 3, 2, 0).reshape(128, 128, 1024)
    out["ev"] = f("peer_expert_v")[0].reshape(128, 128, 1024).transpose(1, 0, 2)
    out["keysT"] = f("peer_sub_keys")[0].transpose(2, 0, 1).reshape(128, 256)
    cols = np.zeros((128, NCOL), np.float32)

    def put(name, v):
        a, w = COLS[name]
        cols[0:v.shape[0], a:a + w] = v

    for name, key in (("nmix", "norm_mix"), ("nffn", "norm_ffn"), ("nple", "norm_ple"),
                      ("nmix2", "norm_mix_g_2"), ("nffn2", "norm_ffn_g_2"), ("nfin", "norm_final_g_2")):
        put(name, _cols(f(key)))
    for name, key, j in (("qna", "qk_norm_na", 0), ("kna", "qk_norm_na", 1), ("qdil", "qk_norm_dil", 0),
                         ("kdil", "qk_norm_dil", 1)):
        put(name, np.tile(f(key)[0, j], 2)[:, None])
    put("psc", _cols(f("pool_scale_2")))
    put("ang", f("attn_norm_g_2")[0].T)
    for j in range(3):
        put(f"cw{j}", _cols(f("conv_w_2")[0, j]))
    put("cb", _cols(f("conv_b_2")[0]))
    put("lam", np.stack([f("lambda_q1_2")[0], f("lambda_k1_2")[0], f("lambda_q2_2")[0], f("lambda_k2_2")[0]], 1))
    out["cols"] = cols
    c = np.arange(64)
    dc = np.clip(c[None, :] - c[:, None] + 15, 0, 30)
    r = np.arange(4)
    dr = r[None, :] - r[:, None] + 7
    b = f("na_rel_bias")[0][:, dr[:, None, :, None], dc[None, :, None, :]]
    b = b.reshape(8, 2, 128, 256).transpose(2, 0, 1, 3).reshape(128, 4096)
    out["nab"] = b
    out["pT"] = f("p")[0, 0].T.reshape(2, 128, 256).transpose(1, 0, 2).reshape(128, 512)
    out["poolw"] = f("pool_w_2")[0].transpose(1, 0, 2).reshape(128, 512)
    out["pos"] = f("positions_2").reshape(256)
    out["c0"], out["c1"], out["c2"] = _constants()
    return {k: np.ascontiguousarray(v) for k, v in out.items()}


def program(nc, arrays):
    A = {k: nc.dram_tensor(f"in_{k}", v.shape, mybir.dt.from_np(v.dtype), kind="ExternalInput").ap()
         for k, v in arrays.items()}
    A["out"] = nc.dram_tensor("out_y", (128, 2048), mybir.dt.float32, kind="ExternalOutput").ap()
    build(nc, A)


def kernel(**inputs):
    import concourse.bacc as _bacc
    from concourse.bass_utils import run_bass_kernel_spmd as _run

    arrays = _layout(inputs)
    nc = _bacc.Bacc("TRN2", target_bir_lowering=False, num_devices=1)
    program(nc, arrays)
    r = _run(nc, [{f"in_{k}": v for k, v in arrays.items()}], core_ids=[0])
    y = r.results[0]["out_y"].reshape(128, 8, 256)
    return np.ascontiguousarray(y.transpose(2, 1, 0).reshape(1, 256, 1024))
```
